# Optimizing a Trainium2 kernel written in Bass

```python
import math
import numpy as np
import jax
import jax.numpy as jnp
from jax import lax

D_MODEL = 1024
BATCH = 1
SEQ = 256
DEPTH = 1

NSA_HEADS = 8
NSA_KV_GROUPS = 2
NSA_HPG = NSA_HEADS // NSA_KV_GROUPS
NSA_HEAD_DIM = 64
NSA_WIDTH = NSA_HEADS * NSA_HEAD_DIM
NSA_KV_WIDTH = NSA_KV_GROUPS * NSA_HEAD_DIM
CMP_BLK = 32
CMP_STRIDE = 16
CMP_HID = 256
SEL_BLK = 64
N_SEL = 16
WINDOW = 512
Q_BLK = 128
ROPE_THETA = 10000.0

GDN_HEADS = 4
GDN_HEAD_DIM = 128
GDN_WIDTH = GDN_HEADS * GDN_HEAD_DIM
CONV_K = 4
GDN_CHUNK = 64

MIX_WIDTH = NSA_WIDTH + GDN_WIDTH
IN_SPLITS = (NSA_WIDTH, 6 * NSA_KV_WIDTH, 3 * NSA_HEADS, 3 * GDN_WIDTH, GDN_WIDTH, GDN_HEADS, GDN_HEADS)
IN_COLS = NSA_WIDTH + 6 * NSA_KV_WIDTH + 3 * NSA_HEADS + 4 * GDN_WIDTH + 2 * GDN_HEADS

PEER_HEADS = 8
PEER_TOPK = 16
N_KEYS = 128
N_EXPERTS = N_KEYS * N_KEYS
PEER_DKEY = 256
PEER_TBLK = 128

NEG_INF = -1e30
FORCE = 1e4

kernel_name = 'hybrid_nsa_gdn_peer'

def _rmsnorm(x, g, eps=1e-6):
    xf = x.astype(jnp.float32)
    y = xf * lax.rsqrt(jnp.mean(xf * xf, axis=-1, keepdims=True) + eps)
    return (y * g.astype(jnp.float32)).astype(x.dtype)

def _l2norm(x, eps=1e-6):
    return x * lax.rsqrt(jnp.sum(x * x, axis=-1, keepdims=True) + eps)

def _rope(x, pos):
    d = x.shape[-1]
    half = d // 2
    inv = jnp.exp(-math.log(ROPE_THETA) * 2.0 * jnp.arange(half, dtype=jnp.float32) / d)
    ang = pos.astype(jnp.float32)[:, None] * inv[None, :]
    cos, sin = jnp.cos(ang), jnp.sin(ang)
    xf = x.astype(jnp.float32)
    x1, x2 = xf[..., :half], xf[..., half:]
    return jnp.concatenate([x1 * cos - x2 * sin, x2 * cos + x1 * sin], axis=-1).astype(x.dtype)

def _masked_softmax(s, mask):
    s = jnp.where(mask, s.astype(jnp.float32), NEG_INF)
    p = jax.nn.softmax(s, axis=-1)
    return p * jnp.any(mask, axis=-1, keepdims=True).astype(jnp.float32)

def _cmp_to_sel(p_cmp, n_blk):
    r = SEL_BLK // CMP_STRIDE
    l = CMP_BLK // CMP_STRIDE
    n_cmp = p_cmp.shape[-1]
    pad = [(0, 0)] * (p_cmp.ndim - 1) + [(l - 1, r * n_blk - n_cmp)]
    padded = jnp.pad(p_cmp, pad)
    out = jnp.zeros(p_cmp.shape[:-1] + (n_blk,), jnp.float32)
    for o in range(-(l - 1), r):
        w = float(min(o + l, r) - max(o, 0))
        start = o + l - 1
        out = out + w * padded[..., start:start + r * n_blk:r]
    return out

def _nsa(q_in, kc_in, vc_in, ks_in, vs_in, kw_in, vw_in, gate_in, q_gain, k_gain, cmp_pos, cmp_w1, cmp_w2):
    B, S, _ = q_in.shape
    G, HPG, DH = NSA_KV_GROUPS, NSA_HPG, NSA_HEAD_DIM
    pos = jnp.arange(S)
    q = q_in.reshape(B, S, G, HPG, DH).transpose(0, 2, 3, 1, 4)
    q = _rope(_rmsnorm(q, q_gain), pos)

    def heads(a):
        return a.reshape(B, S, G, DH).transpose(0, 2, 1, 3)

    l = CMP_BLK // CMP_STRIDE
    n_cmp = S // CMP_STRIDE - l + 1

    def compress(a, j):
        a16 = a.reshape(B, G, S // CMP_STRIDE, CMP_STRIDE, DH)
        blocks = jnp.concatenate([a16[:, :, i:i + n_cmp] for i in range(l)], axis=3)
        blocks = (blocks + cmp_pos[j]).reshape(B, G, n_cmp, CMP_BLK * DH)
        return jax.nn.gelu(blocks @ cmp_w1[j]) @ cmp_w2[j]

    cmp_end = jnp.arange(n_cmp) * CMP_STRIDE + CMP_BLK - 1
    kc = _rope(_rmsnorm(compress(heads(kc_in), 0), k_gain[0]), cmp_end)
    vc = compress(heads(vc_in), 1)
    n_blk = S // SEL_BLK
    ks = _rope(_rmsnorm(heads(ks_in), k_gain[1]), pos)
    ks_blk = ks.reshape(B, G, n_blk, SEL_BLK, DH)
    vs_blk = heads(vs_in).reshape(B, G, n_blk, SEL_BLK, DH)
    kw = _rope(_rmsnorm(heads(kw_in), k_gain[2]), pos)
    kw_pad = jnp.pad(kw, ((0, 0), (0, 0), (WINDOW, 0), (0, 0)))
    vw_pad = jnp.pad(heads(vw_in), ((0, 0), (0, 0), (WINDOW, 0), (0, 0)))

    n_sel = min(N_SEL, n_blk)
    scale = DH ** -0.5
    bi = jnp.arange(B)[:, None, None, None]
    gi = jnp.arange(G)[None, :, None, None]
    blk_ids = jnp.arange(n_blk)
    sel_off = jnp.arange(SEL_BLK)
    win_off = jnp.arange(WINDOW + Q_BLK) - WINDOW

    def block(args):
        qb, qq = args
        t0 = qb * Q_BLK
        t = t0 + jnp.arange(Q_BLK)
        s_c = jnp.einsum('bghtd,bgnd->bghtn', qq, kc) * scale
        p_c = _masked_softmax(s_c, cmp_end[None, :] <= t[:, None])
        o_c = jnp.einsum('bghtn,bgnd->bghtd', p_c.astype(vc.dtype), vc)
        imp = _cmp_to_sel(p_c, n_blk).sum(axis=2)
        cur = t // SEL_BLK
        forced = (blk_ids[None, :] == 0) | (blk_ids[None, :] == cur[:, None]) | (blk_ids[None, :] == cur[:, None] - 1)
        causal_blk = blk_ids[None, :] * SEL_BLK <= t[:, None]
        score = jnp.where(causal_blk, jnp.where(forced, FORCE, imp), NEG_INF)
        _, idx = lax.top_k(score, n_sel)
        k_g = ks_blk[bi, gi, idx].reshape(B, G, Q_BLK, n_sel * SEL_BLK, DH)
        v_g = vs_blk[bi, gi, idx].reshape(B, G, Q_BLK, n_sel * SEL_BLK, DH)
        pos_g = (idx[..., None] * SEL_BLK + sel_off).reshape(B, G, Q_BLK, n_sel * SEL_BLK)
        s_s = jnp.einsum('bghtd,bgtkd->bghtk', qq, k_g) * scale
        p_s = _masked_softmax(s_s, (pos_g <= t[:, None])[:, :, None])
        o_s = jnp.einsum('bghtk,bgtkd->bghtd', p_s.astype(v_g.dtype), v_g)
        k_w = lax.dynamic_slice_in_dim(kw_pad, t0, WINDOW + Q_BLK, axis=2)
        v_w = lax.dynamic_slice_in_dim(vw_pad, t0, WINDOW + Q_BLK, axis=2)
        pos_w = t0 + win_off
        rel = t[:, None] - pos_w[None, :]
        mask_w = (pos_w[None, :] >= 0) & (rel >= 0) & (rel < WINDOW)
        s_w = jnp.einsum('bghtd,bgkd->bghtk', qq, k_w) * scale
        p_w = _masked_softmax(s_w, mask_w)
        o_w = jnp.einsum('bghtk,bgkd->bghtd', p_w.astype(v_w.dtype), v_w)
        return o_c, o_s, o_w

    n_qb = S // Q_BLK
    q_blocks = q.reshape(B, G, HPG, n_qb, Q_BLK, DH).transpose(3, 0, 1, 2, 4, 5)
    o_c, o_s, o_w = lax.map(block, (jnp.arange(n_qb), q_blocks))
    o = jnp.stack([o_c, o_s, o_w], axis=-1)
    o = o.transpose(1, 0, 4, 2, 3, 5, 6).reshape(B, S, NSA_HEADS, DH, 3)
    gate = jax.nn.sigmoid(gate_in.astype(jnp.float32)).reshape(B, S, NSA_HEADS, 1, 3)
    return (o.astype(jnp.float32) * gate).sum(-1).reshape(B, S, NSA_WIDTH).astype(q_in.dtype)

def _gated_delta_chunked(q, k, v, g, beta):
    B, H, S, dk = q.shape
    dv = v.shape[-1]
    C = GDN_CHUNK
    N = S // C
    q = q.reshape(B, H, N, C, dk)
    k = k.reshape(B, H, N, C, dk)
    v = v.reshape(B, H, N, C, dv)
    beta = beta.reshape(B, H, N, C)
    g = jnp.cumsum(g.reshape(B, H, N, C), axis=-1)
    incl = jnp.tril(jnp.ones((C, C), bool))
    strict = jnp.tril(jnp.ones((C, C), bool), -1)
    diff = g[..., :, None] - g[..., None, :]
    decay = jnp.where(incl, jnp.exp(jnp.where(incl, diff, 0.0)), 0.0)
    kb = k * beta[..., None]
    a_mat = jnp.where(strict, jnp.einsum('bhnid,bhnjd->bhnij', kb, k) * decay, 0.0)
    m = a_mat + jnp.eye(C, dtype=jnp.float32)
    u = lax.linalg.triangular_solve(m, v * beta[..., None], left_side=True, lower=True)
    w = lax.linalg.triangular_solve(m, kb * jnp.exp(g)[..., None], left_side=True, lower=True)
    intra = jnp.where(incl, jnp.einsum('bhnid,bhnjd->bhnij', q, k) * decay, 0.0)
    q_dec = q * jnp.exp(g)[..., None]
    k_dec = k * jnp.exp(g[..., -1:] - g)[..., None]
    g_last = jnp.exp(g[..., -1])

    def step(state, xs):
        qd, kd, u_c, w_c, a_c, gl = xs
        v_new = u_c - jnp.einsum('bhck,bhkv->bhcv', w_c, state)
        o = jnp.einsum('bhck,bhkv->bhcv', qd, state) + jnp.einsum('bhcj,bhjv->bhcv', a_c, v_new)
        state = state * gl[..., None, None] + jnp.einsum('bhck,bhcv->bhkv', kd, v_new)
        return state, o

    xs = tuple(jnp.moveaxis(a, 2, 0) for a in (q_dec, k_dec, u, w, intra, g_last))
    _, o = lax.scan(step, jnp.zeros((B, H, dk, dv), jnp.float32), xs)
    return jnp.moveaxis(o, 0, 2).reshape(B, H, S, dv)

def _gdn(qkv, z, a, b, conv_w, a_log, dt_bias, out_gain):
    B, S, _ = qkv.shape
    H, DH = GDN_HEADS, GDN_HEAD_DIM
    xp = jnp.pad(qkv, ((0, 0), (CONV_K - 1, 0), (0, 0)))
    conv = xp[:, 0:S] * conv_w[0]
    for j in range(1, CONV_K):
        conv = conv + xp[:, j:j + S] * conv_w[j]
    conv = jax.nn.silu(conv)
    q, k, v = jnp.split(conv, 3, axis=-1)

    def heads(t):
        return t.reshape(B, S, H, DH).transpose(0, 2, 1, 3).astype(jnp.float32)

    q = _l2norm(heads(q)) * (DH ** -0.5)
    k = _l2norm(heads(k))
    v = heads(v)
    beta = jax.nn.sigmoid(b.astype(jnp.float32)).transpose(0, 2, 1)
    g = (-jnp.exp(a_log.astype(jnp.float32)) * jax.nn.softplus(a.astype(jnp.float32) + dt_bias.astype(jnp.float32))).transpose(0, 2, 1)
    o = _gated_delta_chunked(q, k, v, g, beta).transpose(0, 2, 1, 3)
    o = _rmsnorm(o, out_gain) * jax.nn.silu(z.reshape(B, S, H, DH).astype(jnp.float32))
    return o.reshape(B, S, GDN_WIDTH).astype(qkv.dtype)

def _peer(h, w_query, subkeys, u_tab, v_tab):
    B, S, D = h.shape
    T = B * S
    hf = h.reshape(T, D)
    qry = (hf @ w_query).reshape(T, PEER_HEADS, 2, PEER_DKEY // 2).astype(jnp.float32)
    s1 = jnp.einsum('thd,nd->thn', qry[:, :, 0], subkeys[0].astype(jnp.float32))
    s2 = jnp.einsum('thd,nd->thn', qry[:, :, 1], subkeys[1].astype(jnp.float32))
    v1, i1 = lax.top_k(s1, PEER_TOPK)
    v2, i2 = lax.top_k(s2, PEER_TOPK)
    cand = (v1[..., :, None] + v2[..., None, :]).reshape(T, PEER_HEADS, PEER_TOPK * PEER_TOPK)
    cidx = (i1[..., :, None] * N_KEYS + i2[..., None, :]).reshape(T, PEER_HEADS, PEER_TOPK * PEER_TOPK)
    top_s, top_pos = lax.top_k(cand, PEER_TOPK)
    eidx = jnp.take_along_axis(cidx, top_pos, axis=-1)
    gate = jax.nn.softmax(top_s, axis=-1)
    nb = T // PEER_TBLK

    def block(args):
        xb, eb, gb = args
        ue = u_tab[eb]
        act = jax.nn.gelu(jnp.einsum('td,thkd->thk', xb, ue).astype(jnp.float32))
        coef = (gb * act).astype(v_tab.dtype)
        return jnp.einsum('thk,thkd->td', coef, v_tab[eb])

    out = lax.map(block, (hf.reshape(nb, PEER_TBLK, D),
                          eidx.reshape(nb, PEER_TBLK, PEER_HEADS, PEER_TOPK),
                          gate.reshape(nb, PEER_TBLK, PEER_HEADS, PEER_TOPK)))
    return out.reshape(B, S, D).astype(h.dtype)

def setup_inputs(seed: int = 0) -> dict:
    key = jax.random.key(seed)
    ks = jax.random.split(key, 20)
    f32 = jnp.float32
    nrm = lambda k, shape, s: jax.random.normal(k, shape, f32) * s
    dt = jnp.exp(jax.random.uniform(ks[10], (DEPTH, GDN_HEADS), f32, math.log(1e-3), math.log(1e-1)))
    return {
        'x': nrm(ks[0], (BATCH, SEQ, D_MODEL), 1.0),
        'attn_norm': 1.0 + nrm(ks[1], (DEPTH, D_MODEL), 0.02),
        'w_in': nrm(ks[2], (DEPTH, D_MODEL, IN_COLS), D_MODEL ** -0.5),
        'nsa_q_gain': 1.0 + nrm(ks[3], (DEPTH, NSA_HEAD_DIM), 0.02),
        'nsa_k_gain': 1.0 + nrm(ks[4], (DEPTH, 3, NSA_HEAD_DIM), 0.02),
        'cmp_pos': nrm(ks[5], (DEPTH, 2, CMP_BLK, NSA_HEAD_DIM), 0.1),
        'cmp_w1': nrm(ks[6], (DEPTH, 2, CMP_BLK * NSA_HEAD_DIM, CMP_HID), (CMP_BLK * NSA_HEAD_DIM) ** -0.5),
        'cmp_w2': nrm(ks[7], (DEPTH, 2, CMP_HID, NSA_HEAD_DIM), CMP_HID ** -0.5),
        'gdn_conv': nrm(ks[8], (DEPTH, CONV_K, 3 * GDN_WIDTH), CONV_K ** -0.5),
        'gdn_a_log': jnp.log(jax.random.uniform(ks[9], (DEPTH, GDN_HEADS), f32, 1.0, 16.0)),
        'gdn_dt_bias': dt + jnp.log(-jnp.expm1(-dt)),
        'gdn_out_gain': 1.0 + nrm(ks[11], (DEPTH, GDN_HEAD_DIM), 0.02),
        'w_out': nrm(ks[12], (DEPTH, MIX_WIDTH, D_MODEL), MIX_WIDTH ** -0.5),
        'ffn_norm': 1.0 + nrm(ks[13], (DEPTH, D_MODEL), 0.02),
        'peer_w_query': nrm(ks[14], (DEPTH, D_MODEL, PEER_HEADS * PEER_DKEY), D_MODEL ** -0.5),
        'peer_subkeys': nrm(ks[15], (DEPTH, 2, N_KEYS, PEER_DKEY // 2), (PEER_DKEY // 2) ** -0.5),
        'peer_u': nrm(ks[16], (DEPTH, N_EXPERTS, D_MODEL), D_MODEL ** -0.5),
        'peer_v': nrm(ks[17], (DEPTH, N_EXPERTS, D_MODEL), 0.5),
    }

def reference(x, attn_norm, w_in, nsa_q_gain, nsa_k_gain, cmp_pos, cmp_w1, cmp_w2, gdn_conv, gdn_a_log,
              gdn_dt_bias, gdn_out_gain, w_out, ffn_norm, peer_w_query, peer_subkeys, peer_u, peer_v):
    offsets = np.cumsum(np.array(IN_SPLITS))[:-1].tolist()
    for l in range(DEPTH):
        h = _rmsnorm(x, attn_norm[l])
        proj = h @ w_in[l]
        q_a, kv_a, gate_a, qkv_b, z_b, a_b, b_b = jnp.split(proj, offsets, axis=-1)
        kc, vc, ks_, vs_, kw, vw = jnp.split(kv_a, 6, axis=-1)
        o_a = _nsa(q_a, kc, vc, ks_, vs_, kw, vw, gate_a, nsa_q_gain[l], nsa_k_gain[l],
                   cmp_pos[l], cmp_w1[l], cmp_w2[l])
        o_b = _gdn(qkv_b, z_b, a_b, b_b, gdn_conv[l], gdn_a_log[l], gdn_dt_bias[l], gdn_out_gain[l])
        x = x + jnp.concatenate([o_a, o_b], axis=-1) @ w_out[l]
        x = x + _peer(_rmsnorm(x, ffn_norm[l]), peer_w_query[l], peer_subkeys[l], peer_u[l], peer_v[l])
    return x


_drawn_inputs = setup_inputs


def setup_inputs(seed=0):
    import zlib

    import numpy as np

    out = dict(_drawn_inputs(seed))
    spreads = {}
    factors = {'nsa_q_gain': 4.114, 'nsa_k_gain': 4.711}
    for name, (base, spread) in spreads.items():
        noise = np.random.default_rng([zlib.crc32(name.encode()), seed]).standard_normal(out[name].shape)
        drawn = base * np.exp(spread * noise) if base else spread * noise
        out[name] = jnp.asarray(drawn.astype(out[name].dtype))
    for name, factor in factors.items():
        out[name] = (out[name] * factor).astype(out[name].dtype)
    return out
```

```python
import math

import numpy as np
import concourse.bass as bass
from concourse import mybir
from concourse.alu_op_type import AluOpType as ALU
from contextlib import ExitStack

F32 = mybir.dt.float32
F32R = mybir.dt.float32r
U32 = mybir.dt.uint32
BF16 = mybir.dt.bfloat16
ACT = mybir.ActivationFunctionType
AX = mybir.AxisListType

P = 128
D, S = 1024, 256
DC = D // P
NT = S // P
HEADS, GROUPS, DH = 8, 2, 64
CMP_BLK, CMP_STRIDE, CMP_HID = 32, 16, 256
NCMP = S // CMP_STRIDE - CMP_BLK // CMP_STRIDE + 1
NC16 = 16
THETA = 10000.0
GH, GD, CONV_K, CHUNK = 4, 128, 4, 64
GW = GH * GD
PH, TOPK, NKEYS = 8, 16, 128
NEG = -1e30
LOWEST = -3.0e38
EPS = 1e-6
SLOT = DC * 512
MISC = 2 * GROUPS * DH + 3 * HEADS + 2 * GH
LEVELS = 6

CONST = {}


def _layout(table, widths):
    at = 0
    for name, n in widths:
        table[name] = (at, at + n)
        at += n
    return at


NCONST = _layout(CONST, [("upper", P), ("nlower", P), ("strict", P), ("nm0", P), ("nm0t", P)]
                 + [(f"mt{l}", P) for l in range(1, LEVELS)]
                 + [("negc", NT * S), ("cneg", NT * NC16), ("any", NT), ("cos", NT * DH), ("sin", NT * DH),
                    ("cosc", DH), ("sinc", DH), ("pm", 2), ("hm", HEADS)])
PARAM = {}
NPARAM = _layout(PARAM, [("gains", 12 * DH), ("kg0", DH), ("outg", GD), ("alog", GH), ("dtb", GH), ("attng", DC),
                         ("conv", 12 * CONV_K), ("pos", 2 * CMP_BLK // 2), ("w2", 2 * 2 * DH)])


def constants():
    c = np.zeros((P, NCONST), np.float32)

    def put(name, a):
        lo, hi = CONST[name]
        c[:a.shape[0], lo:hi] = a.reshape(a.shape[0], -1)

    p, x = np.arange(P)[:, None], np.arange(P)[None, :]
    same = p // CHUNK == x // CHUNK
    put("upper", (p <= x) & same)
    put("nlower", -1.0 * ((p >= x) & same))
    put("strict", (p > x) & same)
    for l in range(LEVELS):
        s = 1 << l
        m = (p // (2 * s) == x // (2 * s)) & (p // s % 2 == 1) & (x // s % 2 == 0)
        if l == 0:
            put("nm0", -1.0 * m)
            put("nm0t", -1.0 * m.T)
        else:
            put(f"mt{l}", m.T)
    t = np.arange(S).reshape(NT, P)
    put("negc", np.where(np.arange(S)[None, None, :] <= t.T[:, :, None], 0.0, NEG))
    n = np.arange(NC16)
    ends = n * CMP_STRIDE + CMP_BLK - 1
    seen = (ends[None, None, :] <= t.T[:, :, None]) & (n < NCMP)[None, None, :]
    put("cneg", np.where(seen, 0.0, NEG))
    put("any", seen.any(-1))
    half = DH // 2
    inv = np.exp(np.float32(-math.log(THETA) * 2.0) * np.arange(half, dtype=np.float32) / np.float32(DH)).astype(np.float32)

    def rope(pos):
        a = pos.astype(np.float32)[..., None] * inv
        return np.concatenate([np.cos(a)] * 2, -1), np.concatenate([-np.sin(a), np.sin(a)], -1)

    cos, sin = rope(t.T)
    put("cos", cos)
    put("sin", sin)
    cos, sin = rope(np.concatenate([ends, ends]))
    put("cosc", cos)
    put("sinc", sin)
    put("pm", p // 64 == np.arange(2)[None, :])
    put("hm", p // NC16 == np.arange(HEADS)[None, :])
    return c


def keep_constants():
    c = np.zeros((P, 2 * P), np.float32)
    c[:, :P] = np.eye(P)
    c[:, P:] = np.arange(P)[None, :]
    return c


def units():
    out = [(0, br, h, 4) for br in range(2) for h in (0, 4)]
    return out + [(1, br, h, 2) for br in range(2) for h in range(0, 8, 2)]


UNITS = units()


def job_list():
    jobs = [("ssq",), ("misc", 0), ("misc", 1)]
    jobs += [("qkv", b) for b in range(6)]
    jobs += [("gcol",), ("gb", 0), ("gb", 1)]
    jobs += [("l2", b) for b in range(4)]
    jobs += [("qp", 0), ("qp", 1), ("kvp", 0), ("kvp", 1), ("zp", 0), ("zp", 1)]
    jobs += [("kk", 0), ("kk", 1), ("at", 0), ("at", 1), ("kq", 0), ("kq", 1)]
    jobs += [("ktok", 0), ("ktok", 1), ("vtok", 0), ("vtok", 1)]
    jobs += [("kvct", 0), ("kvct", 1), ("qt", 0), ("kt", 0), ("qt", 1), ("kt", 1)]
    gdn = []
    for l in range(1, LEVELS):
        gdn += [[("w", l, 0), ("w", l, 1)], [("pa", l, 0), ("pb", l, 0), ("pa", l, 1), ("pb", l, 1)]]
    gdn += [[("u", 0), ("wt", 0), ("u", 1), ("wt", 1)], [("kv", 0)]]
    for c in range(1, 4):
        gdn += [[("vn", c)], [("o1", c)] + ([("kv", c)] if c < 3 else [])]
        if c % 2:
            gdn[-1] += [("o2", c // 2)]
    nsa = [("h1", 0), ("h1", 1), ("c2k",), ("c2v",), ("s", 0), ("s", 1), ("kct",), ("sc", 0), ("sc", 1)]
    tail = []
    for u in range(len(UNITS) + 2):
        if u >= 2:
            tail.append(("o", u - 2))
        if u < len(UNITS):
            tail.append(("pt", u))
        if u + 2 < len(UNITS):
            tail.append(("s", u + 2))
        if u == 0:
            tail += [("pct", 0), ("pct", 1)]
        if u == 1:
            tail += [("oc", 0), ("oc", 1)]
    nsa += tail
    at = 0
    for i, g in enumerate(gdn):
        jobs += g
        until = len(nsa) * (i + 1) // len(gdn)
        jobs += nsa[at:until]
        at = until
    jobs += [("ot", T, hf) for T in range(NT) for hf in range(2)]
    jobs += [("y", T, hf) for T in range(NT) for hf in range(2)]
    jobs += [("xt", b) for b in range(4)]
    jobs += [("q", b) for b in range(8)]
    jobs += [("sk", T, b) for T in range(NT) for b in range(4)]
    return jobs


JOBS = job_list()
JOB = {j: n for n, j in enumerate(JOBS)}
BANKS = 8
TOPK_LINKS = 10
PARTS = 3
OH_TOKENS = 8
RSLOTS = 4
NBLK = NKEYS
Q = NBLK // 2 // RSLOTS
SPLIT = (512, 384, 384, 512)
G_BANK, A_BANK = 4, 6
SLOTS = 4
LOADS = [("misc", 1), ("qkv", 1), ("qkv", 3), ("qkv", 5), ("qp", 1), ("kvp", 1), ("zp", 1), ("h1", 0), ("h1", 1),
         ("y", 1, 0), ("y", 1, 1), ("q", 1), ("q", 3), ("q", 5), ("q", 7)]


def build(nc, dram, out_d):
    consts_d, keep_d, params_d, ffng_d, xt_d, x_d, wmisc_d, wslots_d, subk_d, u_d, v_d = (
        dram[n] for n in ("consts", "keep", "params", "ffng", "xt", "x", "wmisc", "wslots", "subk", "u", "v"))
    ctx = ExitStack()
    with ctx:
        def sem(name):
            return ctx.enter_context(nc.semaphore(name))

        def sb(name, cols, dt=F32, where=None, parts=P):
            return (where or ctx).enter_context(nc.sbuf_tensor(name, [parts, cols], dt))

        X = sb("X", NT * D)[:, :].rearrange("p (t d) -> p t d", t=NT)
        KEEP = sb("KEEP", 2 * P)
        IDENT, IOTA = KEEP[:, 0:P], KEEP[:, P:2 * P]
        FFNG = sb("FFNG", DC)[:, :]
        MHALF = sb("MHALF", 1)[:, :]
        SUBK = sb("SUBK", 2 * P)[:, :].rearrange("p (h n) -> p h n", h=2)
        PS = ctx.enter_context(nc.psum_tensor("PS", [P, BANKS, 512], F32))

        early = ExitStack()
        W = sb("W", SLOTS * SLOT, where=early)
        ONES = sb("ONES", P, where=early)
        F_COLS = 34000
        FB = sb("FB", F_COLS, where=early)
        top = [0]

        def take(n, at=None):
            lo = top[0] if at is None else at
            if at is None:
                top[0] += n
                assert top[0] <= F_COLS, top[0]
            return FB[:, lo:lo + n]

        early.close()

        C = take(NCONST)
        PR = take(NPARAM)

        def const(name):
            return C[:, CONST[name][0]:CONST[name][1]]

        def param(name):
            return PR[:, PARAM[name][0]:PARAM[name][1]]

        XT_AT = top[0]
        XT = take(DC * S).rearrange("p (c t) -> p c t", c=DC)
        HT = take(DC * S).rearrange("p (c t) -> p c t", c=DC)
        QP_AT = top[0]
        QPW = S + 4
        QP = take(12 * QPW).rearrange("p (b t) -> p b t", b=12)
        CV_AT = top[0]
        CV = take(12 * S).rearrange("p (b t) -> p b t", b=12)
        RN_AT = top[0]
        RN = take(8 * S).rearrange("p (b t) -> p b t", b=8)
        OC_AT = top[0]
        XR = take(NT * 8 * DH).rearrange("p (t h d) -> p t h d", t=NT, d=DH)
        KR = take(NT * 4 * 2 * DH).rearrange("p (t h r d) -> p t h r d", t=NT, r=2, d=DH)
        VSW = take(NT * 4 * DH).rearrange("p (t h d) -> p t h d", t=NT, d=DH)
        GAB = take(NT * 32).rearrange("p (t n) -> p t n", t=NT)
        SG = take(NT * 28).rearrange("p (t n) -> p t n", t=NT)
        Z = take(NT * GW).rearrange("p (t n) -> p t n", t=NT)

        def mat():
            return take(NT * GW).rearrange("p (t h n) -> p t h n", t=NT, h=GH)

        DL, DU, EG, AM, AT_, TI, TT, KBG, KD, VB = (mat() for _ in range(10))
        STATE = take(GW).rearrange("p (h n) -> p h n", h=GH)
        TMP = take(1024)
        TMP2 = take(512)
        KCBD = take(64).rearrange("p (g r n) -> p g r n", g=2, r=2)
        HK = take(64).rearrange("p (c n) -> p c n", c=2)
        HV = take(256).rearrange("p (c g m n) -> p c g m n", c=2, g=2, m=4)
        PC = [take(128) for _ in range(2)]
        KC, KC2, KC3 = take(64), take(128), take(64)
        SQ = take(8 * S, at=XT_AT).rearrange("p (b t) -> p b t", b=8)
        XN = X[:, :, 0:768].rearrange("p t (h d) -> p t h d", d=DH)
        KCV = take(NT * 4 * 2 * DH, at=RN_AT).rearrange("p (t h r d) -> p t h r d", t=NT, r=2, d=DH)
        X2 = take(4 * S, at=XT_AT).rearrange("p (k t) -> p k t", k=4)
        YB = take(2 * 16 * 32, at=XT_AT + 4 * S).rearrange("p (k m g n) -> p k m g n", k=2, m=16, g=2)
        KZ = take(4 * 2 * S, at=CV_AT).rearrange("p (b g r t) -> p b g r t", b=2, g=2, r=2)
        QT = take(NT * 512, at=CV_AT + 8 * S).rearrange("p (a t) -> p a t", a=4)
        CT = [take(NT * GW, at=RN_AT + i * NT * GW).rearrange("p (t h n) -> p t h n", t=NT, h=GH) for i in range(2)]
        SM = [take(512, at=QP_AT + 512 * i) for i in range(2)]
        PT = [take(512, at=QP_AT + 1024 + 512 * i).rearrange("p (b t) -> p b t", b=4) for i in range(3)]
        VBD = take(512, at=QP_AT + 2560).rearrange("p (h d) -> p h d", h=HEADS)
        OC = take(NT * D, at=OC_AT).rearrange("p (t d) -> p t d", t=NT)
        OT = take(DC * S, at=XT_AT + 2048).rearrange("p (c t) -> p c t", c=DC)
        XNORM = take(NT * D, at=RN_AT).rearrange("p (t d) -> p t d", t=NT)
        WW, U, WT, OG, QD = AM, DL, AM, TI, EG
        PCT = take(256)
        SMA = take(320)
        sm_at = [0]

        def small(n):
            lo = sm_at[0]
            sm_at[0] += n
            assert sm_at[0] <= 320
            return SMA[:, lo:lo + n]

        rs12 = small(24).rearrange("p (t n) -> p t n", t=NT)
        gcs = small(16).rearrange("p (t n) -> p t n", t=NT)
        egs = small(16).rearrange("p (t n) -> p t n", t=NT)
        gate_b = small(8).rearrange("p (t n) -> p t n", t=NT)
        gls = small(16).rearrange("p (t f n) -> p t f n", t=NT, f=2)
        bg = small(8).rearrange("p (t n) -> p t n", t=NT)
        gstep = small(8).rearrange("p (t n) -> p t n", t=NT)
        aexp = small(4)
        sp1 = small(8).rearrange("p (t n) -> p t n", t=NT)
        sp2 = small(8).rearrange("p (t n) -> p t n", t=NT)
        mx = small(8)
        nm = [small(4), small(4)]
        rs = small(48).rearrange("p (u n) -> p u n", u=12)
        rr = small(48).rearrange("p (u n) -> p u n", u=12)
        cs = [small(8), small(8)]
        rc = [small(8), small(8)]
        gr = small(8).rearrange("p (t n) -> p t n", t=NT)
        xs = small(2)
        kcs = small(1)
        EPSC = small(1)

        GATED = sb("GATED", NKEYS * S)
        H2H, H2L = sb("H2H", DC * S, F32R), sb("H2L", DC * S, F32R)
        TABH, TABL = sb("TABH", 2 * D, F32R), sb("TABL", 2 * D, F32R)
        RING = sb("RING", RSLOTS * D)
        CFH, CFL = sb("CFH", 2 * S, F32R), sb("CFL", 2 * S, F32R)
        H2T = sb("H2T", DC * S)
        ROUTE = sb("ROUTE", 3 * S)
        ROUTE_T = sb("ROUTE_T", (2 + PARTS) * S)
        GPART = sb("GPART", S, BF16)
        TOK = sb("TOK", (2 + PARTS) * 16)[:, :].rearrange("p (c q) -> p c q", c=2 + PARTS)
        h2t_at = [0]

        def after_h2t(n):
            h2t_at[0] += n
            return H2T[:, h2t_at[0] - n:h2t_at[0]]

        ONEHOT2 = after_h2t(OH_TOKENS * P // 2).bitcast(BF16).rearrange("p (q n) -> p q n", q=OH_TOKENS)
        ONEHOT1 = after_h2t(OH_TOKENS * PARTS * 64 // 2).bitcast(BF16).rearrange("p (q c n) -> p q c n", q=OH_TOKENS, c=PARTS)
        EQ1 = after_h2t(4 * 64).rearrange("p (q n) -> p q n", q=4)
        GREST = after_h2t(S)
        TOPT = 18432
        QRY = GATED[:, TOPT:TOPT + 16 * S].rearrange("p (b t) -> p b t", b=16)
        SCORES = GATED[:, TOPT + 16 * S:TOPT + 32 * S]
        kt_at = [TOPT + 32 * S]

        def ktake(n):
            kt_at[0] += n
            return GATED[:, kt_at[0] - n:kt_at[0]]

        KS = ktake(2 * NKEYS).rearrange("p (f n) -> p f n", f=2)
        KV_ = ktake(2 * TOPK).rearrange("p (f k) -> p f k", f=2)
        KI = ktake(2 * TOPK).bitcast(U32).rearrange("p (f k) -> p f k", f=2)
        KIF = ktake(2 * TOPK).rearrange("p (f k) -> p f k", f=2)
        CAND = ktake(TOPK * TOPK)
        POS = ktake(TOPK).bitcast(U32)
        POSF = ktake(2 * TOPK).rearrange("p (f k) -> p f k", f=2)
        POSU = ktake(2 * TOPK).bitcast(U32).rearrange("p (f k) -> p f k", f=2)
        EQ = ktake(2 * TOPK * TOPK).rearrange("p (f k a) -> p f k a", f=2, k=TOPK)
        RES = ktake(TOPK)
        GSUM = ktake(2 * PH)[:, :]
        CARRIER = ktake(4)

        consts_in, xt_in, x_in, subk_in = sem("consts_in"), sem("xt_in"), sem("x_in"), sem("subk_in")
        weights_in = [sem(f"weights_in{i}") for i in range(SLOTS)]
        ps_full = sem("ps_full")
        ps_free = [sem(f"ps_free{b}") for b in range(BANKS)]
        dve_link, act_link, pool_link = sem("dve_link"), sem("act_link"), sem("pool_link")
        names = ("ones_ready xsq_ready hT_ready qp_zero exp_misc_done sig_ready softplus_in softplus_exp "
                 "softplus_ln g_ready conv_ready silu_done sq_ready kqT_ready eg_exp gcs_exp darg_ready dexp_done "
                 "dmask_done ti_init tt_init ct_ready qd_ready og_zero og_mean og_rstd oc_gdn xq_mean xq_rstd xr_ready "
                 "y_ready kc_mean kc_rstd kcr_ready sm_ready p_ready scm_ready pc_ready oc_nsa x1_mean x1_rstd "
                 "xn_ready gls_ready").split()
        s = {n: sem(n) for n in names}

        table_in = [sem(f"table_in{k}") for k in range(RSLOTS)]
        tab_hi = sem("tab_hi")
        tab_lo_dve, tab_lo_pool = sem("tab_lo_dve"), sem("tab_lo_pool")
        blocks_done = sem("blocks_done")
        gelu_done = sem("gelu_done")
        coef_hi, coef_lo_pool, coef_lo_dve = sem("coef_hi"), sem("coef_lo_pool"), sem("coef_lo_dve")
        onehot_ready, gate_mm, gated = sem("onehot_ready"), sem("gate_mm"), sem("gated")
        route_exp_in, route_exp, route_ready, route_t = sem("route_exp_in"), sem("route_exp"), sem("route_ready"), sem("route_t")
        route_t_in, h2_ready, h2h_ready, h2l_ready = sem("route_t_in"), sem("h2_ready"), sem("h2h_ready"), sem("h2l_ready")
        topk_link, tok_ready = sem("topk_link"), sem("tok_ready")
        eq1_ready, keys_ready, cand_ready = sem("eq1_ready"), sem("keys_ready"), sem("cand_ready")
        places_ready, placed = sem("places_ready"), sem("placed")
        out_ready, out_done = sem("out_ready"), sem("out_done")

        def view(t, offset, *dims):
            a = t[:, 0:1]
            return bass.AP(a.tensor, offset, [list(a.ap[0])] + [list(d) for d in dims])

        def table_rest(engine, k, lo, hi):
            h = k % 2 * D
            return engine.tensor_tensor(TABL[:, h + lo:h + hi], RING[:, k * D + lo:k * D + hi],
                                        TABH[:, h + lo:h + hi].bitcast(F32), ALU.subtract)

        def coef_rest(engine, b, k):
            cols = slice(k % 2 * S, (k % 2 + 1) * S)
            return engine.tensor_tensor(CFL[:, cols], view(GATED, (b - NBLK) * S, (1, S)), CFH[:, cols].bitcast(F32),
                                        ALU.subtract)

        def phases(eng, step, finish=None):
            for ph in range(4):
                step(ph, 0)
                with eng.Fori(1, Q - 1) as m:
                    step(ph, m)
                step(ph, Q - 1)
                if finish:
                    finish(ph)

        def wait(eng, semaphore, value):
            if not isinstance(value, int) or value > 0:
                eng.wait_ge(semaphore, value)

        def full(eng, *job):
            eng.wait_ge(ps_full, JOB[job] + 1)

        def evacuated(eng, *job):
            n = JOB[job]
            eng.wait_ge(ps_free[n % BANKS], n // BANKS + 1)

        def bank(*job):
            return PS[:, JOB[job] % BANKS, :]

        def release(ins, *job):
            ins.then_inc(ps_free[JOB[job] % BANKS], 1)

        def wslot(n):
            return W[:, (n % SLOTS) * SLOT:(n % SLOTS + 1) * SLOT]

        block = ctx.enter_context(nc.Block())

        @block.sync
        def _(sp):
            sp.dma_start(XT.rearrange("p c t -> p (c t)"), xt_d).then_inc(xt_in, 16)
            sp.dma_start(W[:, 0:DC * MISC], wmisc_d).then_inc(weights_in[0], 16)
            sp.dma_start(C, consts_d).then_inc(consts_in, 16)
            sp.dma_start(PR, params_d).then_inc(consts_in, 16)
            sp.dma_start(KEEP[:, :], keep_d).then_inc(consts_in, 16)
            for n in range(1, len(LOADS)):
                if n >= SLOTS:
                    full(sp, *LOADS[n - SLOTS])
                sp.dma_start(wslot(n), wslots_d[n - 1]).then_inc(weights_in[n % SLOTS], 16)
                if n == 6:
                    sp.dma_start(FFNG, ffng_d).then_inc(subk_in, 16)
                    sp.dma_start(SUBK.rearrange("p h n -> p (h n)"), subk_d).then_inc(subk_in, 16)
                if n == 9:
                    sp.wait_ge(s["xr_ready"], 4)
                    sp.dma_start(X.rearrange("p t d -> p (t d)"), x_d).then_inc(x_in, 16)

            def table(t_d, i, k):
                a = t_d[0]
                sp.dma_start(RING[:, k * D:(k + 1) * D], bass.AP(a.tensor, i * (P * D), [[D, P], [1, D]]))\
                    .then_inc(table_in[k], 16)

            def step(ph, m):
                for k in range(RSLOTS):
                    b = 4 * m + 4 * Q * ph + k
                    wait(sp, tab_lo_dve, b - RSLOTS + 1)
                    wait(sp, tab_lo_pool, b - RSLOTS + 1)
                    table(u_d if ph < 2 else v_d, b - (0 if ph < 2 else NBLK), k)

            sp.wait_ge(s["xn_ready"], NT)
            phases(sp, step)
            for t in range(NT):
                sp.wait_ge(out_ready, 2 * (t + 1))
                sp.dma_start(out_d[:, t * D:(t + 1) * D], X[:, t]).then_inc(out_done, 16)
            sp.wait_ge(out_done, 16 * NT)

        @block.gpsimd
        def _(pool):
            g = nc.gpsimd
            count = [0]

            def link(ins):
                count[0] += 1
                ins.then_inc(pool_link, 1)
                pool.wait_ge(pool_link, count[0])

            def power(out, in_, shape):
                e = MHALF[0:shape[0], :]
                for _ in range(len(shape) - 2):
                    e = e.unsqueeze(1)
                return g.tensor_tensor(out, in_, e.to_broadcast(shape), ALU.pow)

            link(g.memset(MHALF, -0.5))
            g.memset(QP[:, :, 0:CONV_K - 1], 0.0).then_inc(s["qp_zero"], 1)
            for T in range(NT):
                pool.wait_ge(s["dexp_done"], 2 * T + 2)
                g.tensor_tensor(DL[:, T], DL[:, T], const("strict").unsqueeze(1).to_broadcast([P, GH, P]), ALU.mult)\
                    .then_inc(s["dmask_done"], 1)
                g.tensor_tensor(DU[:, T], DU[:, T], const("upper").unsqueeze(1).to_broadcast([P, GH, P]), ALU.mult)\
                    .then_inc(s["dmask_done"], 1)
            for T in range(NT):
                pool.wait_ge(s["xq_mean"], T + 1)
                power(rs12[:, T], rs12[:, T], [P, 12]).then_inc(s["xq_rstd"], 1)
            pool.wait_ge(s["kqT_ready"], 8)
            pool.wait_ge(s["gls_ready"], 2 * NT)
            for T in range(NT):
                g.tensor_tensor(QD[:, T], EG[:, T], CV[:, 0:4, T * P:(T + 1) * P], ALU.mult).then_inc(s["qd_ready"], 1)
            for l in range(1, LEVELS):
                for T in range(NT):
                    evacuated(pool, "at", T)
                    if l >= 3:
                        full(pool, "w", l - 2, T)
                    if l == 2:
                        full(pool, "kvct", 1)
                    g.tensor_tensor(CT[l % 2][:, T], AT_[:, T],
                                    const(f"mt{l}").unsqueeze(1).to_broadcast([P, GH, P]), ALU.mult)\
                        .then_inc(s["ct_ready"], 1)
                if l == 2:
                    pool.wait_ge(s["kc_mean"], 1)
                    power(kcs[0:32, :], kcs[0:32, :], [32, 1]).then_inc(s["kc_rstd"], 1)
            for T in range(NT):
                pool.wait_ge(s["og_mean"], T + 1)
                power(gr[:, T], gr[:, T], [P, GH]).then_inc(s["og_rstd"], 1)
            for T in range(NT):
                pool.wait_ge(s["x1_mean"], T + 1)
                power(xs[:, T:T + 1], xs[:, T:T + 1], [P, 1]).then_inc(s["x1_rstd"], 1)

            def step(ph, m):
                for k in range(RSLOTS):
                    b = 4 * m + 4 * Q * ph + k
                    if ph == 2:
                        pool.wait_ge(coef_hi, b - NBLK + 1)
                        coef_rest(g, b, k).then_inc(coef_lo_pool, 1)
                    pool.wait_ge(tab_hi, 2 * b + 1)
                    table_rest(g, k, SPLIT[ph], D).then_inc(tab_lo_pool, 1)
                    if ph == 0 and k == 2 and not (isinstance(m, int) and m == 0):
                        place(m - 1)
                    if ph == 0 and k == 1:
                        pool.wait_ge(keys_ready, m + 1)
                        shape = [P, TOPK, TOPK]
                        g.tensor_tensor(CAND.rearrange("p (a b) -> p a b", a=TOPK), KV_[:, 0].unsqueeze(2).to_broadcast(shape),
                                        KV_[:, 1].unsqueeze(1).to_broadcast(shape), ALU.add).then_inc(cand_ready, 1)

            def place(m):
                pool.wait_ge(places_ready, m + 1)
                g.tensor_tensor(EQ, EQ, KIF.unsqueeze(2).to_broadcast([P, 2, TOPK, TOPK]), ALU.mult).then_inc(placed, 1)

            def finish(ph):
                if ph == 0:
                    place(Q - 1)

            phases(pool, step, finish)

        @block.tensor
        def _(pe):
            mm = nc.tensor.matmul

            def begin(*job):
                n = JOB[job]
                if n >= BANKS:
                    pe.wait_ge(ps_free[n % BANKS], n // BANKS)
                return bank(*job)

            def end(ins):
                ins.then_inc(ps_full, 1)

            def weights(n):
                pe.wait_ge(weights_in[n % SLOTS], 16 * (n // SLOTS + 1))
                return wslot(n)

            def rows(job, b, lhs, w, lo, n):
                for c in range(DC):
                    last = mm(b[:, 0:n], lhs[:, c], w[:, c, lo:lo + n], start=c == 0, stop=c == DC - 1)
                end(last)

            def transposes(job, b, ins_, ident=IDENT):
                for i, a in enumerate(ins_):
                    last = nc.tensor.transpose(b[:, i * P:(i + 1) * P], a, ident)
                end(last)

            def run(job):
                kind, *a = job
                T = a[-1] if a else 0
                b = begin(*job)
                if kind == "ssq":
                    pe.wait_ge(s["ones_ready"], 1)
                    for c in range(DC):
                        pe.wait_ge(s["xsq_ready"], c // 4 + 1)
                        last = mm(b[:, 0:S], ONES[:, :], CV[:, c], start=c == 0, stop=c == DC - 1)
                    end(last)
                elif kind == "misc":
                    w = weights(0)[:, 0:DC * MISC].rearrange("p (c n) -> p c n", c=DC)
                    pe.wait_ge(s["hT_ready"], 1)
                    rows(job, b, HT[:, :, T * P:(T + 1) * P], w, 0, MISC)
                elif kind == "qkv":
                    w = weights(1 + a[0] // 2).rearrange("p (c n) -> p c n", c=DC)
                    for i in range(2):
                        o = (2 * a[0] + i) % 4 * P
                        for c in range(DC):
                            last = mm(b[:, i * S:(i + 1) * S], w[:, c, o:o + P], HT[:, c], start=c == 0, stop=c == DC - 1)
                    end(last)
                elif kind in ("qp", "kvp", "zp"):
                    n = {"qp": 4, "kvp": 5, "zp": 6}[kind]
                    w = weights(n).rearrange("p (c n) -> p c n", c=DC)
                    rows(job, b, HT[:, :, T * P:(T + 1) * P], w, 0, 512)
                elif kind == "gcol":
                    pe.wait_ge(s["g_ready"], 1)
                    for t in range(NT):
                        mm(b[:, t * 8:t * 8 + 4], const("upper"), gstep[:, t], start=True, stop=True)
                        last = mm(b[:, t * 8 + 4:t * 8 + 8], const("strict"), gstep[:, t], start=True, stop=True)
                    end(last)
                elif kind == "gb":
                    for h in range(GH):
                        last = mm(b[:, h * P:(h + 1) * P], gstep[:, T, h:h + 1].to_broadcast([P, P]), const("upper"),
                                  start=True, stop=True)
                    end(last)
                elif kind == "l2":
                    pe.wait_ge(s["sq_ready"], a[0] + 1)
                    last = mm(b[:, :], ONES[:, :], SQ[:, 2 * a[0]:2 * a[0] + 2], start=True, stop=True)
                    end(last)
                elif kind in ("kk", "kq"):
                    pe.wait_ge(s["kqT_ready"], 8)
                    ts = slice(T * P, (T + 1) * P)
                    for h in range(GH):
                        last = mm(b[:, h * P:(h + 1) * P], CV[:, 4 + h, ts], CV[:, (4 if kind == "kk" else 0) + h, ts],
                                  start=True, stop=True)
                    end(last)
                elif kind == "at":
                    evacuated(pe, "kk", T)
                    transposes(job, b, [AM[:, T, h] for h in range(GH)])
                elif kind == "ktok":
                    pe.wait_ge(s["kqT_ready"], 8)
                    transposes(job, b, [CV[:, 4 + h, T * P:(T + 1) * P] for h in range(GH)])
                elif kind == "vtok":
                    pe.wait_ge(s["silu_done"], 6)
                    transposes(job, b, [CV[:, 8 + h, T * P:(T + 1) * P] for h in range(GH)])
                elif kind == "kvct":
                    evacuated(pe, "kvp", T)
                    transposes(job, b, [KCV[:, T, i] for i in range(4)])
                elif kind == "qt":
                    pe.wait_ge(s["xr_ready"], 2 * T + 1)
                    transposes(job, b, [XR[:, T, 2 * i:2 * i + 2] for i in range(4)])
                elif kind == "kt":
                    pe.wait_ge(s["xr_ready"], 2 * T + 2)
                    transposes(job, b, [KR[:, T, i] for i in range(4)])
                elif kind == "w":
                    l = a[0]
                    pe.wait_ge(s["ct_ready"], NT * (l - 1) + T + 1)
                    if l == 1:
                        pe.wait_ge(s["ti_init"], T + 1)
                    else:
                        evacuated(pe, "pa", l - 1, T)
                    for h in range(GH):
                        last = mm(b[:, h * P:(h + 1) * P], CT[l % 2][:, T, h], TI[:, T, h], start=True, stop=True)
                    end(last)
                elif kind in ("pa", "pb"):
                    l = a[0]
                    evacuated(pe, "w", l, T)
                    if l == 1:
                        pe.wait_ge(s["tt_init"], T + 1)
                    else:
                        evacuated(pe, "pb", l - 1, T)
                    for h in range(GH):
                        lhs, rhs = (TT[:, T, h], WW[:, T, h]) if kind == "pa" else (WW[:, T, h], TT[:, T, h])
                        last = mm(b[:, h * P:(h + 1) * P], lhs, rhs, start=True, stop=True)
                    end(last)
                elif kind in ("u", "wt"):
                    evacuated(pe, "pb", LEVELS - 1, T)
                    evacuated(pe, "vtok" if kind == "u" else "ktok", T)
                    for h in range(GH):
                        lhs, rhs = (TT[:, T, h], VB[:, T, h]) if kind == "u" else (KBG[:, T, h], TT[:, T, h])
                        last = mm(b[:, h * P:(h + 1) * P], lhs, rhs, start=True, stop=True)
                    end(last)
                elif kind == "kv":
                    c = a[0]
                    t, r = c // 2, slice(64 * (c % 2), 64 * (c % 2) + 64)
                    if c == 0:
                        evacuated(pe, "u", 0)
                    else:
                        evacuated(pe, "vn", c)
                    for h in range(GH):
                        last = mm(b[:, h * P:(h + 1) * P], KD[r, t, h], U[r, t, h], start=True, stop=True)
                    end(last)
                elif kind in ("vn", "o1"):
                    c = a[0]
                    t, r = c // 2, slice(64 * (c % 2), 64 * (c % 2) + 64)
                    if kind == "vn":
                        evacuated(pe, "wt", t)
                        evacuated(pe, "kv", c - 1)
                    else:
                        pe.wait_ge(s["qd_ready"], NT)
                    src = WT if kind == "vn" else QD
                    for h in range(GH):
                        last = mm(b[r, h * P:(h + 1) * P], src[:, t, h, r], STATE[:, h], start=True, stop=True)
                    end(last)
                elif kind == "o2":
                    evacuated(pe, "vn", 2 * T + 1)
                    if T:
                        evacuated(pe, "vn", 2 * T)
                    evacuated(pe, "kq", T)
                    for h in range(GH):
                        last = mm(b[:, h * P:(h + 1) * P], DU[:, T, h], U[:, T, h], start=True, stop=True)
                    end(last)
                elif kind == "h1":
                    kv = a[0]
                    w = weights(7 + kv).rearrange("p (m n) -> p m n", m=16)
                    pe.wait_ge(s["y_ready"], kv + 1)
                    for hc in range(2):
                        for m in range(16):
                            last = mm(b[:, hc * 32:hc * 32 + 32], w[:, m, hc * P:(hc + 1) * P], YB[:, kv, m],
                                      start=m == 0, stop=m == 15)
                    end(last)
                elif kind == "c2k":
                    evacuated(pe, "h1", 0)
                    w2 = param("w2").rearrange("p (k c n) -> p k c n", k=2, c=2)
                    for hc in range(2):
                        last = mm(b[0:32, 0:DH], HK[:, hc], w2[:, 0, hc], start=hc == 0, stop=hc == 1)
                    end(last)
                elif kind == "c2v":
                    evacuated(pe, "h1", 1)
                    w2 = param("w2").rearrange("p (k c n) -> p k c n", k=2, c=2)
                    for hc in range(2):
                        last = mm(b[:, 0:DH], HV[:, hc].rearrange("p g m n -> p (g m n)"), w2[:, 1, hc], start=hc == 0, stop=hc == 1)
                    end(last)
                elif kind == "kct":
                    pe.wait_ge(s["kcr_ready"], 1)
                    end(nc.tensor.transpose(b[:, 0:32], KC2[0:32, :], IDENT[0:32, 0:32]))
                elif kind == "sc":
                    evacuated(pe, "kct")
                    evacuated(pe, "qt", T)
                    for p in range(4):
                        last = mm(b[:, p * 32:p * 32 + 32], QT[:, p, T * P:(T + 1) * P], KCBD[:, p // 2], start=True, stop=True)
                    end(last)
                elif kind == "pct":
                    pe.wait_ge(s["pc_ready"], T + 1)
                    transposes(job, b, [PC[T]])
                elif kind == "oc":
                    evacuated(pe, "pct", T)
                    evacuated(pe, "c2v")
                    end(mm(b[:, :], PCT[:, T * P:(T + 1) * P], VBD, start=True, stop=True))
                elif kind == "s":
                    t, br, h0, nh = UNITS[a[0]]
                    evacuated(pe, "qt", t)
                    for t_ in range(t + 1):
                        evacuated(pe, "kt", t_)
                    nk = (t + 1) * P
                    for i in range(nh // 2):
                        last = mm(b[:, i * 2 * nk:(i + 1) * 2 * nk], QT[:, h0 // 2 + i, t * P:(t + 1) * P],
                                  KZ[:, br, h0 // 4, :, 0:nk], start=True, stop=True)
                    end(last)
                elif kind == "pt":
                    pe.wait_ge(s["p_ready"], a[0] + 1)
                    transposes(job, b, [SM[a[0] % 2][:, i * P:(i + 1) * P] for i in range(4)])
                elif kind == "o":
                    u = a[0]
                    t, br, h0, nh = UNITS[u]
                    evacuated(pe, "pt", u)
                    nb = t + 1
                    for i in range(nh):
                        for kb in range(nb):
                            last = mm(b[:, i * DH:(i + 1) * DH], PT[u % 3][:, i * nb + kb],
                                      VSW[:, kb, 2 * br + (h0 + i) // 4], start=kb == 0, stop=kb == nb - 1)
                    end(last)
                elif kind == "ot":
                    t, hf = a
                    if hf == 0:
                        pe.wait_ge(s["oc_nsa"], len(UNITS))
                    else:
                        pe.wait_ge(s["oc_gdn"], t + 1)
                    transposes(job, b, [OC[:, t, (4 * hf + i) * P:(4 * hf + i + 1) * P] for i in range(4)])
                elif kind == "y":
                    t, hf = a
                    w = weights(9 + hf).rearrange("p (c n) -> p c n", c=DC)
                    for i in range(2):
                        evacuated(pe, "ot", t, i)
                    rows(job, b, OT[:, :, t * P:(t + 1) * P], w, 0, 512)
                elif kind == "xt":
                    pe.wait_ge(s["xn_ready"], NT)
                    transposes(job, b, [XNORM[:, t, (2 * a[0] + i) * P:(2 * a[0] + i + 1) * P]
                                        for i in range(2) for t in range(NT)])
                elif kind == "q":
                    w = weights(11 + a[0] // 2).rearrange("p (c n) -> p c n", c=DC)
                    for i in range(4):
                        evacuated(pe, "xt", i)
                    for i in range(2):
                        o = (2 * a[0] + i) % 4 * P
                        for c in range(DC):
                            last = mm(b[:, i * S:(i + 1) * S], w[:, c, o:o + P], H2T[:, c * S:(c + 1) * S],
                                      start=c == 0, stop=c == DC - 1)
                    end(last)
                elif kind == "sk":
                    t, k = a
                    pe.wait_ge(subk_in, 32)
                    for i in range(2):
                        evacuated(pe, "q", 2 * k + i)
                    for i in range(4):
                        last = mm(b[:, i * P:(i + 1) * P], QRY[:, 4 * k + i, t * P:(t + 1) * P], SUBK[:, i % 2],
                                  start=True, stop=True)
                    end(last)

            for job in JOBS:
                run(job)

            def gates(ph, m, k):
                g = m + Q * (ph - 1)
                pe.wait_ge(onehot_ready, 4 * g + k + 1)
                for idx in range(4 * k, 4 * k + 4):
                    if idx % 8 == 0:
                        wait(pe, gated, 2 * g - 1 + idx // 8)
                    q = idx % OH_TOKENS
                    for c in range(PARTS):
                        last = mm(PS[:, G_BANK + idx // 8, idx % 8 * 64:idx % 8 * 64 + 64], ONEHOT2[:, q], ONEHOT1[:, q, c],
                                  start=c == 0, stop=c == PARTS - 1)
                last.then_inc(gate_mm, 1)

            def step(ph, m):
                for k in range(RSLOTS):
                    b = 4 * m + 4 * Q * ph + k
                    if ph in (1, 2):
                        gates(ph, m, k)
                    pe.wait_ge(tab_lo_dve, b + 1)
                    pe.wait_ge(tab_lo_pool, b + 1)
                    hi, lo = (t[:, k % 2 * D:(k % 2 + 1) * D] for t in (TABH, TABL))
                    if ph < 2:
                        wait(pe, gelu_done, b - 1)
                        out = PS[:, A_BANK + k % 2, 0:S]
                        terms = [(hi, H2H), (hi, H2L), (lo, H2H)]
                        for n, (u, h) in enumerate(terms):
                            for c in range(DC):
                                last = mm(out, u[:, c * P:(c + 1) * P], h[:, c * S:(c + 1) * S],
                                          start=n == 0 and c == 0, stop=n == 2 and c == DC - 1)
                    else:
                        if ph == 2:
                            pe.wait_ge(coef_lo_pool, b - NBLK + 1)
                        else:
                            pe.wait_ge(coef_lo_dve, b - NBLK - NBLK // 2 + 1)
                        first = ph == 2 and isinstance(m, int) and m == 0 and k == 0
                        final = ph == 3 and isinstance(m, int) and m == Q - 1 and k == RSLOTS - 1
                        for t in range(NT):
                            chi, clo = (x[:, k % 2 * S + t * P:k % 2 * S + (t + 1) * P] for x in (CFH, CFL))
                            for n, (cf, tab) in enumerate(((chi, hi), (chi, lo), (clo, hi))):
                                for hf in range(2):
                                    last = mm(PS[:, 2 * t + hf, :], cf, tab[:, hf * 512:(hf + 1) * 512],
                                              start=first and n == 0, stop=final and n == 2)
                    last.then_inc(blocks_done, 1)

            def finish(ph):
                if ph == 0:
                    pe.wait_ge(route_ready, 1)
                    for c in range(3):
                        for t in range(NT):
                            i = c * NT + t
                            last = nc.tensor.transpose(PS[:, G_BANK + i // 4, i % 4 * P:(i % 4 + 1) * P],
                                                       ROUTE[:, i * P:(i + 1) * P], IDENT)
                    last.then_inc(route_t_in, 1)

            pe.wait_ge(h2l_ready, 4)
            phases(pe, step, finish)

        @block.scalar
        def _(act):
            A = nc.scalar.activation

            def run(job):
                kind, *a = job
                T = a[-1] if a else 0
                b = bank(*job)
                if kind == "ssq":
                    act.wait_ge(xt_in, 16)
                    for i in range(2):
                        A(CV[:, 4 * i:4 * i + 4], XT[:, 4 * i:4 * i + 4], ACT.Square).then_inc(s["xsq_ready"], 1)
                    act.wait_ge(s["ones_ready"], 2)
                    full(act, *job)
                    release(A(TMP[:, 0:S], b[:, 0:S], ACT.Sqrt, bias=EPSC, scale=1.0 / D), *job)
                elif kind == "qkv":
                    full(act, *job)
                    act.wait_ge(s["qp_zero"], 1)
                    release(A(QP[:, 2 * a[0]:2 * a[0] + 2, CONV_K - 1:CONV_K - 1 + S],
                              b.rearrange("p (b t) -> p b t", b=2), ACT.Copy), *job)
                    if a[0] == 1:
                        act.wait_ge(s["softplus_in"], 1)
                        A(SG, GAB[:, :, 0:28], ACT.Exp, scale=-1.0).then_inc(s["exp_misc_done"], 1)
                        A(aexp, param("alog"), ACT.Exp).then_inc(s["exp_misc_done"], 1)
                        A(sp1, sp1, ACT.Exp, scale=-1.0).then_inc(s["softplus_exp"], 1)
                        act.wait_ge(s["softplus_exp"], 1)
                        A(sp1, sp1, ACT.Ln, bias=1.0).then_inc(s["softplus_ln"], 1)
                elif kind == "l2":
                    i = a[0]
                    if i == 0:
                        for n in range(6):
                            act.wait_ge(s["conv_ready"], n + 1)
                            A(CV[:, 2 * n:2 * n + 2], CV[:, 2 * n:2 * n + 2], ACT.Silu).then_inc(s["silu_done"], 1)
                            if n < 4:
                                act.wait_ge(s["silu_done"], n + 1)
                                if n == 0:
                                    act.wait_ge(s["hT_ready"], 1)
                                A(SQ[:, 2 * n:2 * n + 2], CV[:, 2 * n:2 * n + 2], ACT.Square).then_inc(s["sq_ready"], 1)
                    full(act, *job)
                    release(A(RN[:, 2 * i:2 * i + 2], b.rearrange("p (b t) -> p b t", b=2), ACT.Sqrt, bias=EPSC), *job)
                elif kind == "gcol":
                    evacuated(act, *job)
                    A(egs, gcs, ACT.Exp).then_inc(s["gcs_exp"], 1)
                elif kind == "gb":
                    full(act, *job)
                    A(EG[:, T], b.rearrange("p (h n) -> p h n", h=GH), ACT.Exp).then_inc(s["eg_exp"], 1)
                    for i, m in enumerate((DL, DU)):
                        act.wait_ge(s["darg_ready"], 2 * T + i + 1)
                        A(m[:, T], m[:, T], ACT.Exp).then_inc(s["dexp_done"], 1)
                elif kind == "zp":
                    full(act, *job)
                    release(A(Z[:, T], b, ACT.Silu), *job)
                elif kind in ("at", "w", "u", "wt", "qt", "kvct", "pct", "pt"):
                    full(act, *job)
                    dst = {"at": lambda: AT_[:, T], "w": lambda: WW[:, T], "u": lambda: U[:, T], "wt": lambda: WT[:, T],
                           "qt": lambda: QT[:, :, T * P:(T + 1) * P], "kvct": lambda: X2[:, :, T * P:(T + 1) * P],
                           "pct": lambda: PCT[:, T * P:(T + 1) * P], "pt": lambda: PT[a[0] % 3]}[kind]()
                    if kind == "kvct":
                        full(act, "l2", 3)
                    if kind == "w" and a[0] == 1:
                        act.wait_ge(s["ti_init"], T + 1)
                    if kind == "pt" and a[0] >= 3:
                        full(act, "o", a[0] - 3)
                    src = b[:, 0:P] if kind == "pct" else b
                    if kind != "pct":
                        src = src.rearrange("p (h n) -> p h n", h=4)
                    release(A(dst, src, ACT.Copy), *job)
                elif kind == "o1":
                    c = a[0]
                    r = slice(64 * (c % 2), 64 * (c % 2) + 64)
                    full(act, *job)
                    release(A(OG[r, c // 2], b[r, :].rearrange("p (h n) -> p h n", h=GH), ACT.Copy), *job)
                elif kind == "h1":
                    full(act, *job)
                    src = b[:, 0:64].rearrange("p (c n) -> p c n", c=2)
                    if a[0] == 0:
                        ins = A(HK, src, ACT.Gelu_apprx_tanh)
                    else:
                        for c in range(2):
                            ins = A(HV[:, c], src[:, c].rearrange("p (g n) -> p g n", g=2).unsqueeze(2)
                                    .to_broadcast([P, 2, 4, NC16]), ACT.Gelu_apprx_tanh)
                    release(ins, *job)
                elif kind == "s":
                    u = a[0]
                    t, br, h0, nh = UNITS[u]
                    nk = (t + 1) * P
                    act.wait_ge(s["sm_ready"], u + 1)
                    for i in range(nh):
                        v = SM[u % 2][:, i * nk:(i + 1) * nk]
                        last = A(v, v, ACT.Exp, bias=nm[u % 2][:, i:i + 1], scale=DH ** -0.5, accum_out=rs[:, u, i:i + 1])
                    last.then_inc(s["p_ready"], 1)
                elif kind == "sc":
                    act.wait_ge(s["scm_ready"], T + 1)
                    A(PC[T], PC[T], ACT.Exp, scale=DH ** -0.5).then_inc(s["pc_ready"], 1)
                elif kind == "ot":
                    full(act, *job)
                    t, hf = a
                    release(A(OT[:, 4 * hf:4 * hf + 4, t * P:(t + 1) * P], b.rearrange("p (c n) -> p c n", c=4), ACT.Copy),
                            *job)
                elif kind == "xt":
                    evacuated(act, *job)
                    cols = slice(2 * a[0] * S, (2 * a[0] + 2) * S)
                    A(H2H[:, cols], H2T[:, cols], ACT.Copy).then_inc(h2h_ready, 1)
                elif kind == "q":
                    full(act, *job)
                    release(A(QRY[:, 2 * a[0]:2 * a[0] + 2], b.rearrange("p (b t) -> p b t", b=2), ACT.Copy), *job)
                elif kind == "sk":
                    full(act, *job)
                    t, k = a
                    o = t * 16 * NKEYS + k * 512
                    release(A(SCORES[:, o:o + 512], b, ACT.Copy), *job)

            for job in JOBS:
                run(job)

            def gelu(b, k):
                act.wait_ge(blocks_done, b + 1)
                A(view(GATED, b * S, (1, S)), PS[:, A_BANK + k % 2, 0:S], ACT.Gelu_apprx_tanh).then_inc(gelu_done, 1)

            def coef_round(ph, b, k):
                if k == 0:
                    act.wait_ge(gated, 2 * Q * (ph - 1))
                A(CFH[:, k % 2 * S:(k % 2 + 1) * S], view(GATED, (b - NBLK) * S, (1, S)), ACT.Copy).then_inc(coef_hi, 1)

            def step(ph, m):
                for k in range(RSLOTS):
                    b = 4 * m + 4 * Q * ph + k
                    act.wait_ge(table_in[k], 16 * (m + Q * ph + 1))
                    wait(act, blocks_done, b - 1)
                    if ph == 2:
                        if isinstance(b, int) and b == NBLK:
                            gelu(b - 2, 0)
                            gelu(b - 1, 1)
                        coef_round(ph, b, k)
                    for lo, hi in ((SPLIT[ph], D), (0, SPLIT[ph])):
                        A(TABH[:, k % 2 * D + lo:k % 2 * D + hi], RING[:, k * D + lo:k * D + hi], ACT.Copy)\
                            .then_inc(tab_hi, 1)
                    if ph == 3:
                        coef_round(ph, b, k)
                    if ph < 2 and not (isinstance(b, int) and b < 2):
                        gelu(b - 2, k)

            def finish(ph):
                if ph == 0:
                    act.wait_ge(route_exp_in, 1)
                    A(ROUTE[:, 2 * S:3 * S], ROUTE[:, 2 * S:3 * S], ACT.Exp).then_inc(route_exp, 1)

            phases(act, step, finish)

        @block.vector
        def _(dve):
            v = nc.vector
            count = [0]

            def link(ins):
                count[0] += 1
                ins.then_inc(dve_link, 1)
                dve.wait_ge(dve_link, count[0])

            def bc(a, axis, shape):
                return a.unsqueeze(axis).to_broadcast(shape)

            def heads(b, h):
                return b.rearrange("p (h n) -> p h n", h=h)

            def run(job):
                kind, *a = job
                T = a[-1] if a else 0
                b = bank(*job)
                if kind == "ssq":
                    v.memset(ONES[:, :], 1.0).then_inc(s["ones_ready"], 1)
                    v.memset(EPSC, EPS).then_inc(s["ones_ready"], 1)
                    evacuated(dve, *job)
                    link(v.reciprocal(TMP[:, 0:S], TMP[:, 0:S]))
                    dve.wait_ge(consts_in, 48)
                    for c in range(DC):
                        last = v.scalar_tensor_tensor(HT[:, c], XT[:, c], param("attng")[:, c:c + 1], TMP[:, 0:S],
                                                      ALU.mult, ALU.mult)
                    last.then_inc(s["hT_ready"], 1)
                elif kind == "misc":
                    full(dve, *job)
                    v.tensor_copy(VSW[:, T], b[:, 0:256].rearrange("p (h d) -> p h d", d=DH))
                    release(v.tensor_copy(GAB[:, T], b[:, 256:288]), *job)
                    if T == 1:
                        evacuated(dve, *job)
                        link(v.tensor_tensor(sp2, GAB[:, :, 28:32], bc(param("dtb"), 1, [P, NT, GH]), ALU.add))
                        link(v.tensor_scalar(sp1, sp2, -1.0, None, ALU.mult))
                        v.tensor_tensor(sp1, sp1, sp2, ALU.max).then_inc(s["softplus_in"], 1)
                        link(v.tensor_scalar(sp2, sp2, 0.0, None, ALU.max))
                        dve.wait_ge(s["softplus_ln"], 1)
                        dve.wait_ge(s["exp_misc_done"], 2)
                        link(v.tensor_tensor(sp2, sp2, sp1, ALU.add))
                        link(v.tensor_scalar(aexp, aexp, -1.0, None, ALU.mult))
                        v.tensor_tensor(gstep, sp2, bc(aexp, 1, [P, NT, GH]), ALU.mult).then_inc(s["g_ready"], 1)
                        link(v.tensor_scalar(SG, SG, 1.0, None, ALU.add))
                        v.reciprocal(SG, SG).then_inc(s["sig_ready"], 1)
                elif kind == "qkv":
                    evacuated(dve, *job)
                    w = param("conv").rearrange("p (b j) -> p b j", b=12)
                    for j in range(CONV_K):
                        for i in (2 * a[0], 2 * a[0] + 1):
                            src = QP[:, i, j:j + S]
                            if j == 0:
                                ins = v.tensor_scalar(CV[:, i], src, w[:, i, 0:1], None, ALU.mult)
                            else:
                                ins = v.scalar_tensor_tensor(CV[:, i], src, w[:, i, j:j + 1], CV[:, i], ALU.mult, ALU.add)
                        if j < CONV_K - 1:
                            link(ins)
                    ins.then_inc(s["conv_ready"], 1)
                elif kind == "gcol":
                    full(dve, *job)
                    release(v.tensor_copy(gcs, b[:, 0:16].rearrange("p (t n) -> p t n", t=NT)), *job)
                    dve.wait_ge(s["gcs_exp"], 1)
                    dve.wait_ge(s["sig_ready"], 1)
                    v.tensor_tensor(bg, egs[:, :, 0:4], SG[:, :, 24:28], ALU.mult)
                elif kind == "gb":
                    dve.wait_ge(s["eg_exp"], T + 1)
                    release(v.tensor_tensor(TMP2.rearrange("p (h n) -> p h n", h=GH), heads(b, GH),
                                            bc(gcs[:, T, 0:4], 2, [P, GH, P]), ALU.subtract), *job)
                    evacuated(dve, *job)
                    src = TMP2.rearrange("p (h n) -> p h n", h=GH)
                    v.tensor_tensor(DL[:, T], src, bc(const("nlower"), 1, [P, GH, P]), ALU.mult).then_inc(s["darg_ready"], 1)
                    v.tensor_tensor(DU[:, T], src, bc(const("upper"), 1, [P, GH, P]), ALU.mult).then_inc(s["darg_ready"], 1)
                    for f in range(2):
                        v.tensor_copy(gls[:, T, f], EG[:, T, :, 64 * f + 63]).then_inc(s["gls_ready"], 1)
                elif kind == "l2":
                    i = a[0]
                    evacuated(dve, *job)
                    link(v.reciprocal(RN[:, 2 * i:2 * i + 2], RN[:, 2 * i:2 * i + 2]))
                    dve.wait_ge(s["silu_done"], i + 1)
                    dve.wait_ge(s["sq_ready"], i + 1)
                    for k in range(2):
                        n = 2 * i + k
                        v.scalar_tensor_tensor(CV[:, n], CV[:, n], GD ** -0.5 if n < 4 else 1.0, RN[:, n],
                                               ALU.mult, ALU.mult).then_inc(s["kqT_ready"], 1)
                elif kind == "qp":
                    full(dve, *job)
                    release(v.tensor_copy(XN[:, T, 0:8], b.rearrange("p (h d) -> p h d", d=DH)), *job)
                elif kind == "kvp":
                    full(dve, *job)
                    v.tensor_copy(XN[:, T, 8:12], b[:, 0:256].rearrange("p (h d) -> p h d", d=DH))
                    release(v.tensor_copy(KCV[:, T], bc(b[:, 256:512].rearrange("p (h d) -> p h d", d=DH), 2, [P, 4, 2, DH])),
                            *job)
                    evacuated(dve, *job)
                    sq = TMP[:, 0:768].rearrange("p (h d) -> p h d", d=DH)
                    link(v.tensor_tensor(sq, XN[:, T], XN[:, T], ALU.mult))
                    link(v.tensor_reduce(rs12[:, T], sq, AX.X, ALU.add))
                    v.tensor_scalar(rs12[:, T], rs12[:, T], 1.0 / DH, EPS, ALU.mult, ALU.add).then_inc(s["xq_mean"], 1)
                    dve.wait_ge(s["xq_rstd"], T + 1)
                    link(v.tensor_tensor(XN[:, T], XN[:, T], bc(rs12[:, T], 2, [P, 12, DH]), ALU.mult))
                    link(v.tensor_tensor(XN[:, T], XN[:, T], param("gains").rearrange("p (h d) -> p h d", d=DH), ALU.mult))
                    cos = const("cos").rearrange("p (t d) -> p t d", t=NT)[:, T]
                    sin = const("sin").rearrange("p (t d) -> p t d", t=NT)[:, T]
                    hd = DH // 2
                    v.tensor_tensor(XR[:, T], XN[:, T, 0:8], bc(cos, 1, [P, 8, DH]), ALU.mult)
                    kr = TMP2[:, 0:4 * DH].rearrange("p (h d) -> p h d", d=DH)
                    v.tensor_tensor(kr, XN[:, T, 8:12], bc(cos, 1, [P, 4, DH]), ALU.mult)
                    v.tensor_tensor(sq[:, :, 0:hd], XN[:, T, :, hd:DH], bc(sin[:, 0:hd], 1, [P, 12, hd]), ALU.mult)
                    link(v.tensor_tensor(sq[:, :, hd:DH], XN[:, T, :, 0:hd], bc(sin[:, hd:DH], 1, [P, 12, hd]), ALU.mult))
                    v.tensor_tensor(XR[:, T], XR[:, T], sq[:, 0:8], ALU.add).then_inc(s["xr_ready"], 1)
                    v.tensor_tensor(KR[:, T], bc(kr, 2, [P, 4, 2, DH]), bc(sq[:, 8:12], 2, [P, 4, 2, DH]), ALU.add)\
                        .then_inc(s["xr_ready"], 1)
                elif kind == "kk":
                    full(dve, *job)
                    dve.wait_ge(s["dmask_done"], 2 * T + 1)
                    for h in range(GH):
                        ins = v.scalar_tensor_tensor(AM[:, T, h], b[:, h * P:(h + 1) * P], SG[:, T, 24 + h:25 + h],
                                                     DL[:, T, h], ALU.mult, ALU.mult)
                    release(ins, *job)
                    evacuated(dve, *job)
                    link(v.tensor_tensor(TI[:, T], AM[:, T], bc(const("nm0"), 1, [P, GH, P]), ALU.mult))
                    v.tensor_tensor(TI[:, T], TI[:, T], bc(IDENT, 1, [P, GH, P]), ALU.add).then_inc(s["ti_init"], 1)
                elif kind == "kq":
                    full(dve, *job)
                    dve.wait_ge(s["dmask_done"], 2 * T + 2)
                    release(v.tensor_tensor(DU[:, T], heads(b, GH), DU[:, T], ALU.mult), *job)
                elif kind == "at":
                    evacuated(dve, *job)
                    link(v.tensor_tensor(TT[:, T], AT_[:, T], bc(const("nm0t"), 1, [P, GH, P]), ALU.mult))
                    v.tensor_tensor(TT[:, T], TT[:, T], bc(IDENT, 1, [P, GH, P]), ALU.add).then_inc(s["tt_init"], 1)
                elif kind == "ktok":
                    full(dve, *job)
                    v.tensor_tensor(KBG[:, T], heads(b, GH), bc(bg[:, T], 2, [P, GH, P]), ALU.mult)
                    release(v.tensor_tensor(KD[:, T], heads(b, GH), bc(egs[:, T, 4:8], 2, [P, GH, P]), ALU.mult), *job)
                elif kind == "vtok":
                    full(dve, *job)
                    release(v.tensor_tensor(VB[:, T], heads(b, GH), bc(SG[:, T, 24:28], 2, [P, GH, P]), ALU.mult), *job)
                elif kind == "kt":
                    full(dve, *job)
                    dve.wait_ge(s["qd_ready"], NT)
                    pmv = const("pm")
                    for br in range(2):
                        o = KZ[:, br, :, :, T * P:(T + 1) * P]
                        i0 = bc(b[:, br * 256:br * 256 + 256].rearrange("p (g t) -> p g t", g=2), 2, [P, 2, 2, P])
                        ins = v.tensor_tensor(o, i0, pmv.unsqueeze(1).unsqueeze(3).to_broadcast([P, 2, 2, P]), ALU.mult)
                    release(ins, *job)
                    if T == 1:
                        for t in range(NT):
                            evacuated(dve, "kvct", t)
                        link(v.memset(YB[:, :, :, :, NCMP:NC16], 0.0))
                        pos = param("pos").rearrange("p (k m) -> p k m", k=2)
                        for kv in range(2):
                            for g in range(GROUPS):
                                for r in range(2):
                                    pr = slice(64 * r, 64 * r + 64)
                                    base = X2[pr, 2 * kv + g, r:r + 1]
                                    src = bass.AP(base.tensor, base.offset,
                                                  [list(base.ap[0]), [2, 16], [CMP_STRIDE, NCMP]])
                                    last = v.tensor_tensor(YB[pr, kv, :, g, 0:NCMP], src,
                                                           bc(pos[pr, kv], 2, [64, 16, NCMP]), ALU.add)
                            last.then_inc(s["y_ready"], 1)
                elif kind in ("pa", "pb"):
                    m = TI if kind == "pa" else TT
                    full(dve, *job)
                    release(v.tensor_tensor(m[:, T], m[:, T], heads(b, GH), ALU.subtract), *job)
                elif kind == "u":
                    if T == 0:
                        for t in range(NT):
                            evacuated(dve, "pb", LEVELS - 1, t)
                        v.memset(OG[0:64, 0], 0.0).then_inc(s["og_zero"], 1)
                elif kind == "kv":
                    c = a[0]
                    full(dve, *job)
                    for h in range(GH):
                        if c == 0:
                            ins = v.tensor_copy(STATE[:, h], b[:, h * P:(h + 1) * P])
                        else:
                            ins = v.scalar_tensor_tensor(STATE[:, h], STATE[:, h], gls[:, c // 2, c % 2, h:h + 1],
                                                         b[:, h * P:(h + 1) * P], ALU.mult, ALU.add)
                    release(ins, *job)
                elif kind == "vn":
                    c = a[0]
                    r = slice(64 * (c % 2), 64 * (c % 2) + 64)
                    full(dve, *job)
                    evacuated(dve, "u", c // 2)
                    release(v.tensor_tensor(U[r, c // 2], U[r, c // 2], heads(b[r, :], GH), ALU.subtract), *job)
                elif kind == "o2":
                    full(dve, *job)
                    evacuated(dve, "o1", 2 * T + 1)
                    if T == 1:
                        evacuated(dve, "o1", 2)
                    release(v.tensor_tensor(OG[:, T], OG[:, T], heads(b, GH), ALU.add), *job)
                    evacuated(dve, *job)
                    sq = TMP[:, 512:1024].rearrange("p (h n) -> p h n", h=GH)
                    link(v.tensor_tensor(sq, OG[:, T], OG[:, T], ALU.mult))
                    link(v.tensor_reduce(gr[:, T], sq, AX.X, ALU.add))
                    v.tensor_scalar(gr[:, T], gr[:, T], 1.0 / GD, EPS, ALU.mult, ALU.add).then_inc(s["og_mean"], 1)
                    dve.wait_ge(s["og_rstd"], T + 1)
                    link(v.tensor_tensor(sq, OG[:, T], bc(gr[:, T], 2, [P, GH, GD]), ALU.mult))
                    link(v.tensor_tensor(sq, sq, bc(param("outg"), 1, [P, GH, GD]), ALU.mult))
                    v.tensor_tensor(OC[:, T, 512:1024].rearrange("p (h n) -> p h n", h=GH), sq, heads(Z[:, T], GH), ALU.mult)\
                        .then_inc(s["oc_gdn"], 1)
                elif kind == "c2k":
                    k = KC[0:32, :]
                    full(dve, *job)
                    release(v.tensor_copy(k, b[0:32, 0:DH]), *job)
                    evacuated(dve, *job)
                    k2 = KC3[0:32, :]
                    link(v.tensor_tensor(k2, k, k, ALU.mult))
                    link(v.tensor_reduce(kcs[0:32, :], k2, AX.X, ALU.add))
                    v.tensor_scalar(kcs[0:32, :], kcs[0:32, :], 1.0 / DH, EPS, ALU.mult, ALU.add).then_inc(s["kc_mean"], 1)
                    dve.wait_ge(s["kc_rstd"], 1)
                    link(v.scalar_tensor_tensor(k, k, kcs[0:32, :], param("kg0")[0:32, :], ALU.mult, ALU.mult))
                    hd = DH // 2
                    sin = const("sinc")[0:32, :]
                    q = TMP2[0:32, 0:DH]
                    v.tensor_tensor(k2, k, const("cosc")[0:32, :], ALU.mult)
                    v.tensor_tensor(q[:, 0:hd], k[:, hd:DH], sin[:, 0:hd], ALU.mult)
                    link(v.tensor_tensor(q[:, hd:DH], k[:, 0:hd], sin[:, hd:DH], ALU.mult))
                    v.tensor_tensor(KC2[0:32, :].rearrange("p (r d) -> p r d", r=2), bc(k2, 1, [32, 2, DH]),
                                    bc(q, 1, [32, 2, DH]), ALU.add).then_inc(s["kcr_ready"], 1)
                elif kind == "kct":
                    full(dve, *job)
                    i0 = bc(b[:, 0:32].rearrange("p (g n) -> p g n", g=2), 2, [P, 2, 2, NC16])
                    release(v.tensor_tensor(KCBD, i0, const("pm").unsqueeze(1).unsqueeze(3).to_broadcast([P, 2, 2, NC16]),
                                            ALU.mult), *job)
                    evacuated(dve, *job)
                elif kind == "c2v":
                    full(dve, *job)
                    release(v.tensor_tensor(VBD, bc(b[:, 0:DH], 1, [P, HEADS, DH]), bc(const("hm"), 2, [P, HEADS, DH]),
                                            ALU.mult), *job)
                    evacuated(dve, *job)
                elif kind == "sc":
                    pc = PC[T].rearrange("p (h n) -> p h n", h=HEADS)
                    cneg = const("cneg").rearrange("p (t n) -> p t n", t=NT)[:, T]
                    full(dve, *job)
                    release(v.tensor_tensor(pc, b[:, 0:P].rearrange("p (h n) -> p h n", h=HEADS),
                                            bc(cneg, 1, [P, HEADS, NC16]), ALU.add), *job)
                    evacuated(dve, *job)
                    link(v.tensor_reduce(mx, pc, AX.X, ALU.max))
                    v.tensor_tensor(pc, pc, bc(mx, 2, [P, HEADS, NC16]), ALU.subtract).then_inc(s["scm_ready"], 1)
                    dve.wait_ge(s["pc_ready"], T + 1)
                    link(v.tensor_reduce(cs[T], pc, AX.X, ALU.add))
                    link(v.reciprocal(cs[T], cs[T]))
                    gate = SG[:, T, 0:24].rearrange("p (h b) -> p h b", b=3)[:, :, 0]
                    link(v.scalar_tensor_tensor(rc[T], cs[T], const("any")[:, T:T + 1], gate, ALU.mult, ALU.mult))
                elif kind == "oc":
                    full(dve, *job)
                    dve.wait_ge(s["xr_ready"], 4)
                    for t in range(NT):
                        evacuated(dve, "qt", t)
                        full(dve, "kt", t)
                        full(dve, "kvct", t)
                    release(v.tensor_tensor(OC[:, T, 0:512].rearrange("p (h d) -> p h d", d=DH),
                                            b.rearrange("p (h d) -> p h d", d=DH), bc(rc[T], 2, [P, HEADS, DH]), ALU.mult),
                            *job)
                elif kind == "s":
                    u = a[0]
                    t, br, h0, nh = UNITS[u]
                    nk = (t + 1) * P
                    full(dve, *job)
                    if u >= 2:
                        full(dve, "pt", u - 2)
                    sm = SM[u % 2].rearrange("p (h k) -> p h k", h=nh)
                    neg = const("negc").rearrange("p (t k) -> p t k", t=NT)[:, t, 0:nk]
                    release(v.tensor_tensor(sm, b.rearrange("p (h k) -> p h k", h=nh), bc(neg, 1, [P, nh, nk]), ALU.add), *job)
                    evacuated(dve, *job)
                    link(v.tensor_reduce(mx[:, 0:nh], sm, AX.X, ALU.max))
                    v.tensor_scalar(nm[u % 2][:, 0:nh], mx[:, 0:nh], -DH ** -0.5, None, ALU.mult).then_inc(s["sm_ready"], 1)
                elif kind == "o":
                    u = a[0]
                    t, br, h0, nh = UNITS[u]
                    dve.wait_ge(s["p_ready"], u + 1)
                    link(v.reciprocal(rr[:, u, 0:nh], rs[:, u, 0:nh]))
                    gate = SG[:, t, 0:24].rearrange("p (h b) -> p h b", b=3)[:, h0:h0 + nh, 1 + br]
                    link(v.tensor_tensor(rr[:, u, 0:nh], rr[:, u, 0:nh], gate, ALU.mult))
                    full(dve, *job)
                    tmp = TMP[:, 0:nh * DH].rearrange("p (h d) -> p h d", d=DH)
                    release(v.tensor_tensor(tmp, b[:, 0:nh * DH].rearrange("p (h d) -> p h d", d=DH),
                                            bc(rr[:, u, 0:nh], 2, [P, nh, DH]), ALU.mult), *job)
                    evacuated(dve, *job)
                    o = OC[:, t, h0 * DH:(h0 + nh) * DH]
                    v.tensor_tensor(o, o, TMP[:, 0:nh * DH], ALU.add).then_inc(s["oc_nsa"], 1)
                elif kind == "y":
                    t, hf = a
                    full(dve, *job)
                    dve.wait_ge(x_in, 16)
                    xv = X[:, t, hf * 512:(hf + 1) * 512]
                    release(v.tensor_tensor(xv, xv, b, ALU.add), *job)
                    evacuated(dve, *job)
                    if hf == 1:
                        link(v.tensor_tensor(XNORM[:, t], X[:, t], X[:, t], ALU.mult))
                        link(v.tensor_reduce(xs[:, t:t + 1], XNORM[:, t], AX.X, ALU.add))
                        v.tensor_scalar(xs[:, t:t + 1], xs[:, t:t + 1], 1.0 / D, EPS, ALU.mult, ALU.add)\
                            .then_inc(s["x1_mean"], 1)
                        dve.wait_ge(s["x1_rstd"], t + 1)
                        v.tensor_scalar(XNORM[:, t], X[:, t], xs[:, t:t + 1], None, ALU.mult).then_inc(s["xn_ready"], 1)
                elif kind == "xt":
                    full(dve, *job)
                    dve.wait_ge(subk_in, 32)
                    for i in range(2):
                        c = 2 * a[0] + i
                        ins = v.tensor_scalar(H2T[:, c * S:(c + 1) * S], b[:, i * S:(i + 1) * S], FFNG[:, c:c + 1], None,
                                              ALU.mult)
                    release(ins, *job)
                    cols = slice(2 * a[0] * S, (2 * a[0] + 2) * S)
                    dve.wait_ge(h2h_ready, a[0] + 1)
                    v.tensor_tensor(H2L[:, cols], H2T[:, cols], H2H[:, cols].bitcast(F32), ALU.subtract)\
                        .then_inc(h2l_ready, 1)

            for job in JOBS:
                run(job)

            marked, carried = [0], [0]

            def topk(m, k):

                def mark(ins):
                    marked[0] += 1
                    ins.then_inc(topk_link, 1)

                def carry():
                    v.memset(CARRIER[:, carried[0] % 4:carried[0] % 4 + 1], 0.0)
                    carried[0] += 1

                def hold(by_carry=True):
                    dve.wait_ge(topk_link, TOPK_LINKS * m + marked[0])
                    if by_carry:
                        carry()

                first = isinstance(m, int) and m == 0
                if k == 0:
                    marked[0] = 0
                    mark(v.tensor_copy(KS, view(GATED, TOPT + 16 * S + m * 2 * NKEYS, (NKEYS, 2), (1, NKEYS))))
                    hold()
                    for f in range(2):
                        ins = v.max(KV_[:, f, 0:8], KS[:, f])
                    mark(ins)
                    hold()
                    for f in range(2):
                        v.max_index(KI[:, f, 0:8], KV_[:, f, 0:8], KS[:, f])
                    for f in range(2):
                        ins = v.match_replace(KS[:, f], KV_[:, f, 0:8], KS[:, f], LOWEST)
                    mark(ins)
                elif k == 1:
                    hold()
                    for f in range(2):
                        ins = v.max(KV_[:, f, 8:16], KS[:, f])
                    ins.then_inc(keys_ready, 1)
                    if not first:
                        compare()
                    dve.wait_ge(keys_ready, m + 1)
                    carry()
                    for f in range(2):
                        ins = v.max_index(KI[:, f, 8:16], KV_[:, f, 8:16], KS[:, f])
                    mark(ins)
                elif k == 2:
                    dve.wait_ge(cand_ready, m + 1)
                    carry()
                    mark(v.max(RES[:, 0:8], CAND))
                    hold()
                    v.max_index(POS[:, 0:8], RES[:, 0:8], CAND)
                    mark(v.match_replace(CAND, RES[:, 0:8], CAND, LOWEST))
                else:
                    hold()
                    mark(v.max(RES[:, 8:16], CAND))
                    if not first:
                        collect(m - 1)
                    hold()
                    mark(v.max_index(POS[:, 8:16], RES[:, 8:16], CAND))
                    v.tensor_copy(KIF, KI)
                    hold(by_carry=False)
                    v.tensor_scalar(POSU[:, 0], POS, 4, None, ALU.logical_shift_right)
                    mark(v.tensor_scalar(POSU[:, 1], POS, TOPK - 1, None, ALU.bitwise_and))
                    v.tensor_copy(view(ROUTE, 2 * S + m * TOPK, (1, TOPK)), RES)
                    hold(by_carry=False)
                    mark(v.tensor_copy(POSF, POSU))
                    assert marked[0] == TOPK_LINKS

            def compare():
                shape = [P, 2 * TOPK, TOPK]
                v.tensor_tensor(EQ.rearrange("p f k a -> p (f k) a"), bc(IOTA[:, 0:TOPK], 1, shape),
                                bc(POSF.rearrange("p f k -> p (f k)"), 2, shape), ALU.is_equal).then_inc(places_ready, 1)

            def collect(m):
                dve.wait_ge(placed, m + 1)
                return v.tensor_reduce(view(ROUTE, m * TOPK, (S, 2), (1, TOPK)), EQ, AX.X, ALU.add)

            def multiply(ph, m, bk):
                g = m + Q * (ph - 1)
                dve.wait_ge(gate_mm, 4 * g + 2 * bk + 2)
                o = view(GATED, (ph - 1) * 64 * S + m * 16 + 8 * bk, (S, 64), (1, 8))
                v.tensor_tensor(o, o, PS[:, G_BANK + bk, :].rearrange("p (t i) -> p i t", i=64), ALU.mult).then_inc(gated, 1)

            def onehots(ph, m, k):
                g = m + Q * (ph - 1)
                lo = (ph - 1) * 64
                wait(dve, onehot_ready, 4 * g + k)
                if k == 0:
                    v.tensor_copy(TOK, view(ROUTE_T, m * 16, (S, 2 + PARTS), (1, 16))).then_inc(tok_ready, 1)
                    dve.wait_ge(tok_ready, g + 1)
                wait(dve, gate_mm, 4 * g + k - 1)
                q, t = 4 * k % OH_TOKENS, slice(4 * k, 4 * k + 4)
                shape = [P, 4, 64]
                v.tensor_tensor(EQ1, bc(IOTA[:, lo:lo + 64], 1, shape), bc(TOK[:, 0, t], 2, shape), ALU.is_equal)\
                    .then_inc(eq1_ready, 1)
                shape = [P, 4, P]
                v.tensor_tensor(ONEHOT2[:, q:q + 4], bc(IOTA, 1, shape), bc(TOK[:, 1, t], 2, shape), ALU.is_equal)
                dve.wait_ge(eq1_ready, 4 * g + k + 1)
                shape = [P, 4, PARTS, 64]
                last = v.tensor_tensor(ONEHOT1[:, q:q + 4], bc(EQ1, 2, shape),
                                       bc(TOK[:, 2:2 + PARTS, t].rearrange("p c q -> p q c"), 3, shape), ALU.mult)
                last.then_inc(onehot_ready, 1)

            def step(ph, m):
                for k in range(RSLOTS):
                    b = 4 * m + 4 * Q * ph + k
                    dve.wait_ge(tab_hi, 2 * b + 2)
                    table_rest(v, k, 0, SPLIT[ph]).then_inc(tab_lo_dve, 1)
                    if ph == 3:
                        dve.wait_ge(coef_hi, b - NBLK + 1)
                        coef_rest(v, b, k).then_inc(coef_lo_dve, 1)
                    if ph == 0:
                        topk(m, k)
                    elif ph < 3:
                        if k == 0 and not (isinstance(m, int) and m == 0):
                            multiply(ph, m - 1, 1)
                        elif k == 2:
                            if isinstance(m, int) and m == 0:
                                dve.wait_ge(gelu_done, NBLK // 2 * ph)
                            multiply(ph, m, 0)
                        if k < 3:
                            onehots(ph, m, k + 1)
                        elif not (isinstance(m, int) and m == Q - 1):
                            onehots(ph, m + 1, 0)
                        elif ph == 1:
                            onehots(2, 0, 0)

            def finish(ph):
                if ph in (1, 2):
                    multiply(ph, Q - 1, 1)
                if ph == 0:
                    dve.wait_ge(topk_link, TOPK_LINKS * Q)
                    compare()
                    link(collect(Q - 1))
                    gv = ROUTE[:, 2 * S:3 * S].rearrange("p (u k) -> p u k", k=TOPK)
                    shape = [P, 2 * PH, TOPK]
                    link(v.tensor_copy(GSUM, gv[:, :, 0]))
                    v.tensor_tensor(gv, gv, bc(GSUM, 2, shape), ALU.subtract).then_inc(route_exp_in, 1)
                    dve.wait_ge(route_exp, 1)
                    link(v.tensor_reduce(GSUM, gv, AX.X, ALU.add))
                    link(v.reciprocal(GSUM, GSUM))
                    v.tensor_tensor(gv, gv, bc(GSUM, 2, shape), ALU.mult).then_inc(route_ready, 1)
                    dve.wait_ge(route_t_in, 1)
                    v.tensor_copy(ROUTE_T[:, 0:2 * S], PS[:, G_BANK, :])
                    link(v.tensor_copy(GREST, PS[:, G_BANK + 1, 0:S]))
                    for c in range(PARTS):
                        part = ROUTE_T[:, (2 + c) * S:(3 + c) * S]
                        link(v.tensor_copy(GPART[:, :], GREST))
                        link(v.tensor_copy(part, GPART[:, :]))
                        if c < PARTS - 1:
                            link(v.tensor_tensor(GREST, GREST, part, ALU.subtract))
                    onehots(1, 0, 0)

            phases(dve, step, finish)
            dve.wait_ge(blocks_done, 2 * NBLK)
            for t in range(NT):
                for hf in range(2):
                    xv = X[:, t, hf * 512:(hf + 1) * 512]
                    v.tensor_tensor(xv, xv, PS[:, 2 * t + hf, :], ALU.add).then_inc(out_ready, 1)

    return


def prepare(inputs):
    i = {k: np.asarray(v) for k, v in inputs.items()}
    x = i["x"][0]
    w_in = i["w_in"][0]
    kv0 = HEADS * DH

    def kvcols(n):
        return w_in[:, kv0 + n * 128:kv0 + (n + 1) * 128]

    g0 = kv0 + 6 * 128
    qkv0 = g0 + 3 * HEADS
    z0 = qkv0 + 3 * GW
    a0 = z0 + GW

    def rows(a):
        return np.ascontiguousarray(a.reshape(-1, P, a.shape[1]).transpose(1, 0, 2).reshape(P, -1))

    misc = np.concatenate([kvcols(3), kvcols(5), w_in[:, g0:qkv0], w_in[:, a0 + GH:a0 + 2 * GH], w_in[:, a0:a0 + GH]], 1)
    slots = [w_in[:, qkv0 + j * 512:qkv0 + (j + 1) * 512] for j in range(3)]
    slots += [w_in[:, 0:512], np.concatenate([kvcols(2), kvcols(4), kvcols(0), kvcols(1)], 1), w_in[:, z0:z0 + 512]]
    slots = [rows(a) for a in slots]
    slots += [rows(i["cmp_w1"][0, j]) for j in range(2)]
    slots += [rows(i["w_out"][0][:, j * 512:(j + 1) * 512]) for j in range(2)]
    slots += [rows(i["peer_w_query"][0][:, j * 512:(j + 1) * 512]) for j in range(4)]
    par = np.zeros((P, NPARAM), np.float32)

    def put(name, a):
        lo, hi = PARAM[name]
        par[:, lo:hi] = a

    kg = i["nsa_k_gain"][0]
    put("gains", np.concatenate([np.tile(i["nsa_q_gain"][0], 8), np.tile(kg[1], 2), np.tile(kg[2], 2)])[None])
    put("kg0", kg[0][None])
    put("outg", i["gdn_out_gain"][0][None])
    put("alog", i["gdn_a_log"][0][None])
    put("dtb", i["gdn_dt_bias"][0][None])
    put("attng", i["attn_norm"][0].reshape(DC, P).T)
    put("conv", i["gdn_conv"][0].reshape(CONV_K, 12, P).transpose(2, 1, 0).reshape(P, -1))
    put("pos", i["cmp_pos"][0].reshape(2, 16, 2, DH).transpose(2, 3, 0, 1).reshape(P, -1))
    put("w2", i["cmp_w2"][0].reshape(2, 2, P, DH).transpose(2, 0, 1, 3).reshape(P, -1))
    return {
        "consts": constants(), "keep": keep_constants(), "params": par,
        "ffng": np.ascontiguousarray(i["ffn_norm"][0].reshape(DC, P).T),
        "xt": rows(np.ascontiguousarray(x.T)), "x": rows(x), "wmisc": rows(misc), "wslots": np.stack(slots),
        "u": np.ascontiguousarray(i["peer_u"][0].reshape(NKEYS, NKEYS, DC, P).transpose(0, 3, 2, 1)).reshape(NKEYS, P, D),
        "v": i["peer_v"][0].reshape(NKEYS, NKEYS, D),
        "subk": np.ascontiguousarray(i["peer_subkeys"][0].transpose(2, 0, 1).reshape(P, -1)),
    }




def kernel(**inputs):
    import concourse.bacc as bacc
    from concourse.bass_utils import run_bass_kernel_spmd

    arrays = prepare(inputs)
    nc = bacc.Bacc("TRN2", target_bir_lowering=False, num_devices=1)
    d = {n: nc.dram_tensor("in_" + n, a.shape, F32, kind="ExternalInput").ap() for n, a in arrays.items()}
    out = nc.dram_tensor("out", (P, NT * D), F32, kind="ExternalOutput").ap()
    build(nc, d, out)
    r = run_bass_kernel_spmd(nc, [{"in_" + n: a for n, a in arrays.items()}], core_ids=[0])
    y = r.results[0]["out"]
    return y.reshape(P, NT, D).transpose(1, 0, 2).reshape(1, S, D)
```

```python
import math

import numpy as np
import concourse.bass as bass
from concourse import mybir
from concourse.alu_op_type import AluOpType as ALU
from contextlib import ExitStack

F32 = mybir.dt.float32
F32R = mybir.dt.float32r
U32 = mybir.dt.uint32
BF16 = mybir.dt.bfloat16
ACT = mybir.ActivationFunctionType
AX = mybir.AxisListType

P = 128
D, S = 1024, 256
DC = D // P
NT = S // P
HEADS, GROUPS, DH = 8, 2, 64
CMP_BLK, CMP_STRIDE, CMP_HID = 32, 16, 256
NCMP = S // CMP_STRIDE - CMP_BLK // CMP_STRIDE + 1
NC16 = 16
THETA = 10000.0
GH, GD, CONV_K, CHUNK = 4, 128, 4, 64
GW = GH * GD
PH, TOPK, NKEYS = 8, 16, 128
NEG = -1e30
LOWEST = -3.0e38
EPS = 1e-6
SLOT = DC * 512
MISC = 2 * GROUPS * DH + 3 * HEADS + 2 * GH
LEVELS = 6

CONST = {}


def _layout(table, widths):
    at = 0
    for name, n in widths:
        table[name] = (at, at + n)
        at += n
    return at


NCONST = _layout(CONST, [("upper", P), ("nlower", P), ("strict", P), ("nm0", P), ("nm0t", P)]
                 + [(f"mt{l}", P) for l in range(1, LEVELS)]
                 + [("negc", NT * S), ("cneg", NT * NC16), ("any", NT), ("cos", NT * DH), ("sin", NT * DH),
                    ("cosc", DH), ("sinc", DH), ("pm", 2), ("hm", HEADS)])
PARAM = {}
NPARAM = _layout(PARAM, [("gains", 12 * DH), ("kg0", DH), ("outg", GD), ("alog", GH), ("dtb", GH), ("conv", 12 * CONV_K), ("pos", 2 * CMP_BLK // 2), ("w2", 2 * 2 * DH)])


def constants():
    c = np.zeros((P, NCONST), np.float32)

    def put(name, a):
        lo, hi = CONST[name]
        c[:a.shape[0], lo:hi] = a.reshape(a.shape[0], -1)

    p, x = np.arange(P)[:, None], np.arange(P)[None, :]
    same = p // CHUNK == x // CHUNK
    put("upper", (p <= x) & same)
    put("nlower", -1.0 * ((p >= x) & same))
    put("strict", (p > x) & same)
    for l in range(LEVELS):
        s = 1 << l
        m = (p // (2 * s) == x // (2 * s)) & (p // s % 2 == 1) & (x // s % 2 == 0)
        if l == 0:
            put("nm0", -1.0 * m)
            put("nm0t", -1.0 * m.T)
        else:
            put(f"mt{l}", m.T)
    t = np.arange(S).reshape(NT, P)
    put("negc", np.where(np.arange(S)[None, None, :] <= t.T[:, :, None], 0.0, NEG))
    n = np.arange(NC16)
    ends = n * CMP_STRIDE + CMP_BLK - 1
    seen = (ends[None, None, :] <= t.T[:, :, None]) & (n < NCMP)[None, None, :]
    put("cneg", np.where(seen, 0.0, NEG))
    put("any", seen.any(-1))
    half = DH // 2
    inv = np.exp(np.float32(-math.log(THETA) * 2.0) * np.arange(half, dtype=np.float32) / np.float32(DH)).astype(np.float32)

    def rope(pos):
        a = pos.astype(np.float32)[..., None] * inv
        return np.concatenate([np.cos(a)] * 2, -1), np.concatenate([-np.sin(a), np.sin(a)], -1)

    cos, sin = rope(t.T)
    put("cos", cos)
    put("sin", sin)
    cos, sin = rope(np.concatenate([ends, ends]))
    put("cosc", cos)
    put("sinc", sin)
    put("pm", p // 64 == np.arange(2)[None, :])
    put("hm", p // NC16 == np.arange(HEADS)[None, :])
    return c


def keep_constants():
    c = np.zeros((P, 2 * P), np.float32)
    c[:, :P] = np.eye(P)
    c[:, P:] = np.arange(P)[None, :]
    return c


def units():
    out = [(0, br, h, 4) for br in range(2) for h in (0, 4)]
    return out + [(1, br, h, 2) for br in range(2) for h in range(0, 8, 2)]


UNITS = units()


def job_list():
    jobs = [("misc", 0), ("ssq",), ("misc", 1), ("rrow",), ("qkv", 0), ("qkv", 1), ("gcol",), ("qkv", 2), ("l2", 0),
            ("gb", 0), ("qkv", 3), ("l2b", 0), ("l2", 1), ("gb", 1), ("qkv", 4), ("l2b", 1), ("l2", 2), ("qkv", 5),
            ("l2b", 2), ("l2", 3), ("qp", 0), ("l2b", 3), ("kvp", 0), ("kk", 0), ("kk", 1), ("ktok", 0), ("qp", 1),
            ("at", 0), ("at", 1), ("kvp", 1), ("kq", 0), ("kq", 1), ("ktok", 1), ("zp", 0), ("vtok", 0), ("vtok", 1),
            ("zp", 1)]
    gdn = []
    for l in range(1, LEVELS):
        gdn += [[("w", l, 0), ("w", l, 1)], [("pa", l, 0), ("pb", l, 0), ("pa", l, 1), ("pb", l, 1)]]
    gdn += [[("u", 0), ("wt", 0), ("u", 1), ("wt", 1)], [("kv", 0)]]
    for c in range(1, 4):
        gdn += [[("vn", c)], [("o1", c)] + ([("kv", c)] if c < 3 else [])]
        if c % 2:
            gdn[-1] += [("o2", c // 2)]
    nsa = [("kvct", 0), ("kvct", 1), ("qt", 0), ("kt", 0), ("qt", 1), ("kt", 1)]
    nsa += [("h1", 0), ("h1", 1), ("c2k",), ("c2v",), ("s", 0), ("s", 1), ("kct",), ("s", 2), ("sc", 0), ("sc", 1)]
    tail = []
    for u in range(len(UNITS) + 2):
        if u >= 2:
            tail.append(("o", u - 2))
        if u < len(UNITS):
            tail.append(("pt", u))
        if u + 3 < len(UNITS):
            tail.append(("s", u + 3))
        if u == 0:
            tail += [("pct", 0), ("pct", 1)]
        if u == 1:
            tail += [("oc", 0), ("oc", 1)]
    nsa += tail
    at = 0
    for i, g in enumerate(gdn):
        jobs += g
        until = len(nsa) * (i + 1) // len(gdn)
        jobs += nsa[at:until]
        at = until
    jobs += [("ot", T, hf) for T in range(NT) for hf in range(2)]
    jobs += [("y", 0, 0), ("y", 0, 1), ("y", 1, 0), ("xt", 0, 0), ("xt", 0, 1), ("y", 1, 1), ("xt", 1, 0), ("xt", 1, 1)]
    jobs += [("q", b) for b in range(2 * PH)]
    jobs += [("sk", T, b) for T in range(NT) for b in range(4)]
    return jobs


JOBS = job_list()
JOB = {j: n for n, j in enumerate(JOBS)}
BANKS = 8
TOPK_LINKS = 10
PARTS = 3
OH_TOKENS = 8
RSLOTS = 4
NBLK = NKEYS
Q = NBLK // 2 // RSLOTS
SPLIT = (512, 384, 384, 512)
G_BANK, A_BANK = 4, 6
SLOTS = 4
LOADS = [("misc", 1), ("qkv", 1), ("qkv", 3), ("qkv", 5), ("qp", 1), ("kvp", 1), ("zp", 1), ("h1", 0), ("h1", 1),
         ("y", 1, 0), ("y", 1, 1), ("q", 3), ("q", 7), ("q", 11), ("q", 15)]


def build(nc, dram, out_d):
    consts_d, keep_d, params_d, ffng_d, xt_d, x_d, wmisc_d, wslots_d, subk_d, u_d, v_d = (
        dram[n] for n in ("consts", "keep", "params", "ffng", "xt", "x", "wmisc", "wslots", "subk", "u", "v"))
    ctx = ExitStack()
    with ctx:
        def sem(name):
            return ctx.enter_context(nc.semaphore(name))

        def sb(name, cols, dt=F32, where=None, parts=P):
            return (where or ctx).enter_context(nc.sbuf_tensor(name, [parts, cols], dt))

        X = sb("X", NT * D)[:, :].rearrange("p (t d) -> p t d", t=NT)
        KEEP = sb("KEEP", 2 * P)
        IDENT, IOTA = KEEP[:, 0:P], KEEP[:, P:2 * P]
        FFNG = sb("FFNG", DC)[:, :]
        MHALF = sb("MHALF", 1)[:, :]
        SUBK = sb("SUBK", 2 * P)[:, :].rearrange("p (h n) -> p h n", h=2)
        PS = ctx.enter_context(nc.psum_tensor("PS", [P, BANKS, 512], F32))

        early = ExitStack()
        W = sb("W", SLOTS * SLOT, where=early)
        ONES = sb("ONES", P, where=early)
        F_COLS = 34000
        FB = sb("FB", F_COLS, where=early)
        top = [0]

        def take(n, at=None):
            lo = top[0] if at is None else at
            if at is None:
                top[0] += n
                assert top[0] <= F_COLS, top[0]
            return FB[:, lo:lo + n]

        early.close()

        C = take(NCONST)
        PR = take(NPARAM)

        def const(name):
            return C[:, CONST[name][0]:CONST[name][1]]

        def param(name):
            return PR[:, PARAM[name][0]:PARAM[name][1]]

        XT_AT = top[0]
        XG = take(DC + DC * S)
        XT = XG[:, DC:].rearrange("p (c t) -> p c t", c=DC)
        HT = take(DC * S).rearrange("p (c t) -> p c t", c=DC)
        QP_AT = top[0]
        QPW = S + 4
        QP = take(12 * QPW).rearrange("p (b t) -> p b t", b=12)
        CV_AT = top[0]
        CV = take(12 * S).rearrange("p (b t) -> p b t", b=12)
        RN_AT = top[0]
        RN = take(8 * S).rearrange("p (b t) -> p b t", b=8)
        OC_AT = top[0]
        XR = take(NT * 8 * DH).rearrange("p (t h d) -> p t h d", t=NT, d=DH)
        KR = take(NT * 4 * 2 * DH).rearrange("p (t h r d) -> p t h r d", t=NT, r=2, d=DH)
        VSW = take(NT * 4 * DH).rearrange("p (t h d) -> p t h d", t=NT, d=DH)
        GAB = take(NT * 32).rearrange("p (t n) -> p t n", t=NT)
        SG = take(NT * 28).rearrange("p (t n) -> p t n", t=NT)
        Z = take(NT * GW).rearrange("p (t n) -> p t n", t=NT)

        def mat():
            return take(NT * GW).rearrange("p (t h n) -> p t h n", t=NT, h=GH)

        DL, DU, EG, AM, AT_, TI, TT, KBG, KD, VB = (mat() for _ in range(10))
        STATE = take(GW).rearrange("p (h n) -> p h n", h=GH)
        RSTD = take(S)
        TMP = take(1024)
        TMP2 = take(512)
        KCBD = take(64).rearrange("p (g r n) -> p g r n", g=2, r=2)
        HK = take(64).rearrange("p (c n) -> p c n", c=2)
        HV = take(256).rearrange("p (c g m n) -> p c g m n", c=2, g=2, m=4)
        PC = [take(128) for _ in range(2)]
        KC, KC2, KC3 = take(64), take(128), take(64)
        SQ = take(8 * S, at=XT_AT).rearrange("p (b t) -> p b t", b=8)
        XN = X[:, :, 0:768].rearrange("p t (h d) -> p t h d", d=DH)
        KCV = take(NT * 4 * 2 * DH, at=QP_AT).rearrange("p (t h r d) -> p t h r d", t=NT, r=2, d=DH)
        X2 = take(4 * S, at=XT_AT).rearrange("p (k t) -> p k t", k=4)
        YB = take(2 * 16 * 32, at=XT_AT + 4 * S).rearrange("p (k m g n) -> p k m g n", k=2, m=16, g=2)
        KZ = take(4 * 2 * S, at=CV_AT).rearrange("p (b g r t) -> p b g r t", b=2, g=2, r=2)
        QT = take(NT * 512, at=CV_AT + 8 * S).rearrange("p (a t) -> p a t", a=4)
        CT = [take(NT * GW, at=RN_AT + i * NT * GW).rearrange("p (t h n) -> p t h n", t=NT, h=GH) for i in range(2)]
        SM = [take(512, at=at) for at in (QP_AT, QP_AT + 512, XT_AT + 2 * DC * S - 512)]
        PT = [take(512, at=QP_AT + 1024 + 512 * i).rearrange("p (b t) -> p b t", b=4) for i in range(3)]
        VBD = take(512, at=QP_AT + 2560).rearrange("p (h d) -> p h d", h=HEADS)
        OC = take(NT * D, at=OC_AT).rearrange("p (t d) -> p t d", t=NT)
        OT = take(DC * S, at=XT_AT + 2048).rearrange("p (c t) -> p c t", c=DC)
        XNORM = take(NT * D, at=RN_AT).rearrange("p (t d) -> p t d", t=NT)
        WW, U, WT, OG, QD = AM, DL, AM, TI, EG
        PCT = take(256)
        SMA = take(320)
        sm_at = [0]

        def small(n):
            lo = sm_at[0]
            sm_at[0] += n
            assert sm_at[0] <= 320
            return SMA[:, lo:lo + n]

        rs12 = small(24).rearrange("p (t n) -> p t n", t=NT)
        gcs = small(16).rearrange("p (t n) -> p t n", t=NT)
        egs = small(16).rearrange("p (t n) -> p t n", t=NT)
        gate_b = small(8).rearrange("p (t n) -> p t n", t=NT)
        gls = small(16).rearrange("p (t f n) -> p t f n", t=NT, f=2)
        bg = small(8).rearrange("p (t n) -> p t n", t=NT)
        gstep = small(8).rearrange("p (t n) -> p t n", t=NT)
        aexp = small(4)
        rcol = small(NT)
        sp1 = small(8).rearrange("p (t n) -> p t n", t=NT)
        sp2 = small(8).rearrange("p (t n) -> p t n", t=NT)
        mx = small(8)
        nm = [small(4) for _ in range(3)]
        rs = small(48).rearrange("p (u n) -> p u n", u=12)
        rr = small(48).rearrange("p (u n) -> p u n", u=12)
        cs = [small(8), small(8)]
        rc = [small(8), small(8)]
        gr = small(8).rearrange("p (t n) -> p t n", t=NT)
        xs = small(2)
        xss = small(4).rearrange("p (t n) -> p t n", t=NT)
        l2c = small(16).rearrange("p (i n) -> p i n", i=4)
        kcs = small(1)
        EPSC = small(1)

        GATED = sb("GATED", NKEYS * S)
        H2H, H2L = sb("H2H", DC * S, F32R), sb("H2L", DC * S, F32R)
        TABH, TABL = sb("TABH", 2 * D, F32R), sb("TABL", 2 * D, F32R)
        RING = sb("RING", RSLOTS * D)
        CFH, CFL = sb("CFH", 2 * S, F32R), sb("CFL", 2 * S, F32R)
        H2T = sb("H2T", DC * S)
        ROUTE = sb("ROUTE", 3 * S)
        ROUTE_T = sb("ROUTE_T", (2 + PARTS) * S)
        GPART = sb("GPART", S, BF16)
        TOK = sb("TOK", (2 + PARTS) * 16)[:, :].rearrange("p (c q) -> p c q", c=2 + PARTS)
        h2t_at = [0]

        def after_h2t(n):
            h2t_at[0] += n
            return H2T[:, h2t_at[0] - n:h2t_at[0]]

        ONEHOT2 = after_h2t(OH_TOKENS * P // 2).bitcast(BF16).rearrange("p (q n) -> p q n", q=OH_TOKENS)
        ONEHOT1 = after_h2t(OH_TOKENS * PARTS * 64 // 2).bitcast(BF16).rearrange("p (q c n) -> p q c n", q=OH_TOKENS, c=PARTS)
        EQ1 = after_h2t(4 * 64).rearrange("p (q n) -> p q n", q=4)
        GREST = after_h2t(S)
        TOPT = 18432
        QRY = GATED[:, TOPT:TOPT + 16 * S].rearrange("p (b t) -> p b t", b=16)
        SCORES = GATED[:, TOPT + 16 * S:TOPT + 32 * S]
        kt_at = [TOPT + 32 * S]

        def ktake(n):
            kt_at[0] += n
            return GATED[:, kt_at[0] - n:kt_at[0]]

        KS = ktake(2 * NKEYS).rearrange("p (f n) -> p f n", f=2)
        KV_ = ktake(2 * TOPK).rearrange("p (f k) -> p f k", f=2)
        KI = ktake(2 * TOPK).bitcast(U32).rearrange("p (f k) -> p f k", f=2)
        KIF = ktake(2 * TOPK).rearrange("p (f k) -> p f k", f=2)
        CAND = ktake(TOPK * TOPK)
        POS = ktake(TOPK).bitcast(U32)
        POSF = ktake(2 * TOPK).rearrange("p (f k) -> p f k", f=2)
        POSU = ktake(2 * TOPK).bitcast(U32).rearrange("p (f k) -> p f k", f=2)
        EQ = ktake(2 * TOPK * TOPK).rearrange("p (f k a) -> p f k a", f=2, k=TOPK)
        RES = ktake(TOPK)
        GSUM = ktake(2 * PH)[:, :]
        CARRIER = ktake(4)

        params_in, consts_in, keep_in = sem("params_in"), sem("consts_in"), sem("keep_in")
        x_in, subk_in = sem("x_in"), sem("subk_in")
        xt_in, misc_in = [[sem(f"{name}_in{i}") for i in range(2)] for name in ("xt", "misc")]
        weights_in = [sem(f"weights_in{i}") for i in range(SLOTS)]
        ps_full = sem("ps_full")
        ps_free = [sem(f"ps_free{b}") for b in range(BANKS)]
        dve_link, act_link, pool_link = sem("dve_link"), sem("act_link"), sem("pool_link")
        names = ("ones_ready rcol_ready l2_ready x1_sq xsq_ready hT_ready qp_zero exp_misc_done sig_ready softplus_in softplus_exp "
                 "softplus_ln g_ready conv_ready silu_done sq_ready eg_exp gcs_exp darg_ready dexp_done "
                 "dmask_done ti_init tt_init ct_ready qd_ready og_zero og_mean og_rstd oc_gdn xq_mean xq_rstd xr_ready "
                 "y_ready kc_mean kc_rstd kcr_ready sm_ready p_ready scm_ready pc_ready oc_nsa x1_mean x1_rstd "
                 "xn_ready gls_ready").split()
        s = {n: sem(n) for n in names}

        table_in = [sem(f"table_in{k}") for k in range(RSLOTS)]
        query_hi, query_lo_dve, query_lo_pool = sem("query_hi"), sem("query_lo_dve"), sem("query_lo_pool")
        tab_hi = sem("tab_hi")
        tab_lo_dve, tab_lo_pool = sem("tab_lo_dve"), sem("tab_lo_pool")
        blocks_done = sem("blocks_done")
        gelu_done = sem("gelu_done")
        coef_hi, coef_lo_pool, coef_lo_dve = sem("coef_hi"), sem("coef_lo_pool"), sem("coef_lo_dve")
        onehot_ready, gate_mm, gated = sem("onehot_ready"), sem("gate_mm"), sem("gated")
        route_exp_in, route_exp, route_ready, route_t = sem("route_exp_in"), sem("route_exp"), sem("route_ready"), sem("route_t")
        route_t_in, h2_ready, h2h_ready, h2l_ready = sem("route_t_in"), sem("h2_ready"), sem("h2h_ready"), sem("h2l_ready")
        topk_link, tok_ready = sem("topk_link"), sem("tok_ready")
        eq1_ready, keys_ready, cand_ready = sem("eq1_ready"), sem("keys_ready"), sem("cand_ready")
        places_ready, placed = sem("places_ready"), sem("placed")
        out_ready, out_done = sem("out_ready"), sem("out_done")

        def view(t, offset, *dims):
            a = t[:, 0:1]
            return bass.AP(a.tensor, offset, [list(a.ap[0])] + [list(d) for d in dims])

        def query_weights(eng, n):
            load = 11 + n // 4
            eng.wait_ge(weights_in[load % SLOTS], 16 * (load // SLOTS + (load % SLOTS > 0)))
            return wslot(load).rearrange("p (c n) -> p c n", c=DC)[:, :, n % 4 * P:(n % 4 + 1) * P]

        def query_rest(engine, eng, n, lo, hi):
            w = query_weights(eng, n)
            eng.wait_ge(query_hi, n + 1)
            if n >= 2:
                full(eng, "q", n - 2)
            h, r = (t[:, n % 2 * D:(n % 2 + 1) * D].rearrange("p (c n) -> p c n", c=DC)[:, lo:hi] for t in (TABH, TABL))
            return engine.tensor_tensor(r, w[:, lo:hi], h.bitcast(F32), ALU.subtract)

        def table_rest(engine, k, lo, hi):
            h = k % 2 * D
            return engine.tensor_tensor(TABL[:, h + lo:h + hi], RING[:, k * D + lo:k * D + hi],
                                        TABH[:, h + lo:h + hi].bitcast(F32), ALU.subtract)

        def coef_rest(engine, b, k):
            cols = slice(k % 2 * S, (k % 2 + 1) * S)
            return engine.tensor_tensor(CFL[:, cols], view(GATED, (b - NBLK) * S, (1, S)), CFH[:, cols].bitcast(F32),
                                        ALU.subtract)

        def tile4(t, tile, hf):
            return t[:, :].rearrange("p (c t) -> p c t", c=DC)[:, 4 * hf:4 * hf + 4, tile * P:(tile + 1) * P]

        def phases(eng, step, finish=None):
            for ph in range(4):
                step(ph, 0)
                with eng.Fori(1, Q - 1) as m:
                    step(ph, m)
                step(ph, Q - 1)
                if finish:
                    finish(ph)

        def wait(eng, semaphore, value):
            if not isinstance(value, int) or value > 0:
                eng.wait_ge(semaphore, value)

        def full(eng, *job):
            eng.wait_ge(ps_full, JOB[job] + 1)

        def evacuated(eng, *job):
            n = JOB[job]
            eng.wait_ge(ps_free[n % BANKS], n // BANKS + 1)

        def bank(*job):
            return PS[:, JOB[job] % BANKS, :]

        def release(ins, *job):
            ins.then_inc(ps_free[JOB[job] % BANKS], 1)

        def wslot(n):
            return W[:, (n % SLOTS) * SLOT:(n % SLOTS + 1) * SLOT]

        block = ctx.enter_context(nc.Block())

        @block.sync
        def _(sp):
            for i in range(2):
                lo, hi = ((0, DC + DC // 2 * S), (DC + DC // 2 * S, DC + DC * S))[i]
                sp.dma_start(XG[:, lo:hi], xt_d[:, lo:hi]).then_inc(xt_in[i], 16)
                cols = slice(i * (DC // 2) * MISC, (i + 1) * (DC // 2) * MISC)
                sp.dma_start(W[:, cols], wmisc_d[:, cols]).then_inc(misc_in[i], 16)
            sp.dma_start(KEEP[:, :], keep_d).then_inc(keep_in, 16)
            for n in range(1, len(LOADS)):
                if n >= SLOTS:
                    full(sp, *LOADS[n - SLOTS])
                sp.dma_start(wslot(n), wslots_d[n - 1]).then_inc(weights_in[n % SLOTS], 16)
                if n == 1:
                    sp.dma_start(PR, params_d).then_inc(params_in, 16)
                if n == 2:
                    sp.dma_start(C, consts_d).then_inc(consts_in, 16)
                if n == 6:
                    sp.dma_start(FFNG, ffng_d).then_inc(subk_in, 16)
                    sp.dma_start(SUBK.rearrange("p h n -> p (h n)"), subk_d).then_inc(subk_in, 16)
                if n == 9:
                    sp.wait_ge(s["xr_ready"], 4)
                    sp.dma_start(X.rearrange("p t d -> p (t d)"), x_d).then_inc(x_in, 16)

            def table(t_d, i, k):
                a = t_d[0]
                sp.dma_start(RING[:, k * D:(k + 1) * D], bass.AP(a.tensor, i * (P * D), [[D, P], [1, D]]))\
                    .then_inc(table_in[k], 16)

            def step(ph, m):
                for k in range(RSLOTS):
                    b = 4 * m + 4 * Q * ph + k
                    wait(sp, tab_lo_dve, b - RSLOTS + 1)
                    wait(sp, tab_lo_pool, b - RSLOTS + 1)
                    table(u_d if ph < 2 else v_d, b - (0 if ph < 2 else NBLK), k)

            sp.wait_ge(s["xn_ready"], NT)
            phases(sp, step)
            for t in range(NT):
                sp.wait_ge(out_ready, 2 * (t + 1))
                sp.dma_start(out_d[:, t * D:(t + 1) * D], X[:, t]).then_inc(out_done, 16)
            sp.wait_ge(out_done, 16 * NT)

        @block.gpsimd
        def _(pool):
            g = nc.gpsimd
            count = [0]

            def link(ins):
                count[0] += 1
                ins.then_inc(pool_link, 1)
                pool.wait_ge(pool_link, count[0])

            def power(out, in_, shape):
                e = MHALF[0:shape[0], :]
                for _ in range(len(shape) - 2):
                    e = e.unsqueeze(1)
                return g.tensor_tensor(out, in_, e.to_broadcast(shape), ALU.pow)

            link(g.memset(MHALF, -0.5))
            g.memset(QP[:, :, 0:CONV_K - 1], 0.0).then_inc(s["qp_zero"], 1)
            for T in range(NT):
                pool.wait_ge(s["dexp_done"], 2 * T + 2)
                g.tensor_tensor(DL[:, T], DL[:, T], const("strict").unsqueeze(1).to_broadcast([P, GH, P]), ALU.mult)\
                    .then_inc(s["dmask_done"], 1)
                g.tensor_tensor(DU[:, T], DU[:, T], const("upper").unsqueeze(1).to_broadcast([P, GH, P]), ALU.mult)\
                    .then_inc(s["dmask_done"], 1)
            for T in range(NT):
                pool.wait_ge(s["xq_mean"], T + 1)
                power(rs12[:, T], rs12[:, T], [P, 12]).then_inc(s["xq_rstd"], 1)
            evacuated(pool, "l2b", 3)
            pool.wait_ge(s["gls_ready"], 2 * NT)
            for T in range(NT):
                g.tensor_tensor(QD[:, T], EG[:, T], CV[:, 0:4, T * P:(T + 1) * P], ALU.mult).then_inc(s["qd_ready"], 1)
            for l in range(1, LEVELS):
                for T in range(NT):
                    evacuated(pool, "at", T)
                    if l >= 3:
                        full(pool, "w", l - 2, T)
                    g.tensor_tensor(CT[l % 2][:, T], AT_[:, T],
                                    const(f"mt{l}").unsqueeze(1).to_broadcast([P, GH, P]), ALU.mult)\
                        .then_inc(s["ct_ready"], 1)
                if l == 2:
                    pool.wait_ge(s["kc_mean"], 1)
                    power(kcs[0:32, :], kcs[0:32, :], [32, 1]).then_inc(s["kc_rstd"], 1)
            for T in range(NT):
                pool.wait_ge(s["og_mean"], T + 1)
                power(gr[:, T], gr[:, T], [P, GH]).then_inc(s["og_rstd"], 1)
            for T in range(NT):
                query_rest(g, pool, T, DC // 2, DC).then_inc(query_lo_pool, 1)
                pool.wait_ge(s["x1_mean"], T + 1)
                power(xs[:, T:T + 1], xs[:, T:T + 1], [P, 1]).then_inc(s["x1_rstd"], 1)

            for n in range(2, 2 * PH):
                query_rest(g, pool, n, DC // 2, DC).then_inc(query_lo_pool, 1)

            def step(ph, m):
                for k in range(RSLOTS):
                    b = 4 * m + 4 * Q * ph + k
                    if ph == 2:
                        pool.wait_ge(coef_hi, b - NBLK + 1)
                        coef_rest(g, b, k).then_inc(coef_lo_pool, 1)
                    pool.wait_ge(tab_hi, 2 * b + 1)
                    table_rest(g, k, SPLIT[ph], D).then_inc(tab_lo_pool, 1)
                    if ph == 0 and k == 2 and not (isinstance(m, int) and m == 0):
                        place(m - 1)
                    if ph == 0 and k == 1:
                        pool.wait_ge(keys_ready, m + 1)
                        shape = [P, TOPK, TOPK]
                        g.tensor_tensor(CAND.rearrange("p (a b) -> p a b", a=TOPK), KV_[:, 0].unsqueeze(2).to_broadcast(shape),
                                        KV_[:, 1].unsqueeze(1).to_broadcast(shape), ALU.add).then_inc(cand_ready, 1)

            def place(m):
                pool.wait_ge(places_ready, m + 1)
                g.tensor_tensor(EQ, EQ, KIF.unsqueeze(2).to_broadcast([P, 2, TOPK, TOPK]), ALU.mult).then_inc(placed, 1)

            def finish(ph):
                if ph == 0:
                    place(Q - 1)

            phases(pool, step, finish)

        @block.tensor
        def _(pe):
            mm = nc.tensor.matmul

            def begin(*job):
                n = JOB[job]
                if n >= BANKS:
                    pe.wait_ge(ps_free[n % BANKS], n // BANKS)
                return bank(*job)

            def end(ins):
                ins.then_inc(ps_full, 1)

            def weights(n):
                pe.wait_ge(weights_in[n % SLOTS], 16 * (n // SLOTS + (n % SLOTS > 0)))
                return wslot(n)

            def products(out, k, first=False):
                hi, lo = (t[:, k * D:(k + 1) * D] for t in (TABH, TABL))
                for n, (w, h) in enumerate(((hi, H2H), (lo, H2H), (hi, H2L))):
                    if first and h is H2L:
                        pe.wait_ge(h2l_ready, 2 * NT)
                    for c in range(DC):
                        last = mm(out, w[:, c * P:(c + 1) * P], h[:, c * S:(c + 1) * S],
                                  start=n == 0 and c == 0, stop=n == 2 and c == DC - 1)
                return last

            def rows(job, b, lhs, w, lo, n):
                for c in range(DC):
                    last = mm(b[:, 0:n], lhs[:, c], w[:, c, lo:lo + n], start=c == 0, stop=c == DC - 1)
                end(last)

            def row(b, i, column):
                return mm(b[:, i * P:(i + 1) * P], column.to_broadcast([P, P]), IDENT, start=True, stop=True)

            def transposes(job, b, ins_, ident=IDENT):
                for i, a in enumerate(ins_):
                    last = nc.tensor.transpose(b[:, i * P:(i + 1) * P], a, ident)
                end(last)

            def run(job):
                kind, *a = job
                T = a[-1] if a else 0
                b = begin(*job)
                if kind == "ssq":
                    pe.wait_ge(s["ones_ready"], 1)
                    pe.wait_ge(s["xsq_ready"], 2)
                    for t in range(NT):
                        for c in range(DC):
                            last = mm(b[:, t:t + 1], CV[:, c, t * P:(t + 1) * P], ONES[:, 0:1], start=c == 0, stop=c == DC - 1)
                    end(last)
                elif kind == "misc":
                    w = wslot(0)[:, 0:DC * MISC].rearrange("p (c n) -> p c n", c=DC)
                    for c in range(DC):
                        if T == 0:
                            pe.wait_ge(s["hT_ready"], c + 1)
                            if c % 4 == 0:
                                pe.wait_ge(misc_in[c // 4], 16)
                        last = mm(b[:, 0:MISC], HT[:, c, T * P:(T + 1) * P], w[:, c], start=c == 0, stop=c == DC - 1)
                    end(last)
                elif kind == "rrow":
                    pe.wait_ge(s["rcol_ready"], 1)
                    pe.wait_ge(keep_in, 16)
                    for t in range(NT):
                        last = row(b, t, rcol[:, t:t + 1])
                    end(last)
                elif kind == "qkv":
                    w = weights(1 + a[0] // 2).rearrange("p (c n) -> p c n", c=DC)
                    for i in range(2):
                        o = (2 * a[0] + i) % 4 * P
                        for c in range(DC):
                            last = mm(b[:, i * S:(i + 1) * S], w[:, c, o:o + P], HT[:, c], start=c == 0, stop=c == DC - 1)
                    end(last)
                elif kind in ("qp", "kvp", "zp"):
                    n = {"qp": 4, "kvp": 5, "zp": 6}[kind]
                    w = weights(n).rearrange("p (c n) -> p c n", c=DC)
                    rows(job, b, HT[:, :, T * P:(T + 1) * P], w, 0, 512)
                elif kind == "gcol":
                    pe.wait_ge(s["g_ready"], 1)
                    pe.wait_ge(consts_in, 16)
                    for t in range(NT):
                        mm(b[:, t * 8:t * 8 + 4], const("upper"), gstep[:, t], start=True, stop=True)
                        last = mm(b[:, t * 8 + 4:t * 8 + 8], const("strict"), gstep[:, t], start=True, stop=True)
                    end(last)
                elif kind == "gb":
                    for h in range(GH):
                        last = mm(b[:, h * P:(h + 1) * P], gstep[:, T, h:h + 1].to_broadcast([P, P]), const("upper"),
                                  start=True, stop=True)
                    end(last)
                elif kind == "l2":
                    pe.wait_ge(s["sq_ready"], a[0] + 1)
                    for n in range(4):
                        last = mm(b[:, n:n + 1], SQ[:, 2 * a[0] + n // 2, n % 2 * P:(n % 2 + 1) * P], ONES[:, 0:1],
                                  start=True, stop=True)
                    end(last)
                elif kind == "l2b":
                    pe.wait_ge(s["l2_ready"], a[0] + 1)
                    for n in range(4):
                        last = row(b, n, l2c[:, a[0], n:n + 1])
                    end(last)
                elif kind in ("kk", "kq"):
                    evacuated(pe, "l2b", 3)
                    ts = slice(T * P, (T + 1) * P)
                    for h in range(GH):
                        last = mm(b[:, h * P:(h + 1) * P], CV[:, 4 + h, ts], CV[:, (4 if kind == "kk" else 0) + h, ts],
                                  start=True, stop=True)
                    end(last)
                elif kind == "at":
                    evacuated(pe, "kk", T)
                    transposes(job, b, [AM[:, T, h] for h in range(GH)])
                elif kind == "ktok":
                    evacuated(pe, "l2b", 3)
                    transposes(job, b, [CV[:, 4 + h, T * P:(T + 1) * P] for h in range(GH)])
                elif kind == "vtok":
                    pe.wait_ge(s["silu_done"], 6)
                    transposes(job, b, [CV[:, 8 + h, T * P:(T + 1) * P] for h in range(GH)])
                elif kind == "kvct":
                    evacuated(pe, "kvp", T)
                    transposes(job, b, [KCV[:, T, i] for i in range(4)])
                elif kind == "qt":
                    pe.wait_ge(s["xr_ready"], 2 * T + 1)
                    transposes(job, b, [XR[:, T, 2 * i:2 * i + 2] for i in range(4)])
                elif kind == "kt":
                    pe.wait_ge(s["xr_ready"], 2 * T + 2)
                    transposes(job, b, [KR[:, T, i] for i in range(4)])
                elif kind == "w":
                    l = a[0]
                    pe.wait_ge(s["ct_ready"], NT * (l - 1) + T + 1)
                    if l == 1:
                        pe.wait_ge(s["ti_init"], T + 1)
                    else:
                        evacuated(pe, "pa", l - 1, T)
                    for h in range(GH):
                        last = mm(b[:, h * P:(h + 1) * P], CT[l % 2][:, T, h], TI[:, T, h], start=True, stop=True)
                    end(last)
                elif kind in ("pa", "pb"):
                    l = a[0]
                    evacuated(pe, "w", l, T)
                    if l == 1:
                        pe.wait_ge(s["tt_init"], T + 1)
                    else:
                        evacuated(pe, "pb", l - 1, T)
                    for h in range(GH):
                        lhs, rhs = (TT[:, T, h], WW[:, T, h]) if kind == "pa" else (WW[:, T, h], TT[:, T, h])
                        last = mm(b[:, h * P:(h + 1) * P], lhs, rhs, start=True, stop=True)
                    end(last)
                elif kind in ("u", "wt"):
                    evacuated(pe, "pb", LEVELS - 1, T)
                    evacuated(pe, "vtok" if kind == "u" else "ktok", T)
                    for h in range(GH):
                        lhs, rhs = (TT[:, T, h], VB[:, T, h]) if kind == "u" else (KBG[:, T, h], TT[:, T, h])
                        last = mm(b[:, h * P:(h + 1) * P], lhs, rhs, start=True, stop=True)
                    end(last)
                elif kind == "kv":
                    c = a[0]
                    t, r = c // 2, slice(64 * (c % 2), 64 * (c % 2) + 64)
                    if c == 0:
                        evacuated(pe, "u", 0)
                    else:
                        evacuated(pe, "vn", c)
                    for h in range(GH):
                        last = mm(b[:, h * P:(h + 1) * P], KD[r, t, h], U[r, t, h], start=True, stop=True)
                    end(last)
                elif kind in ("vn", "o1"):
                    c = a[0]
                    t, r = c // 2, slice(64 * (c % 2), 64 * (c % 2) + 64)
                    if kind == "vn":
                        evacuated(pe, "wt", t)
                        evacuated(pe, "kv", c - 1)
                    else:
                        pe.wait_ge(s["qd_ready"], NT)
                    src = WT if kind == "vn" else QD
                    for h in range(GH):
                        last = mm(b[r, h * P:(h + 1) * P], src[:, t, h, r], STATE[:, h], start=True, stop=True)
                    end(last)
                elif kind == "o2":
                    evacuated(pe, "vn", 2 * T + 1)
                    if T:
                        evacuated(pe, "vn", 2 * T)
                    evacuated(pe, "kq", T)
                    for h in range(GH):
                        last = mm(b[:, h * P:(h + 1) * P], DU[:, T, h], U[:, T, h], start=True, stop=True)
                    end(last)
                elif kind == "h1":
                    kv = a[0]
                    w = weights(7 + kv).rearrange("p (m n) -> p m n", m=16)
                    pe.wait_ge(s["y_ready"], kv + 1)
                    for hc in range(2):
                        for m in range(16):
                            last = mm(b[:, hc * 32:hc * 32 + 32], w[:, m, hc * P:(hc + 1) * P], YB[:, kv, m],
                                      start=m == 0, stop=m == 15)
                    end(last)
                elif kind == "c2k":
                    evacuated(pe, "h1", 0)
                    w2 = param("w2").rearrange("p (k c n) -> p k c n", k=2, c=2)
                    for hc in range(2):
                        last = mm(b[0:32, 0:DH], HK[:, hc], w2[:, 0, hc], start=hc == 0, stop=hc == 1)
                    end(last)
                elif kind == "c2v":
                    evacuated(pe, "h1", 1)
                    w2 = param("w2").rearrange("p (k c n) -> p k c n", k=2, c=2)
                    for hc in range(2):
                        last = mm(b[:, 0:DH], HV[:, hc].rearrange("p g m n -> p (g m n)"), w2[:, 1, hc], start=hc == 0, stop=hc == 1)
                    end(last)
                elif kind == "kct":
                    pe.wait_ge(s["kcr_ready"], 1)
                    end(nc.tensor.transpose(b[:, 0:32], KC2[0:32, :], IDENT[0:32, 0:32]))
                elif kind == "sc":
                    evacuated(pe, "kct")
                    evacuated(pe, "qt", T)
                    for p in range(4):
                        last = mm(b[:, p * 32:p * 32 + 32], QT[:, p, T * P:(T + 1) * P], KCBD[:, p // 2], start=True, stop=True)
                    end(last)
                elif kind == "pct":
                    pe.wait_ge(s["pc_ready"], T + 1)
                    transposes(job, b, [PC[T]])
                elif kind == "oc":
                    evacuated(pe, "pct", T)
                    evacuated(pe, "c2v")
                    end(mm(b[:, :], PCT[:, T * P:(T + 1) * P], VBD, start=True, stop=True))
                elif kind == "s":
                    t, br, h0, nh = UNITS[a[0]]
                    evacuated(pe, "qt", t)
                    for t_ in range(t + 1):
                        evacuated(pe, "kt", t_)
                    nk = (t + 1) * P
                    for i in range(nh // 2):
                        last = mm(b[:, i * 2 * nk:(i + 1) * 2 * nk], QT[:, h0 // 2 + i, t * P:(t + 1) * P],
                                  KZ[:, br, h0 // 4, :, 0:nk], start=True, stop=True)
                    end(last)
                elif kind == "pt":
                    pe.wait_ge(s["p_ready"], a[0] + 1)
                    transposes(job, b, [SM[a[0] % 3][:, i * P:(i + 1) * P] for i in range(4)])
                elif kind == "o":
                    u = a[0]
                    t, br, h0, nh = UNITS[u]
                    evacuated(pe, "pt", u)
                    nb = t + 1
                    for i in range(nh):
                        for kb in range(nb):
                            last = mm(b[:, i * DH:(i + 1) * DH], PT[u % 3][:, i * nb + kb],
                                      VSW[:, kb, 2 * br + (h0 + i) // 4], start=kb == 0, stop=kb == nb - 1)
                    end(last)
                elif kind == "ot":
                    t, hf = a
                    if hf == 0:
                        pe.wait_ge(s["oc_nsa"], len(UNITS))
                    else:
                        pe.wait_ge(s["oc_gdn"], t + 1)
                    transposes(job, b, [OC[:, t, (4 * hf + i) * P:(4 * hf + i + 1) * P] for i in range(4)])
                elif kind == "y":
                    t, hf = a
                    w = weights(9 + hf).rearrange("p (c n) -> p c n", c=DC)
                    for i in range(2):
                        evacuated(pe, "ot", t, i)
                    rows(job, b, OT[:, :, t * P:(t + 1) * P], w, 0, 512)
                elif kind == "xt":
                    t, hf = a
                    pe.wait_ge(s["xn_ready"], t + 1)
                    transposes(job, b, [XNORM[:, t, (4 * hf + i) * P:(4 * hf + i + 1) * P] for i in range(4)])
                elif kind == "q":
                    n = a[0]
                    pe.wait_ge(query_lo_dve, n + 1)
                    pe.wait_ge(query_lo_pool, n + 1)
                    pe.wait_ge(h2h_ready, 2 * NT)
                    end(products(b[:, 0:S], n % 2, first=n == 0))
                elif kind == "sk":
                    t, k = a
                    pe.wait_ge(subk_in, 32)
                    for i in range(4):
                        evacuated(pe, "q", 4 * k + i)
                    for i in range(4):
                        last = mm(b[:, i * P:(i + 1) * P], QRY[:, 4 * k + i, t * P:(t + 1) * P], SUBK[:, i % 2],
                                  start=True, stop=True)
                    end(last)

            for job in JOBS:
                run(job)

            def gates(ph, m, k):
                g = m + Q * (ph - 1)
                pe.wait_ge(onehot_ready, 4 * g + k + 1)
                for idx in range(4 * k, 4 * k + 4):
                    if idx % 8 == 0:
                        wait(pe, gated, 2 * g - 1 + idx // 8)
                    q = idx % OH_TOKENS
                    for c in range(PARTS):
                        last = mm(PS[:, G_BANK + idx // 8, idx % 8 * 64:idx % 8 * 64 + 64], ONEHOT2[:, q], ONEHOT1[:, q, c],
                                  start=c == 0, stop=c == PARTS - 1)
                last.then_inc(gate_mm, 1)

            def step(ph, m):
                for k in range(RSLOTS):
                    b = 4 * m + 4 * Q * ph + k
                    if ph in (1, 2):
                        gates(ph, m, k)
                    pe.wait_ge(tab_lo_dve, b + 1)
                    pe.wait_ge(tab_lo_pool, b + 1)
                    if ph < 2:
                        wait(pe, gelu_done, b - 1)
                        last = products(PS[:, A_BANK + k % 2, 0:S], k % 2)
                    else:
                        if ph == 2:
                            pe.wait_ge(coef_lo_pool, b - NBLK + 1)
                        else:
                            pe.wait_ge(coef_lo_dve, b - NBLK - NBLK // 2 + 1)
                        hi, lo = (t[:, k % 2 * D:(k % 2 + 1) * D] for t in (TABH, TABL))
                        first = ph == 2 and isinstance(m, int) and m == 0 and k == 0
                        final = ph == 3 and isinstance(m, int) and m == Q - 1 and k == RSLOTS - 1
                        for t in range(NT):
                            chi, clo = (x[:, k % 2 * S + t * P:k % 2 * S + (t + 1) * P] for x in (CFH, CFL))
                            for n, (cf, tab) in enumerate(((chi, hi), (chi, lo), (clo, hi))):
                                for hf in range(2):
                                    last = mm(PS[:, 2 * t + hf, :], cf, tab[:, hf * 512:(hf + 1) * 512],
                                              start=first and n == 0, stop=final and n == 2)
                    last.then_inc(blocks_done, 1)

            def finish(ph):
                if ph == 0:
                    pe.wait_ge(route_ready, 1)
                    for c in range(3):
                        for t in range(NT):
                            i = c * NT + t
                            last = nc.tensor.transpose(PS[:, G_BANK + i // 4, i % 4 * P:(i % 4 + 1) * P],
                                                       ROUTE[:, i * P:(i + 1) * P], IDENT)
                    last.then_inc(route_t_in, 1)

            phases(pe, step, finish)

        @block.scalar
        def _(act):
            A = nc.scalar.activation

            def split_query(n):
                w = query_weights(act, n)
                if n < 2:
                    full(act, "ot", 1, 1)
                    act.wait_ge(s["oc_gdn"], NT)
                A(TABH[:, n % 2 * D:(n % 2 + 1) * D].rearrange("p (c n) -> p c n", c=DC), w, ACT.Copy).then_inc(query_hi, 1)

            def run(job):
                kind, *a = job
                T = a[-1] if a else 0
                b = bank(*job)
                if kind == "ssq":
                    for i in range(2):
                        act.wait_ge(xt_in[i], 16)
                        A(CV[:, 4 * i:4 * i + 4], XT[:, 4 * i:4 * i + 4], ACT.Square).then_inc(s["xsq_ready"], 1)
                    act.wait_ge(s["ones_ready"], 2)
                    full(act, *job)
                    release(A(rcol, b[:, 0:NT], ACT.Sqrt, bias=EPSC, scale=1.0 / D), *job)
                elif kind == "rrow":
                    act.wait_ge(s["softplus_in"], 1)
                    A(SG, GAB[:, :, 0:28], ACT.Exp, scale=-1.0).then_inc(s["exp_misc_done"], 1)
                    A(aexp, param("alog"), ACT.Exp).then_inc(s["exp_misc_done"], 1)
                    A(sp1, sp1, ACT.Exp, scale=-1.0).then_inc(s["softplus_exp"], 1)
                    act.wait_ge(s["softplus_exp"], 1)
                    A(sp1, sp1, ACT.Ln, bias=1.0).then_inc(s["softplus_ln"], 1)
                elif kind == "qkv":
                    n = a[0]
                    act.wait_ge(s["conv_ready"], n + 1)
                    A(CV[:, 2 * n:2 * n + 2], CV[:, 2 * n:2 * n + 2], ACT.Silu).then_inc(s["silu_done"], 1)
                    if n < 4:
                        act.wait_ge(s["silu_done"], n + 1)
                        if n == 0:
                            act.wait_ge(s["hT_ready"], DC)
                        A(SQ[:, 2 * n:2 * n + 2], CV[:, 2 * n:2 * n + 2], ACT.Square).then_inc(s["sq_ready"], 1)
                elif kind == "l2":
                    i = a[0]
                    full(act, *job)
                    release(A(l2c[:, i], b[:, 0:4], ACT.Sqrt, bias=EPSC), *job)
                elif kind == "gcol":
                    evacuated(act, *job)
                    A(egs, gcs, ACT.Exp).then_inc(s["gcs_exp"], 1)
                elif kind == "gb":
                    full(act, *job)
                    A(EG[:, T], b.rearrange("p (h n) -> p h n", h=GH), ACT.Exp).then_inc(s["eg_exp"], 1)
                    for i, m in enumerate((DL, DU)):
                        act.wait_ge(s["darg_ready"], 2 * T + i + 1)
                        A(m[:, T], m[:, T], ACT.Exp).then_inc(s["dexp_done"], 1)
                elif kind == "zp":
                    full(act, *job)
                    act.wait_ge(s["rcol_ready"], 1)
                    release(A(Z[:, T], b, ACT.Silu, scale=rcol[:, T:T + 1]), *job)
                elif kind in ("at", "w", "u", "wt", "qt", "kvct", "pct", "pt"):
                    full(act, *job)
                    dst = {"at": lambda: AT_[:, T], "w": lambda: WW[:, T], "u": lambda: U[:, T], "wt": lambda: WT[:, T],
                           "qt": lambda: QT[:, :, T * P:(T + 1) * P], "kvct": lambda: X2[:, :, T * P:(T + 1) * P],
                           "pct": lambda: PCT[:, T * P:(T + 1) * P], "pt": lambda: PT[a[0] % 3]}[kind]()
                    if kind == "kvct":
                        full(act, "l2", 3)
                    if kind == "w" and a[0] == 1:
                        act.wait_ge(s["ti_init"], T + 1)
                    if kind == "pt" and a[0] >= 3:
                        full(act, "o", a[0] - 3)
                    src = b[:, 0:P] if kind == "pct" else b
                    if kind != "pct":
                        src = src.rearrange("p (h n) -> p h n", h=4)
                    release(A(dst, src, ACT.Copy), *job)
                elif kind == "o1":
                    c = a[0]
                    r = slice(64 * (c % 2), 64 * (c % 2) + 64)
                    full(act, *job)
                    release(A(OG[r, c // 2], b[r, :].rearrange("p (h n) -> p h n", h=GH), ACT.Copy), *job)
                elif kind == "h1":
                    full(act, *job)
                    src = b[:, 0:64].rearrange("p (c n) -> p c n", c=2)
                    if a[0] == 0:
                        ins = A(HK, src, ACT.Gelu_apprx_tanh)
                    else:
                        for c in range(2):
                            ins = A(HV[:, c], src[:, c].rearrange("p (g n) -> p g n", g=2).unsqueeze(2)
                                    .to_broadcast([P, 2, 4, NC16]), ACT.Gelu_apprx_tanh)
                    release(ins, *job)
                elif kind == "s":
                    u = a[0]
                    t, br, h0, nh = UNITS[u]
                    nk = (t + 1) * P
                    act.wait_ge(s["sm_ready"], u + 1)
                    for i in range(nh):
                        v = SM[u % 3][:, i * nk:(i + 1) * nk]
                        last = A(v, v, ACT.Exp, bias=nm[u % 3][:, i:i + 1], scale=DH ** -0.5, accum_out=rs[:, u, i:i + 1])
                    last.then_inc(s["p_ready"], 1)
                elif kind == "sc":
                    act.wait_ge(s["scm_ready"], T + 1)
                    A(PC[T], PC[T], ACT.Exp, scale=DH ** -0.5).then_inc(s["pc_ready"], 1)
                elif kind == "ot":
                    full(act, *job)
                    t, hf = a
                    release(A(OT[:, 4 * hf:4 * hf + 4, t * P:(t + 1) * P], b.rearrange("p (c n) -> p c n", c=4), ACT.Copy),
                            *job)
                elif kind == "y":
                    t, hf = a
                    if (t, hf) in ((0, 1), (1, 0)):
                        split_query(t)
                    evacuated(act, *job)
                    A(XNORM[:, t, hf * 512:(hf + 1) * 512], X[:, t, hf * 512:(hf + 1) * 512], ACT.Square,
                      accum_out=xss[:, t, hf:hf + 1]).then_inc(s["x1_sq"], 1)
                elif kind == "xt":
                    evacuated(act, *job)
                    A(tile4(H2H, *a), tile4(H2T, *a), ACT.Copy).then_inc(h2h_ready, 1)
                elif kind == "q":
                    full(act, *job)
                    if a[0] + 2 < 2 * PH:
                        split_query(a[0] + 2)
                    release(A(QRY[:, a[0]], b[:, 0:S], ACT.Copy), *job)

            for job in JOBS:
                run(job)

            def gelu(b, k):
                act.wait_ge(blocks_done, b + 1)
                A(view(GATED, b * S, (1, S)), PS[:, A_BANK + k % 2, 0:S], ACT.Gelu_apprx_tanh).then_inc(gelu_done, 1)

            def coef_round(ph, b, k):
                if k == 0:
                    act.wait_ge(gated, 2 * Q * (ph - 1))
                A(CFH[:, k % 2 * S:(k % 2 + 1) * S], view(GATED, (b - NBLK) * S, (1, S)), ACT.Copy).then_inc(coef_hi, 1)

            def step(ph, m):
                for k in range(RSLOTS):
                    b = 4 * m + 4 * Q * ph + k
                    act.wait_ge(table_in[k], 16 * (m + Q * ph + 1))
                    wait(act, blocks_done, b - 1)
                    if ph == 2:
                        if isinstance(b, int) and b == NBLK:
                            gelu(b - 2, 0)
                            gelu(b - 1, 1)
                        coef_round(ph, b, k)
                    for lo, hi in ((SPLIT[ph], D), (0, SPLIT[ph])):
                        A(TABH[:, k % 2 * D + lo:k % 2 * D + hi], RING[:, k * D + lo:k * D + hi], ACT.Copy)\
                            .then_inc(tab_hi, 1)
                    if ph == 3:
                        coef_round(ph, b, k)
                    if ph < 2 and not (isinstance(b, int) and b < 2):
                        gelu(b - 2, k)

            def finish(ph):
                if ph == 0:
                    act.wait_ge(route_exp_in, 1)
                    A(ROUTE[:, 2 * S:3 * S], ROUTE[:, 2 * S:3 * S], ACT.Exp).then_inc(route_exp, 1)

            phases(act, step, finish)

        @block.vector
        def _(dve):
            v = nc.vector
            count = [0]

            def link(ins):
                count[0] += 1
                ins.then_inc(dve_link, 1)
                dve.wait_ge(dve_link, count[0])

            def bc(a, axis, shape):
                return a.unsqueeze(axis).to_broadcast(shape)

            def heads(b, h):
                return b.rearrange("p (h n) -> p h n", h=h)

            def rotate(T):
                dve.wait_ge(s["xq_rstd"], T + 1)
                link(v.tensor_tensor(XN[:, T], XN[:, T], bc(rs12[:, T], 2, [P, 12, DH]), ALU.mult))
                link(v.tensor_tensor(XN[:, T], XN[:, T], param("gains").rearrange("p (h d) -> p h d", d=DH), ALU.mult))
                sq = TMP[:, 0:768].rearrange("p (h d) -> p h d", d=DH)
                cos = const("cos").rearrange("p (t d) -> p t d", t=NT)[:, T]
                sin = const("sin").rearrange("p (t d) -> p t d", t=NT)[:, T]
                hd = DH // 2
                v.tensor_tensor(XR[:, T], XN[:, T, 0:8], bc(cos, 1, [P, 8, DH]), ALU.mult)
                kr = TMP2[:, 0:4 * DH].rearrange("p (h d) -> p h d", d=DH)
                v.tensor_tensor(kr, XN[:, T, 8:12], bc(cos, 1, [P, 4, DH]), ALU.mult)
                v.tensor_tensor(sq[:, :, 0:hd], XN[:, T, :, hd:DH], bc(sin[:, 0:hd], 1, [P, 12, hd]), ALU.mult)
                link(v.tensor_tensor(sq[:, :, hd:DH], XN[:, T, :, 0:hd], bc(sin[:, hd:DH], 1, [P, 12, hd]), ALU.mult))
                v.tensor_tensor(XR[:, T], XR[:, T], sq[:, 0:8], ALU.add).then_inc(s["xr_ready"], 1)
                v.tensor_tensor(KR[:, T], bc(kr, 2, [P, 4, 2, DH]), bc(sq[:, 8:12], 2, [P, 4, 2, DH]), ALU.add)\
                    .then_inc(s["xr_ready"], 1)

            def run(job):
                kind, *a = job
                T = a[-1] if a else 0
                b = bank(*job)
                if kind == "ssq":
                    evacuated(dve, *job)
                    v.reciprocal(rcol, rcol).then_inc(s["rcol_ready"], 1)
                elif kind == "rrow":
                    full(dve, *job)
                    release(v.tensor_copy(RSTD, b[:, 0:S]), *job)
                    dve.wait_ge(s["rcol_ready"], 1)
                    for t in range(NT):
                        full(dve, "misc", t)
                        m = bank("misc", t)
                        v.tensor_scalar(VSW[:, t], m[:, 0:256].rearrange("p (h d) -> p h d", d=DH), rcol[:, t:t + 1], None,
                                        ALU.mult)
                        release(v.tensor_scalar(GAB[:, t], m[:, 256:288], rcol[:, t:t + 1], None, ALU.mult), "misc", t)
                        evacuated(dve, "misc", t)
                    evacuated(dve, *job)
                    dve.wait_ge(params_in, 16)
                    link(v.tensor_tensor(sp2, GAB[:, :, 28:32], bc(param("dtb"), 1, [P, NT, GH]), ALU.add))
                    link(v.tensor_scalar(sp1, sp2, -1.0, None, ALU.mult))
                    v.tensor_tensor(sp1, sp1, sp2, ALU.max).then_inc(s["softplus_in"], 1)
                    link(v.tensor_scalar(sp2, sp2, 0.0, None, ALU.max))
                elif kind == "qkv":
                    full(dve, *job)
                    dve.wait_ge(s["qp_zero"], 1)
                    qp = QP[:, 2 * a[0]:2 * a[0] + 2, CONV_K - 1:CONV_K - 1 + S]
                    release(v.tensor_tensor(qp, b.rearrange("p (b t) -> p b t", b=2), bc(RSTD, 1, [P, 2, S]), ALU.mult), *job)
                    evacuated(dve, *job)
                    w = param("conv").rearrange("p (b j) -> p b j", b=12)
                    for j in range(CONV_K):
                        for i in (2 * a[0], 2 * a[0] + 1):
                            src = QP[:, i, j:j + S]
                            if j == 0:
                                ins = v.tensor_scalar(CV[:, i], src, w[:, i, 0:1], None, ALU.mult)
                            else:
                                ins = v.scalar_tensor_tensor(CV[:, i], src, w[:, i, j:j + 1], CV[:, i], ALU.mult, ALU.add)
                        if j < CONV_K - 1:
                            link(ins)
                    ins.then_inc(s["conv_ready"], 1)
                    if a[0] == 0:
                        dve.wait_ge(s["softplus_ln"], 1)
                        dve.wait_ge(s["exp_misc_done"], 2)
                        link(v.tensor_tensor(sp2, sp2, sp1, ALU.add))
                        link(v.tensor_scalar(aexp, aexp, -1.0, None, ALU.mult))
                        v.tensor_tensor(gstep, sp2, bc(aexp, 1, [P, NT, GH]), ALU.mult).then_inc(s["g_ready"], 1)
                        link(v.tensor_scalar(SG, SG, 1.0, None, ALU.add))
                        v.reciprocal(SG, SG).then_inc(s["sig_ready"], 1)
                elif kind == "gcol":
                    full(dve, *job)
                    dve.wait_ge(consts_in, 16)
                    release(v.tensor_copy(gcs, b[:, 0:16].rearrange("p (t n) -> p t n", t=NT)), *job)
                    dve.wait_ge(s["gcs_exp"], 1)
                    dve.wait_ge(s["sig_ready"], 1)
                    v.tensor_tensor(bg, egs[:, :, 0:4], SG[:, :, 24:28], ALU.mult)
                elif kind == "gb":
                    dve.wait_ge(s["eg_exp"], T + 1)
                    release(v.tensor_tensor(TMP2.rearrange("p (h n) -> p h n", h=GH), heads(b, GH),
                                            bc(gcs[:, T, 0:4], 2, [P, GH, P]), ALU.subtract), *job)
                    evacuated(dve, *job)
                    src = TMP2.rearrange("p (h n) -> p h n", h=GH)
                    v.tensor_tensor(DL[:, T], src, bc(const("nlower"), 1, [P, GH, P]), ALU.mult).then_inc(s["darg_ready"], 1)
                    v.tensor_tensor(DU[:, T], src, bc(const("upper"), 1, [P, GH, P]), ALU.mult).then_inc(s["darg_ready"], 1)
                    for f in range(2):
                        v.tensor_copy(gls[:, T, f], EG[:, T, :, 64 * f + 63]).then_inc(s["gls_ready"], 1)
                elif kind == "l2":
                    i = a[0]
                    evacuated(dve, *job)
                    v.reciprocal(l2c[:, i], l2c[:, i]).then_inc(s["l2_ready"], 1)
                elif kind == "l2b":
                    i = a[0]
                    full(dve, *job)
                    dve.wait_ge(s["silu_done"], i + 1)
                    dve.wait_ge(s["sq_ready"], i + 1)
                    for k in range(2):
                        n = 2 * i + k
                        ins = v.scalar_tensor_tensor(CV[:, n], CV[:, n], GD ** -0.5 if n < 4 else 1.0,
                                                     b[:, k * S:(k + 1) * S], ALU.mult, ALU.mult)
                    release(ins, *job)
                elif kind == "qp":
                    full(dve, *job)
                    release(v.tensor_scalar(XN[:, T, 0:8], b.rearrange("p (h d) -> p h d", d=DH), rcol[:, T:T + 1], None,
                                            ALU.mult), *job)
                elif kind == "kvp":
                    full(dve, *job)
                    v.tensor_scalar(XN[:, T, 8:12], b[:, 0:256].rearrange("p (h d) -> p h d", d=DH), rcol[:, T:T + 1], None,
                                    ALU.mult)
                    release(v.tensor_scalar(KCV[:, T], bc(b[:, 256:512].rearrange("p (h d) -> p h d", d=DH), 2,
                                                          [P, 4, 2, DH]), rcol[:, T:T + 1], None, ALU.mult), *job)
                    evacuated(dve, *job)
                    sq = TMP[:, 0:768].rearrange("p (h d) -> p h d", d=DH)
                    link(v.tensor_tensor(sq, XN[:, T], XN[:, T], ALU.mult))
                    link(v.tensor_reduce(rs12[:, T], sq, AX.X, ALU.add))
                    v.tensor_scalar(rs12[:, T], rs12[:, T], 1.0 / DH, EPS, ALU.mult, ALU.add).then_inc(s["xq_mean"], 1)
                elif kind == "kk":
                    full(dve, *job)
                    dve.wait_ge(s["dmask_done"], 2 * T + 1)
                    for h in range(GH):
                        ins = v.scalar_tensor_tensor(AM[:, T, h], b[:, h * P:(h + 1) * P], SG[:, T, 24 + h:25 + h],
                                                     DL[:, T, h], ALU.mult, ALU.mult)
                    release(ins, *job)
                    evacuated(dve, *job)
                    link(v.tensor_tensor(TI[:, T], AM[:, T], bc(const("nm0"), 1, [P, GH, P]), ALU.mult))
                    v.tensor_tensor(TI[:, T], TI[:, T], bc(IDENT, 1, [P, GH, P]), ALU.add).then_inc(s["ti_init"], 1)
                elif kind == "kq":
                    full(dve, *job)
                    dve.wait_ge(s["dmask_done"], 2 * T + 2)
                    release(v.tensor_tensor(DU[:, T], heads(b, GH), DU[:, T], ALU.mult), *job)
                elif kind == "at":
                    evacuated(dve, *job)
                    link(v.tensor_tensor(TT[:, T], AT_[:, T], bc(const("nm0t"), 1, [P, GH, P]), ALU.mult))
                    v.tensor_tensor(TT[:, T], TT[:, T], bc(IDENT, 1, [P, GH, P]), ALU.add).then_inc(s["tt_init"], 1)
                elif kind == "ktok":
                    full(dve, *job)
                    v.tensor_tensor(KBG[:, T], heads(b, GH), bc(bg[:, T], 2, [P, GH, P]), ALU.mult)
                    release(v.tensor_tensor(KD[:, T], heads(b, GH), bc(egs[:, T, 4:8], 2, [P, GH, P]), ALU.mult), *job)
                    rotate(T)
                elif kind == "vtok":
                    full(dve, *job)
                    release(v.tensor_tensor(VB[:, T], heads(b, GH), bc(SG[:, T, 24:28], 2, [P, GH, P]), ALU.mult), *job)
                elif kind == "kt":
                    full(dve, *job)
                    dve.wait_ge(s["qd_ready"], NT)
                    pmv = const("pm")
                    for br in range(2):
                        o = KZ[:, br, :, :, T * P:(T + 1) * P]
                        i0 = bc(b[:, br * 256:br * 256 + 256].rearrange("p (g t) -> p g t", g=2), 2, [P, 2, 2, P])
                        ins = v.tensor_tensor(o, i0, pmv.unsqueeze(1).unsqueeze(3).to_broadcast([P, 2, 2, P]), ALU.mult)
                    release(ins, *job)
                    if T == 1:
                        for t in range(NT):
                            evacuated(dve, "kvct", t)
                        link(v.memset(YB[:, :, :, :, NCMP:NC16], 0.0))
                        pos = param("pos").rearrange("p (k m) -> p k m", k=2)
                        for kv in range(2):
                            for g in range(GROUPS):
                                for r in range(2):
                                    pr = slice(64 * r, 64 * r + 64)
                                    base = X2[pr, 2 * kv + g, r:r + 1]
                                    src = bass.AP(base.tensor, base.offset,
                                                  [list(base.ap[0]), [2, 16], [CMP_STRIDE, NCMP]])
                                    last = v.tensor_tensor(YB[pr, kv, :, g, 0:NCMP], src,
                                                           bc(pos[pr, kv], 2, [64, 16, NCMP]), ALU.add)
                            last.then_inc(s["y_ready"], 1)
                elif kind in ("pa", "pb"):
                    m = TI if kind == "pa" else TT
                    full(dve, *job)
                    release(v.tensor_tensor(m[:, T], m[:, T], heads(b, GH), ALU.subtract), *job)
                elif kind == "u":
                    if T == 0:
                        for t in range(NT):
                            evacuated(dve, "pb", LEVELS - 1, t)
                        v.memset(OG[0:64, 0], 0.0).then_inc(s["og_zero"], 1)
                elif kind == "kv":
                    c = a[0]
                    full(dve, *job)
                    for h in range(GH):
                        if c == 0:
                            ins = v.tensor_copy(STATE[:, h], b[:, h * P:(h + 1) * P])
                        else:
                            ins = v.scalar_tensor_tensor(STATE[:, h], STATE[:, h], gls[:, c // 2, c % 2, h:h + 1],
                                                         b[:, h * P:(h + 1) * P], ALU.mult, ALU.add)
                    release(ins, *job)
                elif kind == "vn":
                    c = a[0]
                    r = slice(64 * (c % 2), 64 * (c % 2) + 64)
                    full(dve, *job)
                    evacuated(dve, "u", c // 2)
                    release(v.tensor_tensor(U[r, c // 2], U[r, c // 2], heads(b[r, :], GH), ALU.subtract), *job)
                elif kind == "o2":
                    full(dve, *job)
                    evacuated(dve, "o1", 2 * T + 1)
                    if T == 1:
                        evacuated(dve, "o1", 2)
                    release(v.tensor_tensor(OG[:, T], OG[:, T], heads(b, GH), ALU.add), *job)
                    evacuated(dve, *job)
                    sq = TMP[:, 512:1024].rearrange("p (h n) -> p h n", h=GH)
                    link(v.tensor_tensor(sq, OG[:, T], OG[:, T], ALU.mult))
                    link(v.tensor_reduce(gr[:, T], sq, AX.X, ALU.add))
                    v.tensor_scalar(gr[:, T], gr[:, T], 1.0 / GD, EPS, ALU.mult, ALU.add).then_inc(s["og_mean"], 1)
                    dve.wait_ge(s["og_rstd"], T + 1)
                    link(v.tensor_tensor(sq, OG[:, T], bc(gr[:, T], 2, [P, GH, GD]), ALU.mult))
                    link(v.tensor_tensor(sq, sq, bc(param("outg"), 1, [P, GH, GD]), ALU.mult))
                    v.tensor_tensor(OC[:, T, 512:1024].rearrange("p (h n) -> p h n", h=GH), sq, heads(Z[:, T], GH), ALU.mult)\
                        .then_inc(s["oc_gdn"], 1)
                elif kind == "c2k":
                    k = KC[0:32, :]
                    full(dve, *job)
                    release(v.tensor_copy(k, b[0:32, 0:DH]), *job)
                    evacuated(dve, *job)
                    k2 = KC3[0:32, :]
                    link(v.tensor_tensor(k2, k, k, ALU.mult))
                    link(v.tensor_reduce(kcs[0:32, :], k2, AX.X, ALU.add))
                    v.tensor_scalar(kcs[0:32, :], kcs[0:32, :], 1.0 / DH, EPS, ALU.mult, ALU.add).then_inc(s["kc_mean"], 1)
                    dve.wait_ge(s["kc_rstd"], 1)
                    link(v.scalar_tensor_tensor(k, k, kcs[0:32, :], param("kg0")[0:32, :], ALU.mult, ALU.mult))
                    hd = DH // 2
                    sin = const("sinc")[0:32, :]
                    q = TMP2[0:32, 0:DH]
                    v.tensor_tensor(k2, k, const("cosc")[0:32, :], ALU.mult)
                    v.tensor_tensor(q[:, 0:hd], k[:, hd:DH], sin[:, 0:hd], ALU.mult)
                    link(v.tensor_tensor(q[:, hd:DH], k[:, 0:hd], sin[:, hd:DH], ALU.mult))
                    v.tensor_tensor(KC2[0:32, :].rearrange("p (r d) -> p r d", r=2), bc(k2, 1, [32, 2, DH]),
                                    bc(q, 1, [32, 2, DH]), ALU.add).then_inc(s["kcr_ready"], 1)
                elif kind == "kct":
                    full(dve, *job)
                    i0 = bc(b[:, 0:32].rearrange("p (g n) -> p g n", g=2), 2, [P, 2, 2, NC16])
                    release(v.tensor_tensor(KCBD, i0, const("pm").unsqueeze(1).unsqueeze(3).to_broadcast([P, 2, 2, NC16]),
                                            ALU.mult), *job)
                    evacuated(dve, *job)
                elif kind == "c2v":
                    full(dve, *job)
                    release(v.tensor_tensor(VBD, bc(b[:, 0:DH], 1, [P, HEADS, DH]), bc(const("hm"), 2, [P, HEADS, DH]),
                                            ALU.mult), *job)
                    evacuated(dve, *job)
                elif kind == "sc":
                    pc = PC[T].rearrange("p (h n) -> p h n", h=HEADS)
                    cneg = const("cneg").rearrange("p (t n) -> p t n", t=NT)[:, T]
                    full(dve, *job)
                    release(v.tensor_tensor(pc, b[:, 0:P].rearrange("p (h n) -> p h n", h=HEADS),
                                            bc(cneg, 1, [P, HEADS, NC16]), ALU.add), *job)
                    evacuated(dve, *job)
                    link(v.tensor_reduce(mx, pc, AX.X, ALU.max))
                    v.tensor_tensor(pc, pc, bc(mx, 2, [P, HEADS, NC16]), ALU.subtract).then_inc(s["scm_ready"], 1)
                    dve.wait_ge(s["pc_ready"], T + 1)
                    link(v.tensor_reduce(cs[T], pc, AX.X, ALU.add))
                    link(v.reciprocal(cs[T], cs[T]))
                    gate = SG[:, T, 0:24].rearrange("p (h b) -> p h b", b=3)[:, :, 0]
                    link(v.scalar_tensor_tensor(rc[T], cs[T], const("any")[:, T:T + 1], gate, ALU.mult, ALU.mult))
                elif kind == "oc":
                    full(dve, *job)
                    dve.wait_ge(s["xr_ready"], 4)
                    for t in range(NT):
                        evacuated(dve, "qt", t)
                        full(dve, "kt", t)
                        full(dve, "kvct", t)
                    release(v.tensor_tensor(OC[:, T, 0:512].rearrange("p (h d) -> p h d", d=DH),
                                            b.rearrange("p (h d) -> p h d", d=DH), bc(rc[T], 2, [P, HEADS, DH]), ALU.mult),
                            *job)
                elif kind == "s":
                    u = a[0]
                    t, br, h0, nh = UNITS[u]
                    nk = (t + 1) * P
                    full(dve, *job)
                    if u >= 3:
                        full(dve, "pt", u - 3)
                    if u == 2:
                        full(dve, "zp", 1)
                    sm = SM[u % 3].rearrange("p (h k) -> p h k", h=nh)
                    neg = const("negc").rearrange("p (t k) -> p t k", t=NT)[:, t, 0:nk]
                    release(v.tensor_tensor(sm, b.rearrange("p (h k) -> p h k", h=nh), bc(neg, 1, [P, nh, nk]), ALU.add), *job)
                    evacuated(dve, *job)
                    link(v.tensor_reduce(mx[:, 0:nh], sm, AX.X, ALU.max))
                    v.tensor_scalar(nm[u % 3][:, 0:nh], mx[:, 0:nh], -DH ** -0.5, None, ALU.mult).then_inc(s["sm_ready"], 1)
                elif kind == "o":
                    u = a[0]
                    t, br, h0, nh = UNITS[u]
                    dve.wait_ge(s["p_ready"], u + 1)
                    link(v.reciprocal(rr[:, u, 0:nh], rs[:, u, 0:nh]))
                    gate = SG[:, t, 0:24].rearrange("p (h b) -> p h b", b=3)[:, h0:h0 + nh, 1 + br]
                    link(v.tensor_tensor(rr[:, u, 0:nh], rr[:, u, 0:nh], gate, ALU.mult))
                    full(dve, *job)
                    tmp = TMP[:, 0:nh * DH].rearrange("p (h d) -> p h d", d=DH)
                    release(v.tensor_tensor(tmp, b[:, 0:nh * DH].rearrange("p (h d) -> p h d", d=DH),
                                            bc(rr[:, u, 0:nh], 2, [P, nh, DH]), ALU.mult), *job)
                    evacuated(dve, *job)
                    o = OC[:, t, h0 * DH:(h0 + nh) * DH]
                    v.tensor_tensor(o, o, TMP[:, 0:nh * DH], ALU.add).then_inc(s["oc_nsa"], 1)
                elif kind == "y":
                    t, hf = a
                    full(dve, *job)
                    dve.wait_ge(x_in, 16)
                    xv = X[:, t, hf * 512:(hf + 1) * 512]
                    release(v.tensor_tensor(xv, xv, b, ALU.add), *job)
                    evacuated(dve, *job)
                    if (t, hf) in ((0, 1), (1, 0)):
                        query_rest(v, dve, t, 0, DC // 2).then_inc(query_lo_dve, 1)
                    if hf == 1:
                        dve.wait_ge(s["x1_sq"], 2 * t + 2)
                        link(v.tensor_tensor(xs[:, t:t + 1], xss[:, t, 0:1], xss[:, t, 1:2], ALU.add))
                        v.tensor_scalar(xs[:, t:t + 1], xs[:, t:t + 1], 1.0 / D, EPS, ALU.mult, ALU.add)\
                            .then_inc(s["x1_mean"], 1)
                        dve.wait_ge(s["x1_rstd"], t + 1)
                        v.tensor_scalar(XNORM[:, t], X[:, t], xs[:, t:t + 1], None, ALU.mult).then_inc(s["xn_ready"], 1)
                elif kind == "xt":
                    full(dve, *job)
                    dve.wait_ge(subk_in, 32)
                    gain = bc(FFNG[:, 4 * a[1]:4 * a[1] + 4], 2, [P, 4, P])
                    release(v.tensor_tensor(tile4(H2T, *a), b.rearrange("p (c n) -> p c n", c=4), gain, ALU.mult), *job)
                    if a[1] == 1:
                        for hf in range(2):
                            dve.wait_ge(h2h_ready, 2 * a[0] + hf + 1)
                            v.tensor_tensor(tile4(H2L, a[0], hf), tile4(H2T, a[0], hf), tile4(H2H, a[0], hf).bitcast(F32),
                                            ALU.subtract).then_inc(h2l_ready, 1)
                elif kind == "sk":
                    full(dve, *job)
                    t, k = a
                    o = t * 16 * NKEYS + k * 512
                    release(v.tensor_copy(SCORES[:, o:o + 512], b), *job)
                elif kind == "q" and a[0] >= 2:
                    query_rest(v, dve, a[0], 0, DC // 2).then_inc(query_lo_dve, 1)

            v.memset(ONES[:, :], 1.0).then_inc(s["ones_ready"], 1)
            v.memset(EPSC, EPS).then_inc(s["ones_ready"], 1)
            for c in range(DC):
                if c % 4 == 0:
                    dve.wait_ge(xt_in[0], 16)
                    if c:
                        dve.wait_ge(xt_in[1], 16)
                v.tensor_scalar(HT[:, c], XT[:, c], XG[:, c:c + 1], None, ALU.mult).then_inc(s["hT_ready"], 1)
            for job in JOBS:
                run(job)

            marked, carried = [0], [0]

            def topk(m, k):

                def mark(ins):
                    marked[0] += 1
                    ins.then_inc(topk_link, 1)

                def carry():
                    v.memset(CARRIER[:, carried[0] % 4:carried[0] % 4 + 1], 0.0)
                    carried[0] += 1

                def hold(by_carry=True):
                    dve.wait_ge(topk_link, TOPK_LINKS * m + marked[0])
                    if by_carry:
                        carry()

                first = isinstance(m, int) and m == 0
                if k == 0:
                    marked[0] = 0
                    mark(v.tensor_copy(KS, view(GATED, TOPT + 16 * S + m * 2 * NKEYS, (NKEYS, 2), (1, NKEYS))))
                    hold()
                    for f in range(2):
                        ins = v.max(KV_[:, f, 0:8], KS[:, f])
                    mark(ins)
                    hold()
                    for f in range(2):
                        v.max_index(KI[:, f, 0:8], KV_[:, f, 0:8], KS[:, f])
                    for f in range(2):
                        ins = v.match_replace(KS[:, f], KV_[:, f, 0:8], KS[:, f], LOWEST)
                    mark(ins)
                elif k == 1:
                    hold()
                    for f in range(2):
                        ins = v.max(KV_[:, f, 8:16], KS[:, f])
                    ins.then_inc(keys_ready, 1)
                    if not first:
                        compare()
                    dve.wait_ge(keys_ready, m + 1)
                    carry()
                    for f in range(2):
                        ins = v.max_index(KI[:, f, 8:16], KV_[:, f, 8:16], KS[:, f])
                    mark(ins)
                elif k == 2:
                    dve.wait_ge(cand_ready, m + 1)
                    carry()
                    mark(v.max(RES[:, 0:8], CAND))
                    hold()
                    v.max_index(POS[:, 0:8], RES[:, 0:8], CAND)
                    mark(v.match_replace(CAND, RES[:, 0:8], CAND, LOWEST))
                else:
                    hold()
                    mark(v.max(RES[:, 8:16], CAND))
                    if not first:
                        collect(m - 1)
                    hold()
                    mark(v.max_index(POS[:, 8:16], RES[:, 8:16], CAND))
                    v.tensor_copy(KIF, KI)
                    hold(by_carry=False)
                    v.tensor_scalar(POSU[:, 0], POS, 4, None, ALU.logical_shift_right)
                    mark(v.tensor_scalar(POSU[:, 1], POS, TOPK - 1, None, ALU.bitwise_and))
                    v.tensor_copy(view(ROUTE, 2 * S + m * TOPK, (1, TOPK)), RES)
                    hold(by_carry=False)
                    mark(v.tensor_copy(POSF, POSU))
                    assert marked[0] == TOPK_LINKS

            def compare():
                shape = [P, 2 * TOPK, TOPK]
                v.tensor_tensor(EQ.rearrange("p f k a -> p (f k) a"), bc(IOTA[:, 0:TOPK], 1, shape),
                                bc(POSF.rearrange("p f k -> p (f k)"), 2, shape), ALU.is_equal).then_inc(places_ready, 1)

            def collect(m):
                dve.wait_ge(placed, m + 1)
                return v.tensor_reduce(view(ROUTE, m * TOPK, (S, 2), (1, TOPK)), EQ, AX.X, ALU.add)

            def multiply(ph, m, bk):
                g = m + Q * (ph - 1)
                dve.wait_ge(gate_mm, 4 * g + 2 * bk + 2)
                o = view(GATED, (ph - 1) * 64 * S + m * 16 + 8 * bk, (S, 64), (1, 8))
                v.tensor_tensor(o, o, PS[:, G_BANK + bk, :].rearrange("p (t i) -> p i t", i=64), ALU.mult).then_inc(gated, 1)

            def onehots(ph, m, k):
                g = m + Q * (ph - 1)
                lo = (ph - 1) * 64
                wait(dve, onehot_ready, 4 * g + k)
                if k == 0:
                    v.tensor_copy(TOK, view(ROUTE_T, m * 16, (S, 2 + PARTS), (1, 16))).then_inc(tok_ready, 1)
                    dve.wait_ge(tok_ready, g + 1)
                wait(dve, gate_mm, 4 * g + k - 1)
                q, t = 4 * k % OH_TOKENS, slice(4 * k, 4 * k + 4)
                shape = [P, 4, 64]
                v.tensor_tensor(EQ1, bc(IOTA[:, lo:lo + 64], 1, shape), bc(TOK[:, 0, t], 2, shape), ALU.is_equal)\
                    .then_inc(eq1_ready, 1)
                shape = [P, 4, P]
                v.tensor_tensor(ONEHOT2[:, q:q + 4], bc(IOTA, 1, shape), bc(TOK[:, 1, t], 2, shape), ALU.is_equal)
                dve.wait_ge(eq1_ready, 4 * g + k + 1)
                shape = [P, 4, PARTS, 64]
                last = v.tensor_tensor(ONEHOT1[:, q:q + 4], bc(EQ1, 2, shape),
                                       bc(TOK[:, 2:2 + PARTS, t].rearrange("p c q -> p q c"), 3, shape), ALU.mult)
                last.then_inc(onehot_ready, 1)

            def step(ph, m):
                for k in range(RSLOTS):
                    b = 4 * m + 4 * Q * ph + k
                    dve.wait_ge(tab_hi, 2 * b + 2)
                    table_rest(v, k, 0, SPLIT[ph]).then_inc(tab_lo_dve, 1)
                    if ph == 3:
                        dve.wait_ge(coef_hi, b - NBLK + 1)
                        coef_rest(v, b, k).then_inc(coef_lo_dve, 1)
                    if ph == 0:
                        topk(m, k)
                    elif ph < 3:
                        if k == 0 and not (isinstance(m, int) and m == 0):
                            multiply(ph, m - 1, 1)
                        elif k == 2:
                            if isinstance(m, int) and m == 0:
                                dve.wait_ge(gelu_done, NBLK // 2 * ph)
                            multiply(ph, m, 0)
                        if k < 3:
                            onehots(ph, m, k + 1)
                        elif not (isinstance(m, int) and m == Q - 1):
                            onehots(ph, m + 1, 0)
                        elif ph == 1:
                            onehots(2, 0, 0)

            def finish(ph):
                if ph in (1, 2):
                    multiply(ph, Q - 1, 1)
                if ph == 0:
                    dve.wait_ge(topk_link, TOPK_LINKS * Q)
                    compare()
                    link(collect(Q - 1))
                    gv = ROUTE[:, 2 * S:3 * S].rearrange("p (u k) -> p u k", k=TOPK)
                    shape = [P, 2 * PH, TOPK]
                    link(v.tensor_copy(GSUM, gv[:, :, 0]))
                    v.tensor_tensor(gv, gv, bc(GSUM, 2, shape), ALU.subtract).then_inc(route_exp_in, 1)
                    dve.wait_ge(route_exp, 1)
                    link(v.tensor_reduce(GSUM, gv, AX.X, ALU.add))
                    link(v.reciprocal(GSUM, GSUM))
                    v.tensor_tensor(gv, gv, bc(GSUM, 2, shape), ALU.mult).then_inc(route_ready, 1)
                    dve.wait_ge(route_t_in, 1)
                    v.tensor_copy(ROUTE_T[:, 0:2 * S], PS[:, G_BANK, :])
                    link(v.tensor_copy(GREST, PS[:, G_BANK + 1, 0:S]))
                    for c in range(PARTS):
                        part = ROUTE_T[:, (2 + c) * S:(3 + c) * S]
                        link(v.tensor_copy(GPART[:, :], GREST))
                        link(v.tensor_copy(part, GPART[:, :]))
                        if c < PARTS - 1:
                            link(v.tensor_tensor(GREST, GREST, part, ALU.subtract))
                    onehots(1, 0, 0)

            for t in range(NT):
                for k in range(4):
                    evacuated(dve, "sk", t, k)
            phases(dve, step, finish)
            dve.wait_ge(blocks_done, 2 * NBLK)
            for t in range(NT):
                for hf in range(2):
                    xv = X[:, t, hf * 512:(hf + 1) * 512]
                    v.tensor_tensor(xv, xv, PS[:, 2 * t + hf, :], ALU.add).then_inc(out_ready, 1)

    return


def prepare(inputs):
    i = {k: np.asarray(v) for k, v in inputs.items()}
    x = i["x"][0]
    w_in = i["w_in"][0]
    kv0 = HEADS * DH

    def kvcols(n):
        return w_in[:, kv0 + n * 128:kv0 + (n + 1) * 128]

    g0 = kv0 + 6 * 128
    qkv0 = g0 + 3 * HEADS
    z0 = qkv0 + 3 * GW
    a0 = z0 + GW

    def rows(a):
        return np.ascontiguousarray(a.reshape(-1, P, a.shape[1]).transpose(1, 0, 2).reshape(P, -1))

    misc = np.concatenate([kvcols(3), kvcols(5), w_in[:, g0:qkv0], w_in[:, a0 + GH:a0 + 2 * GH], w_in[:, a0:a0 + GH]], 1)
    slots = [w_in[:, qkv0 + j * 512:qkv0 + (j + 1) * 512] for j in range(3)]
    slots += [w_in[:, 0:512], np.concatenate([kvcols(2), kvcols(4), kvcols(0), kvcols(1)], 1), w_in[:, z0:z0 + 512]]
    slots = [rows(a) for a in slots]
    slots += [rows(i["cmp_w1"][0, j]) for j in range(2)]
    slots += [rows(i["w_out"][0][:, j * 512:(j + 1) * 512]) for j in range(2)]
    slots += [rows(i["peer_w_query"][0][:, j * 512:(j + 1) * 512]) for j in range(4)]
    par = np.zeros((P, NPARAM), np.float32)

    def put(name, a):
        lo, hi = PARAM[name]
        par[:, lo:hi] = a

    kg = i["nsa_k_gain"][0]
    put("gains", np.concatenate([np.tile(i["nsa_q_gain"][0], 8), np.tile(kg[1], 2), np.tile(kg[2], 2)])[None])
    put("kg0", kg[0][None])
    put("outg", i["gdn_out_gain"][0][None])
    put("alog", i["gdn_a_log"][0][None])
    put("dtb", i["gdn_dt_bias"][0][None])
    put("conv", i["gdn_conv"][0].reshape(CONV_K, 12, P).transpose(2, 1, 0).reshape(P, -1))
    put("pos", i["cmp_pos"][0].reshape(2, 16, 2, DH).transpose(2, 3, 0, 1).reshape(P, -1))
    put("w2", i["cmp_w2"][0].reshape(2, 2, P, DH).transpose(2, 0, 1, 3).reshape(P, -1))
    return {
        "consts": constants(), "keep": keep_constants(), "params": par,
        "ffng": np.ascontiguousarray(i["ffn_norm"][0].reshape(DC, P).T),
        "xt": np.concatenate([i["attn_norm"][0].reshape(DC, P).T, rows(np.ascontiguousarray(x.T))], 1), "x": rows(x), "wmisc": rows(misc), "wslots": np.stack(slots),
        "u": np.ascontiguousarray(i["peer_u"][0].reshape(NKEYS, NKEYS, DC, P).transpose(0, 3, 2, 1)).reshape(NKEYS, P, D),
        "v": i["peer_v"][0].reshape(NKEYS, NKEYS, D),
        "subk": np.ascontiguousarray(i["peer_subkeys"][0].transpose(2, 0, 1).reshape(P, -1)),
    }




def kernel(**inputs):
    import concourse.bacc as bacc
    from concourse.bass_utils import run_bass_kernel_spmd

    arrays = prepare(inputs)
    nc = bacc.Bacc("TRN2", target_bir_lowering=False, num_devices=1)
    d = {n: nc.dram_tensor("in_" + n, a.shape, F32, kind="ExternalInput").ap() for n, a in arrays.items()}
    out = nc.dram_tensor("out", (P, NT * D), F32, kind="ExternalOutput").ap()
    build(nc, d, out)
    r = run_bass_kernel_spmd(nc, [{"in_" + n: a for n, a in arrays.items()}], core_ids=[0])
    y = r.results[0]["out"]
    return y.reshape(P, NT, D).transpose(1, 0, 2).reshape(1, S, D)
```

```python
import math

import numpy as np
import concourse.bass as bass
from concourse import mybir
from concourse.alu_op_type import AluOpType as ALU
from contextlib import ExitStack

F32 = mybir.dt.float32
F32R = mybir.dt.float32r
U32 = mybir.dt.uint32
BF16 = mybir.dt.bfloat16
ACT = mybir.ActivationFunctionType
AX = mybir.AxisListType

P = 128
D, S = 1024, 256
DC = D // P
NT = S // P
HEADS, GROUPS, DH = 8, 2, 64
CMP_BLK, CMP_STRIDE = 32, 16
NCMP = S // CMP_STRIDE - CMP_BLK // CMP_STRIDE + 1
NC16 = 16
THETA = 10000.0
GH, GD, CONV_K, CHUNK = 4, 128, 4, 64
GW = GH * GD
PH, TOPK, NKEYS = 8, 16, 128
NEG = -1e30
LOWEST = -3.0e38
EPS = 1e-6
SLOT = DC * 512
MISC = 2 * GROUPS * DH + 3 * HEADS + 2 * GH
LEVELS = 6

CONST = {}


def _layout(table, widths):
    at = 0
    for name, n in widths:
        table[name] = (at, at + n)
        at += n
    return at


NCONST = _layout(CONST, [("upper", P), ("nlower", P), ("strict", P), ("nm0", P), ("nm0t", P)]
                 + [(f"mt{l}", P) for l in range(1, LEVELS)]
                 + [("negc", NT * S), ("cneg", NT * NC16), ("any", NT), ("cos", NT * DH), ("sin", NT * DH),
                    ("cosc", DH), ("sinc", DH), ("pm", 2), ("hm", HEADS)])
PARAM = {}
NPARAM = _layout(PARAM, [("gains", 12 * DH), ("kg0", DH), ("outg", GD), ("alog", GH), ("dtb", GH),
                         ("conv", 12 * CONV_K), ("pos", 2 * CMP_BLK // 2), ("w2", 2 * 2 * DH)])


def constants():
    c = np.zeros((P, NCONST), np.float32)

    def put(name, a):
        lo, hi = CONST[name]
        c[:a.shape[0], lo:hi] = a.reshape(a.shape[0], -1)

    p, x = np.arange(P)[:, None], np.arange(P)[None, :]
    same = p // CHUNK == x // CHUNK
    put("upper", (p <= x) & same)
    put("nlower", -1.0 * ((p >= x) & same))
    put("strict", (p > x) & same)
    for l in range(LEVELS):
        s = 1 << l
        m = (p // (2 * s) == x // (2 * s)) & (p // s % 2 == 1) & (x // s % 2 == 0)
        if l == 0:
            put("nm0", -1.0 * m)
            put("nm0t", -1.0 * m.T)
        else:
            put(f"mt{l}", m.T)
    t = np.arange(S).reshape(NT, P)
    put("negc", np.where(np.arange(S)[None, None, :] <= t.T[:, :, None], 0.0, NEG))
    n = np.arange(NC16)
    ends = n * CMP_STRIDE + CMP_BLK - 1
    seen = (ends[None, None, :] <= t.T[:, :, None]) & (n < NCMP)[None, None, :]
    put("cneg", np.where(seen, 0.0, NEG))
    put("any", seen.any(-1))
    half = DH // 2
    inv = np.exp(np.float32(-math.log(THETA) * 2.0) * np.arange(half, dtype=np.float32) / np.float32(DH)).astype(np.float32)

    def rope(pos):
        a = pos.astype(np.float32)[..., None] * inv
        return np.concatenate([np.cos(a)] * 2, -1), np.concatenate([-np.sin(a), np.sin(a)], -1)

    cos, sin = rope(t.T)
    put("cos", cos)
    put("sin", sin)
    cos, sin = rope(np.concatenate([ends, ends]))
    put("cosc", cos)
    put("sinc", sin)
    put("pm", p // 64 == np.arange(2)[None, :])
    put("hm", p // NC16 == np.arange(HEADS)[None, :])
    return c


def keep_constants():
    c = np.zeros((P, 2 * P), np.float32)
    c[:, :P] = np.eye(P)
    c[:, P:] = np.arange(P)[None, :]
    return c


def units():
    out = [(0, br, h, 4) for br in range(2) for h in (0, 4)]
    return out + [(1, br, h, 2) for br in range(2) for h in range(0, 8, 2)]


UNITS = units()


def job_list():
    jobs = [("misc", 0), ("ssq",), ("misc", 1), ("rrow",), ("qkv", 0), ("qkv", 1), ("gcol",), ("qkv", 2), ("l2", 0),
            ("qkv", 3), ("l2", 1), ("qkv", 4), ("l2", 2), ("l2", 3), ("qkv", 5), ("qp", 0), ("qp", 1), ("l2b", 0),
            ("l2b", 1), ("l2b", 2), ("l2b", 3), ("gb", 0), ("gb", 1), ("kvp", 0), ("kvp", 1), ("kk", 0), ("kk", 1),
            ("zp", 0), ("zp", 1), ("at", 0), ("at", 1), ("kq", 0), ("kq", 1), ("ktok", 0), ("ktok", 1), ("vtok", 0),
            ("vtok", 1)]
    gdn = []
    for l in range(1, LEVELS):
        last = l == LEVELS - 1
        gdn += [[("w", l, 0), ("w", l, 1)], [(p, l, T) for T in range(NT) for p in ("pa", "pb") if not (last and p == "pa")]]
    gdn += [[("u", 0), ("wt", 0), ("u", 1), ("wt", 1)], [("kv", 0)]]
    for c in range(1, 4):
        gdn += [[("vn", c)], [("o1", c)] + ([("kv", c)] if c < 3 else [])]
        if c % 2:
            gdn[-1] += [("o2", c // 2)]
    nsa = [("kvct", 0), ("kvct", 1), ("qt", 0), ("kt", 0), ("qt", 1), ("kt", 1)]
    nsa += [("s", 0), ("s", 1), ("h1", 0), ("h1", 1), ("c2k",), ("c2v",), ("kct",), ("s", 2), ("sc", 0), ("sc", 1)]
    tail = []
    for u in range(len(UNITS) + 2):
        if u >= 2:
            tail.append(("o", u - 2))
        if u < len(UNITS):
            tail.append(("pt", u))
        if u + 3 < len(UNITS):
            tail.append(("s", u + 3))
        if u == 0:
            tail += [("pct", 0), ("pct", 1)]
        if u == 1:
            tail += [("oc", 0), ("oc", 1)]
    nsa += tail
    at = 0
    for i, g in enumerate(gdn):
        jobs += g
        until = len(nsa) * (i + 1) // len(gdn)
        jobs += nsa[at:until]
        at = until
    i = jobs.index(("o", 9))
    jobs[i:i] = [("ot", 0, 0), ("ot", 0, 1), ("y", 0, 0)]
    jobs += [("y", 0, 1), ("ot", 1, 0), ("ot", 1, 1)]
    jobs += [("y", 1, 0), ("xt", 0, 0), ("xt", 0, 1), ("y", 1, 1), ("xt", 1, 0), ("xt", 1, 1)]
    jobs += [("q", b) for b in range(2 * PH)]
    jobs += [("sk", T, b) for T in range(NT) for b in range(4)]
    return jobs


JOBS = job_list()
JOB = {j: n for n, j in enumerate(JOBS)}
BANKS = 8
TOPK_LINKS = 10
PARTS = 3
OH_TOKENS = 8
RSLOTS = 4
NBLK = NKEYS
Q = NBLK // 2 // RSLOTS
SPLIT = (512, 384, 384, 512)
G_BANK, A_BANK = 4, 6
SLOTS = 3
ROW_LOADS = (("qp", 4), ("kvp", 5), ("zp", 6))
ROTATE_AT = (("vtok", 1), ("pb", 1, 1))
QKV_BUFS = 3
LOADS = [("misc", 1), ("qkv", 1), ("qkv", 3), ("qkv", 5), ("qp", 1), ("kvp", 1), ("zp", 1), ("h1", 0), ("h1", 1),
         ("y", 1, 0), ("y", 1, 1), ("q", 3), ("q", 7), ("q", 11), ("q", 15)]


def build(nc, dram, out_d):
    consts_d, keep_d, params_d, ffng_d, xt_d, x_d, wmisc_d, wslots_d, subk_d, u_d, v_d = (
        dram[n] for n in ("consts", "keep", "params", "ffng", "xt", "x", "wmisc", "wslots", "subk", "u", "v"))
    ctx = ExitStack()
    with ctx:
        def sem(name):
            return ctx.enter_context(nc.semaphore(name))

        def sb(name, cols, dt=F32, where=None, parts=P):
            return (where or ctx).enter_context(nc.sbuf_tensor(name, [parts, cols], dt))

        X_ALL = sb("X", NT * D)
        X = X_ALL[:, :].rearrange("p (t d) -> p t d", t=NT)
        KEEP = sb("KEEP", 2 * P)
        IDENT, IOTA = KEEP[:, 0:P], KEEP[:, P:2 * P]
        FFNG = sb("FFNG", DC)[:, :]
        MHALF = sb("MHALF", 1)[:, :]
        SUBK = sb("SUBK", 2 * P)[:, :].rearrange("p (h n) -> p h n", h=2)
        PS = ctx.enter_context(nc.psum_tensor("PS", [P, BANKS, 512], F32))

        early = ExitStack()
        W = sb("W", SLOTS * SLOT + 4 * D, where=early)
        ONES = sb("ONES", P, where=early)
        F_COLS = 34000
        FB = sb("FB", F_COLS, where=early)
        top = [0]

        def take(n, at=None):
            lo = top[0] if at is None else at
            if at is None:
                top[0] += -(-n // 8) * 8
                assert top[0] <= F_COLS, top[0]
            return FB[:, lo:lo + n]

        early.close()

        C = take(NCONST)
        PR = take(NPARAM)

        def const(name):
            return C[:, CONST[name][0]:CONST[name][1]]

        def param(name):
            return PR[:, PARAM[name][0]:PARAM[name][1]]

        XT_AT = top[0]
        XG = take(DC + DC * S)
        XT = XG[:, DC:].rearrange("p (c t) -> p c t", c=DC)
        HT = take(DC * S).rearrange("p (c t) -> p c t", c=DC)
        QP_AT = top[0]
        QPW = S + 4
        QP = take(12 * QPW).rearrange("p (b t) -> p b t", b=12)
        CV_AT = top[0]
        CV = take(12 * S).rearrange("p (b t) -> p b t", b=12)
        RN_AT = top[0]
        take(8 * S)
        OC_AT = top[0]
        XR = take(NT * 8 * DH).rearrange("p (t h d) -> p t h d", t=NT, d=DH)
        KR = take(NT * 4 * 2 * DH).rearrange("p (t h r d) -> p t h r d", t=NT, r=2, d=DH)
        VSW = take(NT * 4 * DH).rearrange("p (t h d) -> p t h d", t=NT, d=DH)
        GAB = take(NT * 32).rearrange("p (t n) -> p t n", t=NT)
        SG = take(NT * 28).rearrange("p (t n) -> p t n", t=NT)
        Z = take(NT * GW).rearrange("p (t n) -> p t n", t=NT)

        def mat():
            return take(NT * GW).rearrange("p (t h n) -> p t h n", t=NT, h=GH)

        DL, DU, EG = (mat() for _ in range(3))
        SPLIT_AT = top[0]
        AM, AT_, TI, TT, KBG, KD, VB = (mat() for _ in range(7))
        FB_AT = SLOTS * SLOT + 4 * D + P

        def overlay(name, at, cols):
            with ExitStack() as place:
                sb("under_" + name, at, where=place)
                return sb(name, cols, F32R, where=place)

        HTH, HTL = overlay("HTH", FB_AT + RN_AT, DC * S), overlay("HTL", FB_AT + XT_AT + DC, DC * S)
        QKVH, QKVL = (overlay(name, FB_AT + SPLIT_AT + i * QKV_BUFS * D, QKV_BUFS * D)
                      for i, name in enumerate(("QKVH", "QKVL")))
        rowh, rowl0 = overlay("ROWH", SLOTS * SLOT, 3 * D), overlay("ROWL0", SLOTS * SLOT + 3 * D, D)
        rowl1, rowl2 = overlay("ROWL1", FB_AT + SPLIT_AT + 6 * D, D), overlay("ROWL2", FB_AT + SPLIT_AT + 4 * D, D)
        ROWH = [rowh[:, i * D:(i + 1) * D] for i in range(3)]
        ROWL = [rowl0[:, :], rowl1[:, :], rowl2[:, :]]
        STATE = take(GW).rearrange("p (h n) -> p h n", h=GH)
        RSTD = take(S)
        TMP = take(1024)
        TMP2 = take(512)
        KCBD = take(64).rearrange("p (g r n) -> p g r n", g=2, r=2)
        HK = take(64).rearrange("p (c n) -> p c n", c=2)
        HV = take(256).rearrange("p (c g m n) -> p c g m n", c=2, g=2, m=4)
        PC = [take(128) for _ in range(2)]
        KC, KC2, KC3 = take(64), take(128), take(64)
        SQ = take(8 * S, at=OC_AT).rearrange("p (b t) -> p b t", b=8)
        XN = X[:, :, 0:768].rearrange("p t (h d) -> p t h d", d=DH)
        KCV = take(NT * 4 * 2 * DH, at=QP_AT).rearrange("p (t h r d) -> p t h r d", t=NT, r=2, d=DH)
        XSQ = take(NT * 768, at=OC_AT).rearrange("p (t h d) -> p t h d", t=NT, d=DH)
        X2 = take(4 * S, at=XT_AT).rearrange("p (k t) -> p k t", k=4)
        YB = take(2 * 16 * 32, at=XT_AT + 4 * S).rearrange("p (k m g n) -> p k m g n", k=2, m=16, g=2)
        KZ = take(4 * 2 * S, at=CV_AT).rearrange("p (b g r t) -> p b g r t", b=2, g=2, r=2)
        QT = take(NT * 512, at=CV_AT + 8 * S).rearrange("p (a t) -> p a t", a=4)
        CT = [take(NT * GW, at=RN_AT + i * NT * GW).rearrange("p (t h n) -> p t h n", t=NT, h=GH) for i in range(2)]
        CT.append(take(NT * GW, at=QP_AT + NT * GW).rearrange("p (t h n) -> p t h n", t=NT, h=GH))
        SM = [take(512, at=at) for at in (QP_AT, QP_AT + 512, XT_AT + 4 * S)]
        PT = [take(512, at=QP_AT + 1024 + 512 * i).rearrange("p (b t) -> p b t", b=4) for i in range(3)]
        VBD = take(512, at=QP_AT + 2560).rearrange("p (h d) -> p h d", h=HEADS)
        OC = take(NT * D, at=OC_AT).rearrange("p (t d) -> p t d", t=NT)
        OT = take(DC * S, at=XT_AT + 2048).rearrange("p (c t) -> p c t", c=DC)
        XNORM = take(NT * D, at=RN_AT).rearrange("p (t d) -> p t d", t=NT)
        WW, U, WT, OG, QD = AM, DL, AM, TI, EG
        PCT = take(256)
        SMA = take(320)
        sm_at = [0]

        def small(n):
            lo = sm_at[0]
            sm_at[0] += n
            assert sm_at[0] <= 320
            return SMA[:, lo:lo + n]

        rs12 = small(24).rearrange("p (t n) -> p t n", t=NT)
        gcs = small(16).rearrange("p (t n) -> p t n", t=NT)
        egs = small(16).rearrange("p (t n) -> p t n", t=NT)
        gls = small(16).rearrange("p (t f n) -> p t f n", t=NT, f=2)
        bg = small(8).rearrange("p (t n) -> p t n", t=NT)
        gstep = small(8).rearrange("p (t n) -> p t n", t=NT)
        aexp = small(4)
        rcol = small(NT)
        sp1 = small(8).rearrange("p (t n) -> p t n", t=NT)
        sp2 = small(8).rearrange("p (t n) -> p t n", t=NT)
        mx = small(8)
        nm = [small(4) for _ in range(3)]
        rs = small(48).rearrange("p (u n) -> p u n", u=12)
        rr = small(48).rearrange("p (u n) -> p u n", u=12)
        cs = [small(8), small(8)]
        rc = [small(8), small(8)]
        gr = small(8).rearrange("p (t n) -> p t n", t=NT)
        xs = small(2)
        xss = small(4).rearrange("p (t n) -> p t n", t=NT)
        l2c = small(16).rearrange("p (i n) -> p i n", i=4)
        kcs = small(1)
        EPSC = small(1)

        GATED = sb("GATED", NKEYS * S)
        H2H, H2L = sb("H2H", DC * S, F32R), sb("H2L", DC * S, F32R)
        TABH, TABL = sb("TABH", 2 * D, F32R), sb("TABL", 2 * D, F32R)
        RING = sb("RING", RSLOTS * D)
        CFH, CFL = sb("CFH", 2 * S, F32R), sb("CFL", 2 * S, F32R)
        H2T = sb("H2T", DC * S)
        ROUTE = sb("ROUTE", 3 * S)
        ROUTE_T = sb("ROUTE_T", 2 * S)
        GPART = sb("GPART", PARTS * S, BF16)[:, :].rearrange("p (c t) -> p c t", c=PARTS)
        TOK = sb("TOK", 2 * 16)[:, :].rearrange("p (c q) -> p c q", c=2)
        TOKG = sb("TOKG", PARTS * 16, BF16)[:, :].rearrange("p (c q) -> p c q", c=PARTS)
        h2t_at = [0]

        def after_h2t(n):
            h2t_at[0] += n
            return H2T[:, h2t_at[0] - n:h2t_at[0]]

        ONEHOT2 = after_h2t(OH_TOKENS * P // 2).bitcast(BF16).rearrange("p (q n) -> p q n", q=OH_TOKENS)
        ONEHOT1 = after_h2t(OH_TOKENS * PARTS * 64 // 2).bitcast(BF16).rearrange("p (q c n) -> p q c n", q=OH_TOKENS, c=PARTS)
        EQ1 = after_h2t(4 * 64).rearrange("p (q n) -> p q n", q=4)
        GREST = after_h2t((PARTS - 1) * S).rearrange("p (c t) -> p c t", c=PARTS - 1)
        TOPT = 18432
        QRY = GATED[:, TOPT:TOPT + 16 * S].rearrange("p (b t) -> p b t", b=16)
        SCORES = GATED[:, TOPT + 16 * S:TOPT + 32 * S]
        kt_at = [TOPT + 32 * S]

        def ktake(n):
            kt_at[0] += n
            return GATED[:, kt_at[0] - n:kt_at[0]]

        KS = ktake(2 * NKEYS).rearrange("p (f n) -> p f n", f=2)
        KV_ = ktake(2 * TOPK).rearrange("p (f k) -> p f k", f=2)
        KI = ktake(2 * TOPK).bitcast(U32).rearrange("p (f k) -> p f k", f=2)
        KIF = ktake(2 * TOPK).rearrange("p (f k) -> p f k", f=2)
        CAND = ktake(TOPK * TOPK)
        POS = ktake(TOPK).bitcast(U32)
        POSF = ktake(2 * TOPK).rearrange("p (f k) -> p f k", f=2)
        POSU = ktake(2 * TOPK).bitcast(U32).rearrange("p (f k) -> p f k", f=2)
        EQ = ktake(2 * TOPK * TOPK).rearrange("p (f k a) -> p f k a", f=2, k=TOPK)
        RES = ktake(TOPK)
        GSUM, GEXP = ktake(2 * PH), ktake(2 * PH * TOPK)
        CARRIER = ktake(4)

        params_in, consts_in, keep_in = sem("params_in"), sem("consts_in"), sem("keep_in")
        x_in, subk_in = sem("x_in"), sem("subk_in")
        xt_in, misc_in = [[sem(f"{name}_in{i}") for i in range(2)] for name in ("xt", "misc")]
        weights_in = [sem(f"weights_in{i}") for i in range(SLOTS)]
        ps_full = sem("ps_full")
        ps_free = [sem(f"ps_free{b}") for b in range(BANKS)]
        dve_link, pool_link = sem("dve_link"), sem("pool_link")
        names = ("ones_ready hth_ready htl_ready qkv_hi qkv_lo qkv_first kbg_done bg_ready xn_gain xn_sq "
                 "row_hi row_lo row_done rcol_ready l2_ready x1_sq xsq_ready hT_ready qp_zero exp_misc_done "
                 "sig_ready softplus_in softplus_exp softplus_ln g_ready conv_ready silu_done sq_ready eg_exp "
                 "gcs_exp darg_ready dexp_done dmask_done ti_init tt_init ct_ready qd_ready og_zero og_mean "
                 "og_rstd oc_gdn xq_mean xq_rstd xr_ready y_ready kc_mean kc_rstd kcr_ready sm_ready p_ready "
                 "scm_ready pc_ready oc_nsa x1_mean x1_rstd xn_ready gls_ready").split()
        s = {n: sem(n) for n in names}

        table_in = [sem(f"table_in{k}") for k in range(RSLOTS)]
        query_hi, query_lo_dve, query_lo_pool = sem("query_hi"), sem("query_lo_dve"), sem("query_lo_pool")
        tab_hi = sem("tab_hi")
        tab_lo_dve, tab_lo_pool = sem("tab_lo_dve"), sem("tab_lo_pool")
        blocks_done = sem("blocks_done")
        gelu_done = sem("gelu_done")
        coef_hi, coef_lo_pool, coef_lo_dve = sem("coef_hi"), sem("coef_lo_pool"), sem("coef_lo_dve")
        onehot_ready, gate_mm, gated = sem("onehot_ready"), sem("gate_mm"), sem("gated")
        route_exp_in, route_exp, route_ready = sem("route_exp_in"), sem("route_exp"), sem("route_ready")
        route_t_in, route_keys = sem("route_t_in"), sem("route_keys")
        h2h_ready, h2l_ready = sem("h2h_ready"), sem("h2l_ready")
        topk_link, tok_ready = sem("topk_link"), sem("tok_ready")
        eq1_ready, keys_ready, cand_ready = sem("eq1_ready"), sem("keys_ready"), sem("cand_ready")
        places_ready, placed = sem("places_ready"), sem("placed")
        out_ready, out_done = sem("out_ready"), sem("out_done")

        def view(t, offset, *dims):
            a = t[:, 0:1] if len(t.shape) == 2 else t[:, 0, 0:1]
            return bass.AP(a.tensor, offset, [list(a.ap[0])] + [list(d) for d in dims])

        def row_piece(eng, r):
            load = ROW_LOADS[r // 4][1]
            eng.wait_ge(weights_in[load % SLOTS], 16 * (load // SLOTS + (load % SLOTS > 0)))
            return wslot(load)[:, r % 4 * D:(r % 4 + 1) * D]

        def row_buffer(eng, r):
            if r >= 3:
                kind, n = ROW_LOADS[(r - 3) // 4][0], (r - 3) % 4
                if n == 3:
                    full(eng, kind, 1)
                else:
                    eng.wait_ge(s["row_done"], 3 * ((r - 3) // 4) + n + 1)

        def qkv_weights(eng, n):
            load = 1 + n // 4
            eng.wait_ge(weights_in[load % SLOTS], 16 * (load // SLOTS + (load % SLOTS > 0)))
            return wslot(load).rearrange("p (c n) -> p c n", c=DC)[:, :, n % 4 * P:(n % 4 + 1) * P]

        def query_weights(eng, n):
            load = 11 + n // 4
            eng.wait_ge(weights_in[load % SLOTS], 16 * (load // SLOTS + (load % SLOTS > 0)))
            return wslot(load).rearrange("p (c n) -> p c n", c=DC)[:, :, n % 4 * P:(n % 4 + 1) * P]

        def query_rest(engine, eng, n, lo, hi):
            w = query_weights(eng, n)
            eng.wait_ge(query_hi, n + 1)
            if n >= 2:
                full(eng, "q", n - 2)
            h, r = (t[:, n % 2 * D:(n % 2 + 1) * D].rearrange("p (c n) -> p c n", c=DC)[:, lo:hi] for t in (TABH, TABL))
            return engine.tensor_tensor(r, w[:, lo:hi], h.bitcast(F32), ALU.subtract)

        def table_rest(engine, k, lo, hi):
            h = k % 2 * D
            return engine.tensor_tensor(TABL[:, h + lo:h + hi], RING[:, k * D + lo:k * D + hi],
                                        TABH[:, h + lo:h + hi].bitcast(F32), ALU.subtract)

        def coef_rest(engine, b, k):
            cols = slice(k % 2 * S, (k % 2 + 1) * S)
            return engine.tensor_tensor(CFL[:, cols], view(GATED, (b - NBLK) * S, (1, S)), CFH[:, cols].bitcast(F32),
                                        ALU.subtract)

        def tile4(t, tile, hf):
            return t[:, :].rearrange("p (c t) -> p c t", c=DC)[:, 4 * hf:4 * hf + 4, tile * P:(tile + 1) * P]

        def phases(eng, step, finish=None):
            for ph in range(4):
                step(ph, 0)
                with eng.Fori(1, Q - 1) as m:
                    step(ph, m)
                step(ph, Q - 1)
                if finish:
                    finish(ph)

        def wait(eng, semaphore, value):
            if not isinstance(value, int) or value > 0:
                eng.wait_ge(semaphore, value)

        def full(eng, *job):
            eng.wait_ge(ps_full, JOB[job] + 1)

        def evacuated(eng, *job):
            n = JOB[job]
            eng.wait_ge(ps_free[n % BANKS], n // BANKS + 1)

        def bank(*job):
            return PS[:, JOB[job] % BANKS, :]

        def release(ins, *job):
            ins.then_inc(ps_free[JOB[job] % BANKS], 1)

        def wslot(n):
            return W[:, (n % SLOTS) * SLOT:(n % SLOTS + 1) * SLOT]

        block = ctx.enter_context(nc.Block())

        @block.sync
        def _(sp):
            for i in range(2):
                lo, hi = ((0, DC + DC // 2 * S), (DC + DC // 2 * S, DC + DC * S))[i]
                sp.dma_start(XG[:, lo:hi], xt_d[:, lo:hi]).then_inc(xt_in[i], 16)
                cols = slice(i * (DC // 2) * MISC, (i + 1) * (DC // 2) * MISC)
                sp.dma_start(W[:, cols], wmisc_d[:, cols]).then_inc(misc_in[i], 16)
            sp.dma_start(KEEP[:, :], keep_d).then_inc(keep_in, 16)
            for n in range(1, len(LOADS)):
                if n >= SLOTS:
                    full(sp, *LOADS[n - SLOTS])
                sp.dma_start(wslot(n), wslots_d[n - 1]).then_inc(weights_in[n % SLOTS], 16)
                if n == 1:
                    sp.dma_start(PR, params_d).then_inc(params_in, 16)
                if n == 2:
                    sp.dma_start(C, consts_d).then_inc(consts_in, 16)
                if n == 6:
                    sp.dma_start(FFNG, ffng_d).then_inc(subk_in, 16)
                    sp.dma_start(SUBK.rearrange("p h n -> p (h n)"), subk_d).then_inc(subk_in, 16)
                if n == 9:
                    sp.wait_ge(s["xr_ready"], 4)
                    sp.dma_start(X.rearrange("p t d -> p (t d)"), x_d).then_inc(x_in, 16)

            def table(t_d, i, k):
                a = t_d[0]
                sp.dma_start(RING[:, k * D:(k + 1) * D], bass.AP(a.tensor, i * (P * D), [[D, P], [1, D]]))\
                    .then_inc(table_in[k], 16)

            def step(ph, m):
                for k in range(RSLOTS):
                    b = 4 * m + 4 * Q * ph + k
                    wait(sp, tab_lo_dve, b - RSLOTS + 1)
                    wait(sp, tab_lo_pool, b - RSLOTS + 1)
                    table(u_d if ph < 2 else v_d, b - (0 if ph < 2 else NBLK), k)

            sp.wait_ge(s["xn_ready"], NT)
            phases(sp, step)
            for t in range(NT):
                sp.wait_ge(out_ready, 2 * (t + 1))
                sp.dma_start(out_d[:, t * D:(t + 1) * D], X[:, t]).then_inc(out_done, 16)
            sp.wait_ge(out_done, 16 * NT)

        @block.gpsimd
        def _(pool):
            g = nc.gpsimd
            count = [0]

            def link(ins):
                count[0] += 1
                ins.then_inc(pool_link, 1)
                pool.wait_ge(pool_link, count[0])

            def power(out, in_, shape):
                e = MHALF[0:shape[0], :]
                for _ in range(len(shape) - 2):
                    e = e.unsqueeze(1)
                return g.tensor_tensor(out, in_, e.to_broadcast(shape), ALU.pow)

            link(g.memset(MHALF, -0.5))
            g.memset(QP[:, :, 0:CONV_K - 1], 0.0).then_inc(s["qp_zero"], 1)
            for n in range(12):
                w = qkv_weights(pool, n)
                pool.wait_ge(s["qkv_hi"], n + 1)
                k = n % QKV_BUFS
                h, r = (t[:, k * D:(k + 1) * D].rearrange("p (c n) -> p c n", c=DC) for t in (QKVH, QKVL))
                g.tensor_tensor(r, w, h.bitcast(F32), ALU.subtract).then_inc(s["qkv_lo"], 1)

            def rest_of_rows(*pieces):
                for r in pieces:
                    w = row_piece(pool, r)
                    pool.wait_ge(s["row_hi"], r + 1)
                    if r == 2:
                        pool.wait_ge(s["qkv_first"], 6)
                    g.tensor_tensor(ROWL[r % 3], w, ROWH[r % 3].bitcast(F32), ALU.subtract).then_inc(s["row_lo"], 1)

            rest_of_rows(*range(12))
            pool.wait_ge(params_in, 16)
            for T in range(NT):
                pool.wait_ge(s["xn_sq"], T + 1)
                g.tensor_tensor(XN[:, T], XN[:, T], param("gains").rearrange("p (h d) -> p h d", d=DH), ALU.mult)\
                    .then_inc(s["xn_gain"], 1)
            for T in range(NT):
                pool.wait_ge(s["xq_mean"], T + 1)
                power(rs12[:, T], rs12[:, T], [P, 12]).then_inc(s["xq_rstd"], 1)
            for l in range(1, LEVELS):
                for T in range(NT):
                    evacuated(pool, "at", T)
                    if l == 2:
                        full(pool, "zp", 1)
                    if l >= 3:
                        full(pool, "w", l - 2, T)
                    g.tensor_tensor(CT[l % 2 if l > 1 else 2][:, T], AT_[:, T],
                                    const(f"mt{l}").unsqueeze(1).to_broadcast([P, GH, P]), ALU.mult)\
                        .then_inc(s["ct_ready"], 1)
                if l == 1:
                    evacuated(pool, "l2b", 3)
                    pool.wait_ge(s["gls_ready"], 2 * NT)
                    for T in range(NT):
                        g.tensor_tensor(QD[:, T], EG[:, T], CV[:, 0:4, T * P:(T + 1) * P], ALU.mult).then_inc(s["qd_ready"], 1)
                if l == 2:
                    pool.wait_ge(s["kc_mean"], 1)
                    power(kcs[0:32, :], kcs[0:32, :], [32, 1]).then_inc(s["kc_rstd"], 1)
            for T in range(NT):
                pool.wait_ge(s["og_mean"], T + 1)
                power(gr[:, T], gr[:, T], [P, GH]).then_inc(s["og_rstd"], 1)
            for T in range(NT):
                if T == 1:
                    for n in range(2):
                        query_rest(g, pool, n, DC // 2, DC).then_inc(query_lo_pool, 1)
                pool.wait_ge(s["x1_mean"], T + 1)
                power(xs[:, T:T + 1], xs[:, T:T + 1], [P, 1]).then_inc(s["x1_rstd"], 1)

            for n in range(2, 2 * PH):
                query_rest(g, pool, n, DC // 2, DC).then_inc(query_lo_pool, 1)

            def step(ph, m):
                for k in range(RSLOTS):
                    b = 4 * m + 4 * Q * ph + k
                    turn = isinstance(b, int) and b == NBLK
                    if ph == 2 and not turn:
                        pool.wait_ge(coef_hi, b - NBLK + 1)
                        coef_rest(g, b, k).then_inc(coef_lo_pool, 1)
                    pool.wait_ge(tab_hi, 2 * b + 1)
                    table_rest(g, k, SPLIT[ph], D).then_inc(tab_lo_pool, 1)
                    if turn:
                        pool.wait_ge(coef_hi, b - NBLK + 1)
                        coef_rest(g, b, k).then_inc(coef_lo_pool, 1)
                    if ph == 0 and k == 2 and not (isinstance(m, int) and m == 0):
                        place(m - 1)
                    if ph == 0 and k == 1:
                        pool.wait_ge(keys_ready, m + 1)
                        shape = [P, TOPK, TOPK]
                        g.tensor_tensor(CAND.rearrange("p (a b) -> p a b", a=TOPK), KV_[:, 0].unsqueeze(2).to_broadcast(shape),
                                        KV_[:, 1].unsqueeze(1).to_broadcast(shape), ALU.add).then_inc(cand_ready, 1)

            def place(m):
                pool.wait_ge(places_ready, m + 1)
                g.tensor_tensor(EQ, EQ, KIF.unsqueeze(2).to_broadcast([P, 2, TOPK, TOPK]), ALU.mult).then_inc(placed, 1)

            phases(pool, step)

        @block.tensor
        def _(pe):
            mm = nc.tensor.matmul

            def begin(*job):
                n = JOB[job]
                if n >= BANKS:
                    pe.wait_ge(ps_free[n % BANKS], n // BANKS)
                return bank(*job)

            def end(ins):
                ins.then_inc(ps_full, 1)

            def weights(n):
                pe.wait_ge(weights_in[n % SLOTS], 16 * (n // SLOTS + (n % SLOTS > 0)))
                return wslot(n)

            def products(out, k, first=False, w=None, h=None):
                hi, lo = (t[:, k * D:(k + 1) * D] for t in w or (TABH, TABL))
                h_hi, h_lo = h or (H2H, H2L)
                for n, (w, h) in enumerate(((hi, h_hi), (lo, h_hi), (hi, h_lo))):
                    for c in range(DC):
                        if first and n != 1 and c % 4 == 0:
                            pe.wait_ge((h2h_ready, None, h2l_ready)[n], 2 * NT - 1 + c // 4)
                        last = mm(out, w[:, c * P:(c + 1) * P], h[:, c * S:(c + 1) * S],
                                  start=n == 0 and c == 0, stop=n == 2 and c == DC - 1)
                return last

            def row(b, i, column):
                return mm(b[:, i * P:(i + 1) * P], column.to_broadcast([P, P]), IDENT, start=True, stop=True)

            def transposes(job, b, ins_, ident=IDENT):
                for i, a in enumerate(ins_):
                    last = nc.tensor.transpose(b[:, i * P:(i + 1) * P], a, ident)
                end(last)

            def run(job):
                kind, *a = job
                T = a[-1] if a else 0
                b = begin(*job)
                if kind == "ssq":
                    pe.wait_ge(s["ones_ready"], 1)
                    pe.wait_ge(s["xsq_ready"], 2)
                    for t in range(NT):
                        for c in range(DC):
                            last = mm(b[:, t:t + 1], CV[:, c, t * P:(t + 1) * P], ONES[:, 0:1], start=c == 0, stop=c == DC - 1)
                    end(last)
                elif kind == "misc":
                    w = wslot(0)[:, 0:DC * MISC].rearrange("p (c n) -> p c n", c=DC)
                    for c in range(DC):
                        if T == 0:
                            pe.wait_ge(s["hT_ready"], c + 1)
                            if c % 4 == 0:
                                pe.wait_ge(misc_in[c // 4], 16)
                        last = mm(b[:, 0:MISC], HT[:, c, T * P:(T + 1) * P], w[:, c], start=c == 0, stop=c == DC - 1)
                    end(last)
                elif kind == "rrow":
                    pe.wait_ge(s["rcol_ready"], 1)
                    pe.wait_ge(keep_in, 16)
                    for t in range(NT):
                        last = row(b, t, rcol[:, t:t + 1])
                    end(last)
                elif kind == "qkv":
                    for i in range(2):
                        pe.wait_ge(s["qkv_lo"], 2 * a[0] + i + 1)
                        pe.wait_ge(s["htl_ready"], DC)
                        last = products(b[:, i * S:(i + 1) * S], (2 * a[0] + i) % QKV_BUFS, w=(QKVH, QKVL), h=(HTH, HTL))
                        if i == 0:
                            last.then_inc(s["qkv_first"], 1)
                    end(last)
                elif kind in ("qp", "kvp", "zp"):
                    if T == 1:
                        return
                    first = 4 * [k for k, _ in ROW_LOADS].index(kind)
                    banks = [b, begin(kind, 1)]
                    for r in range(first, first + 4):
                        pe.wait_ge(s["row_lo"], r + 1)
                        hi, lo = (t[r % 3].rearrange("p (c n) -> p c n", c=2) for t in (ROWH, ROWL))
                        for t in range(NT):
                            for n, (h, w) in enumerate(((HTH, hi), (HTL, hi), (HTH, lo))):
                                for i in range(2):
                                    at = (2 * (r - first) + i) * S + t * P
                                    last = mm(banks[t], h[:, at:at + P], w[:, i], start=r == first and n == i == 0,
                                              stop=r == first + 3 and n == 2 and i == 1)
                            if r == first + 3:
                                end(last)
                            elif t == 1:
                                last.then_inc(s["row_done"], 1)
                elif kind == "gcol":
                    pe.wait_ge(s["g_ready"], 1)
                    pe.wait_ge(consts_in, 16)
                    for t in range(NT):
                        mm(b[:, t * 8:t * 8 + 4], const("upper"), gstep[:, t], start=True, stop=True)
                        last = mm(b[:, t * 8 + 4:t * 8 + 8], const("strict"), gstep[:, t], start=True, stop=True)
                    end(last)
                elif kind == "gb":
                    for h in range(GH):
                        last = mm(b[:, h * P:(h + 1) * P], gstep[:, T, h:h + 1].to_broadcast([P, P]), const("upper"),
                                  start=True, stop=True)
                    end(last)
                elif kind == "l2":
                    pe.wait_ge(s["sq_ready"], a[0] + 1)
                    for n in range(4):
                        last = mm(b[:, n:n + 1], SQ[:, 2 * a[0] + n // 2, n % 2 * P:(n % 2 + 1) * P], ONES[:, 0:1],
                                  start=True, stop=True)
                    end(last)
                elif kind == "l2b":
                    pe.wait_ge(s["l2_ready"], a[0] + 1)
                    for n in range(4):
                        last = row(b, n, l2c[:, a[0], n:n + 1])
                    end(last)
                elif kind in ("kk", "kq"):
                    evacuated(pe, "l2b", 3)
                    ts = slice(T * P, (T + 1) * P)
                    for h in range(GH):
                        last = mm(b[:, h * P:(h + 1) * P], CV[:, 4 + h, ts], CV[:, (4 if kind == "kk" else 0) + h, ts],
                                  start=True, stop=True)
                    end(last)
                elif kind == "at":
                    evacuated(pe, "kk", T)
                    transposes(job, b, [AM[:, T, h] for h in range(GH)])
                elif kind == "ktok":
                    evacuated(pe, "l2b", 3)
                    transposes(job, b, [CV[:, 4 + h, T * P:(T + 1) * P] for h in range(GH)])
                elif kind == "vtok":
                    pe.wait_ge(s["silu_done"], 6)
                    transposes(job, b, [CV[:, 8 + h, T * P:(T + 1) * P] for h in range(GH)])
                elif kind == "kvct":
                    evacuated(pe, "kvp", T)
                    transposes(job, b, [KCV[:, T, i] for i in range(4)])
                elif kind == "qt":
                    pe.wait_ge(s["xr_ready"], 2 * T + 1)
                    transposes(job, b, [XR[:, T, 2 * i:2 * i + 2] for i in range(4)])
                elif kind == "kt":
                    pe.wait_ge(s["xr_ready"], 2 * T + 2)
                    transposes(job, b, [KR[:, T, i] for i in range(4)])
                elif kind == "w":
                    l = a[0]
                    pe.wait_ge(s["ct_ready"], NT * (l - 1) + T + 1)
                    if l == 1:
                        pe.wait_ge(s["ti_init"], T + 1)
                    else:
                        evacuated(pe, "pa", l - 1, T)
                    for h in range(GH):
                        last = mm(b[:, h * P:(h + 1) * P], CT[l % 2 if l > 1 else 2][:, T, h], TI[:, T, h],
                                  start=True, stop=True)
                    end(last)
                elif kind in ("pa", "pb"):
                    l = a[0]
                    evacuated(pe, "w", l, T)
                    if l == 1:
                        pe.wait_ge(s["tt_init"], T + 1)
                    else:
                        evacuated(pe, "pb", l - 1, T)
                    for h in range(GH):
                        lhs, rhs = (TT[:, T, h], WW[:, T, h]) if kind == "pa" else (WW[:, T, h], TT[:, T, h])
                        last = mm(b[:, h * P:(h + 1) * P], lhs, rhs, start=True, stop=True)
                    end(last)
                elif kind in ("u", "wt"):
                    evacuated(pe, "pb", LEVELS - 1, T)
                    evacuated(pe, "vtok" if kind == "u" else "ktok", T)
                    for h in range(GH):
                        lhs, rhs = (TT[:, T, h], VB[:, T, h]) if kind == "u" else (KBG[:, T, h], TT[:, T, h])
                        last = mm(b[:, h * P:(h + 1) * P], lhs, rhs, start=True, stop=True)
                    end(last)
                elif kind == "kv":
                    c = a[0]
                    t, r = c // 2, slice(64 * (c % 2), 64 * (c % 2) + 64)
                    if c == 0:
                        evacuated(pe, "u", 0)
                    else:
                        evacuated(pe, "vn", c)
                    for h in range(GH):
                        last = mm(b[:, h * P:(h + 1) * P], KD[r, t, h], U[r, t, h], start=True, stop=True)
                    end(last)
                elif kind in ("vn", "o1"):
                    c = a[0]
                    t, r = c // 2, slice(64 * (c % 2), 64 * (c % 2) + 64)
                    if kind == "vn":
                        evacuated(pe, "wt", t)
                        evacuated(pe, "kv", c - 1)
                    else:
                        pe.wait_ge(s["qd_ready"], NT)
                    src = WT if kind == "vn" else QD
                    for h in range(GH):
                        last = mm(b[r, h * P:(h + 1) * P], src[:, t, h, r], STATE[:, h], start=True, stop=True)
                    end(last)
                elif kind == "o2":
                    evacuated(pe, "vn", 2 * T + 1)
                    if T:
                        evacuated(pe, "vn", 2 * T)
                    evacuated(pe, "kq", T)
                    for h in range(GH):
                        last = mm(b[:, h * P:(h + 1) * P], DU[:, T, h], U[:, T, h], start=True, stop=True)
                    end(last)
                elif kind == "h1":
                    kv = a[0]
                    w = weights(7 + kv).rearrange("p (m n) -> p m n", m=16)
                    pe.wait_ge(s["y_ready"], kv + 1)
                    for hc in range(2):
                        for m in range(16):
                            last = mm(b[:, hc * 32:hc * 32 + 32], w[:, m, hc * P:(hc + 1) * P], YB[:, kv, m],
                                      start=m == 0, stop=m == 15)
                    end(last)
                elif kind == "c2k":
                    evacuated(pe, "h1", 0)
                    w2 = param("w2").rearrange("p (k c n) -> p k c n", k=2, c=2)
                    for hc in range(2):
                        last = mm(b[0:32, 0:DH], HK[:, hc], w2[:, 0, hc], start=hc == 0, stop=hc == 1)
                    end(last)
                elif kind == "c2v":
                    evacuated(pe, "h1", 1)
                    w2 = param("w2").rearrange("p (k c n) -> p k c n", k=2, c=2)
                    for hc in range(2):
                        last = mm(b[:, 0:DH], HV[:, hc].rearrange("p g m n -> p (g m n)"), w2[:, 1, hc],
                                  start=hc == 0, stop=hc == 1)
                    end(last)
                elif kind == "kct":
                    pe.wait_ge(s["kcr_ready"], 1)
                    end(nc.tensor.transpose(b[:, 0:32], KC2[0:32, :], IDENT[0:32, 0:32]))
                elif kind == "sc":
                    evacuated(pe, "kct")
                    evacuated(pe, "qt", T)
                    for p in range(4):
                        last = mm(b[:, p * 32:p * 32 + 32], QT[:, p, T * P:(T + 1) * P], KCBD[:, p // 2],
                                  start=True, stop=True)
                    end(last)
                elif kind == "pct":
                    pe.wait_ge(s["pc_ready"], T + 1)
                    transposes(job, b, [PC[T]])
                elif kind == "oc":
                    evacuated(pe, "pct", T)
                    evacuated(pe, "c2v")
                    end(mm(b[:, :], PCT[:, T * P:(T + 1) * P], VBD, start=True, stop=True))
                elif kind == "s":
                    t, br, h0, nh = UNITS[a[0]]
                    evacuated(pe, "qt", t)
                    for t_ in range(t + 1):
                        evacuated(pe, "kt", t_)
                    nk = (t + 1) * P
                    for i in range(nh // 2):
                        last = mm(b[:, i * 2 * nk:(i + 1) * 2 * nk], QT[:, h0 // 2 + i, t * P:(t + 1) * P],
                                  KZ[:, br, h0 // 4, :, 0:nk], start=True, stop=True)
                    end(last)
                elif kind == "pt":
                    pe.wait_ge(s["p_ready"], a[0] + 1)
                    transposes(job, b, [SM[a[0] % 3][:, i * P:(i + 1) * P] for i in range(4)])
                elif kind == "o":
                    u = a[0]
                    t, br, h0, nh = UNITS[u]
                    evacuated(pe, "pt", u)
                    nb = t + 1
                    for i in range(nh):
                        for kb in range(nb):
                            last = mm(b[:, i * DH:(i + 1) * DH], PT[u % 3][:, i * nb + kb],
                                      VSW[:, kb, 2 * br + (h0 + i) // 4], start=kb == 0, stop=kb == nb - 1)
                    end(last)
                elif kind == "ot":
                    t, hf = a
                    if hf == 0:
                        pe.wait_ge(s["oc_nsa"], sum(u[0] <= t for u in UNITS))
                    else:
                        pe.wait_ge(s["oc_gdn"], t + 1)
                    transposes(job, b, [OC[:, t, (4 * hf + i) * P:(4 * hf + i + 1) * P] for i in range(4)])
                elif kind == "y":
                    t, hf = a
                    w = weights(9 + hf).rearrange("p (c n) -> p c n", c=DC)
                    for c in range(DC):
                        if c % 4 == 0:
                            evacuated(pe, "ot", t, c // 4)
                        last = mm(b, OT[:, c, t * P:(t + 1) * P], w[:, c], start=c == 0, stop=c == DC - 1)
                    end(last)
                elif kind == "xt":
                    t, hf = a
                    pe.wait_ge(s["xn_ready"], t + 1)
                    transposes(job, b, [XNORM[:, t, (4 * hf + i) * P:(4 * hf + i + 1) * P] for i in range(4)])
                elif kind == "q":
                    n = a[0]
                    pe.wait_ge(query_lo_dve, n + 1)
                    pe.wait_ge(query_lo_pool, n + 1)
                    end(products(b[:, 0:S], n % 2, first=n == 0))
                elif kind == "sk":
                    t, k = a
                    pe.wait_ge(subk_in, 32)
                    for i in range(4):
                        evacuated(pe, "q", 4 * k + i)
                    for i in range(4):
                        last = mm(b[:, i * P:(i + 1) * P], QRY[:, 4 * k + i, t * P:(t + 1) * P], SUBK[:, i % 2],
                                  start=True, stop=True)
                    end(last)

            for job in JOBS:
                run(job)

            def gates(ph, m, k):
                g = m + Q * (ph - 1)
                pe.wait_ge(onehot_ready, 4 * g + k + 1)
                for idx in range(4 * k, 4 * k + 4):
                    if idx % 8 == 0:
                        wait(pe, gated, 2 * g - 1 + idx // 8)
                    q = idx % OH_TOKENS
                    for c in range(PARTS):
                        last = mm(PS[:, G_BANK + idx // 8, idx % 8 * 64:idx % 8 * 64 + 64], ONEHOT2[:, q], ONEHOT1[:, q, c],
                                  start=c == 0, stop=c == PARTS - 1)
                last.then_inc(gate_mm, 1)

            def route_transposes():
                pe.wait_ge(route_ready, 1)
                for c in (2, 0, 1):
                    for t in range(NT):
                        i = c * NT + t
                        last = nc.tensor.transpose(PS[:, G_BANK + i // 4, i % 4 * P:(i % 4 + 1) * P],
                                                   ROUTE[:, i * P:(i + 1) * P], IDENT)
                    if c != 0:
                        last.then_inc(route_t_in, 1)

            def step(ph, m):
                for k in range(RSLOTS):
                    b = 4 * m + 4 * Q * ph + k
                    turn = b - NBLK // 2 if isinstance(b, int) else None
                    if ph in (1, 2) and turn not in (0, 1):
                        gates(ph, m, k)
                    pe.wait_ge(tab_lo_dve, b + 1)
                    pe.wait_ge(tab_lo_pool, b + 1)
                    if ph < 2:
                        wait(pe, gelu_done, b - 1)
                        last = products(PS[:, A_BANK + k % 2, 0:S], k % 2)
                    else:
                        if ph == 2:
                            pe.wait_ge(coef_lo_pool, b - NBLK + 1)
                        else:
                            pe.wait_ge(coef_lo_dve, b - NBLK - NBLK // 2 + 1)
                        hi, lo = (t[:, k % 2 * D:(k % 2 + 1) * D] for t in (TABH, TABL))
                        first = ph == 2 and isinstance(m, int) and m == 0 and k == 0
                        final = ph == 3 and isinstance(m, int) and m == Q - 1 and k == RSLOTS - 1
                        for t in range(NT):
                            chi, clo = (x[:, k % 2 * S + t * P:k % 2 * S + (t + 1) * P] for x in (CFH, CFL))
                            for n, (cf, tab) in enumerate(((chi, hi), (chi, lo), (clo, hi))):
                                for hf in range(2):
                                    last = mm(PS[:, 2 * t + hf, :], cf, tab[:, hf * 512:(hf + 1) * 512],
                                              start=first and n == 0, stop=final and n == 2)
                    last.then_inc(blocks_done, 1)
                    if turn == 0:
                        route_transposes()
                    if turn == 1:
                        for g in range(2):
                            gates(1, 0, g)

            phases(pe, step)

        @block.scalar
        def _(act):
            A = nc.scalar.activation

            def split_qkv(n):
                rounded = QKVH[:, n % QKV_BUFS * D:(n % QKV_BUFS + 1) * D].rearrange("p (c n) -> p c n", c=DC)
                A(rounded, qkv_weights(act, n), ACT.Copy).then_inc(s["qkv_hi"], 1)

            def split_rows(*pieces):
                for r in pieces:
                    w = row_piece(act, r)
                    row_buffer(act, r)
                    A(ROWH[r % 3], w, ACT.Copy).then_inc(s["row_hi"], 1)

            def silu(n):
                act.wait_ge(s["conv_ready"], n + 1)
                A(CV[:, 2 * n:2 * n + 2], CV[:, 2 * n:2 * n + 2], ACT.Silu).then_inc(s["silu_done"], 1)
                if n < 4:
                    act.wait_ge(s["silu_done"], n + 1)
                    A(SQ[:, 2 * n:2 * n + 2], CV[:, 2 * n:2 * n + 2], ACT.Square).then_inc(s["sq_ready"], 1)

            def split_query(n):
                w = query_weights(act, n)
                if n < 2:
                    full(act, "ot", 1, 1)
                    act.wait_ge(s["oc_gdn"], NT)
                A(TABH[:, n % 2 * D:(n % 2 + 1) * D].rearrange("p (c n) -> p c n", c=DC), w, ACT.Copy).then_inc(query_hi, 1)

            def run(job):
                kind, *a = job
                T = a[-1] if a else 0
                b = bank(*job)
                if kind == "ssq":
                    for i in range(2):
                        act.wait_ge(xt_in[i], 16)
                        A(CV[:, 4 * i:4 * i + 4], XT[:, 4 * i:4 * i + 4], ACT.Square).then_inc(s["xsq_ready"], 1)
                    act.wait_ge(s["ones_ready"], 2)
                    full(act, *job)
                    release(A(rcol, b[:, 0:NT], ACT.Sqrt, bias=EPSC, scale=1.0 / D), *job)
                elif kind == "rrow":
                    for i in range(2):
                        act.wait_ge(s["hT_ready"], DC // 2 * (i + 1))
                        A(HTH[:, i * DC // 2 * S:(i + 1) * DC // 2 * S].rearrange("p (c t) -> p c t", t=S),
                          HT[:, 4 * i:4 * i + 4], ACT.Copy).then_inc(s["hth_ready"], 1)
                    for n in range(QKV_BUFS):
                        split_qkv(n)
                    act.wait_ge(s["softplus_in"], 1)
                    A(SG, GAB[:, :, 0:28], ACT.Exp, scale=-1.0).then_inc(s["exp_misc_done"], 1)
                    A(aexp, param("alog"), ACT.Exp).then_inc(s["exp_misc_done"], 1)
                    A(sp1, sp1, ACT.Exp, scale=-1.0).then_inc(s["softplus_exp"], 1)
                    act.wait_ge(s["softplus_exp"], 1)
                    A(sp1, sp1, ACT.Ln, bias=1.0).then_inc(s["softplus_ln"], 1)
                elif kind == "qkv":
                    n = a[0]
                    if n == 5:
                        split_rows(0, 1, 2)
                    if 2 * n + QKV_BUFS < 12:
                        act.wait_ge(s["qkv_first"], n + 1)
                        split_qkv(2 * n + QKV_BUFS)
                    if n:
                        silu(n - 1)
                    for i in range(4 if n == 5 else 0):
                        full(act, "l2", i)
                        release(A(l2c[:, i], bank("l2", i)[:, 0:4], ACT.Sqrt, bias=EPSC), "l2", i)
                    if 2 * n + 1 + QKV_BUFS < 12:
                        full(act, *job)
                        split_qkv(2 * n + 1 + QKV_BUFS)
                    if n == 5:
                        silu(n)
                elif kind == "qp":
                    split_rows(*((3, 4), (5, 6))[T])
                    full(act, *job)
                    release(A(XN[:, T, 0:8], b.rearrange("p (h d) -> p h d", d=DH), ACT.Copy, scale=rcol[:, T:T + 1]), *job)
                elif kind == "kvp":
                    split_rows(*((7, 8), (9, 10))[T])
                    full(act, *job)
                    A(XN[:, T, 8:12], b[:, 0:256].rearrange("p (h d) -> p h d", d=DH), ACT.Copy, scale=rcol[:, T:T + 1])
                    release(A(KCV[:, T], b[:, 256:512].rearrange("p (h d) -> p h d", d=DH).unsqueeze(2)
                              .to_broadcast([P, 4, 2, DH]), ACT.Copy, scale=rcol[:, T:T + 1]), *job)
                    evacuated(act, *job)
                    A(XSQ[:, T], XN[:, T], ACT.Square).then_inc(s["xn_sq"], 1)
                elif kind == "gcol":
                    evacuated(act, *job)
                    A(egs, gcs, ACT.Exp).then_inc(s["gcs_exp"], 1)
                elif kind == "gb":
                    full(act, *job)
                    A(EG[:, T], b.rearrange("p (h n) -> p h n", h=GH), ACT.Exp).then_inc(s["eg_exp"], 1)
                    for i, m in enumerate((DL, DU)):
                        act.wait_ge(s["darg_ready"], 2 * T + i + 1)
                        A(m[:, T], m[:, T], ACT.Exp).then_inc(s["dexp_done"], 1)
                elif kind == "zp":
                    if T == 0:
                        split_rows(11)
                    full(act, *job)
                    act.wait_ge(s["rcol_ready"], 1)
                    release(A(Z[:, T], b, ACT.Silu, scale=rcol[:, T:T + 1]), *job)
                elif kind in ("at", "w", "u", "wt", "qt", "kvct", "pct", "pt"):
                    full(act, *job)
                    dst = {"at": lambda: AT_[:, T], "w": lambda: WW[:, T], "u": lambda: U[:, T], "wt": lambda: WT[:, T],
                           "qt": lambda: QT[:, :, T * P:(T + 1) * P], "kvct": lambda: X2[:, :, T * P:(T + 1) * P],
                           "pct": lambda: PCT[:, T * P:(T + 1) * P], "pt": lambda: PT[a[0] % 3]}[kind]()
                    if kind == "kvct":
                        full(act, "l2", 3)
                    if kind == "w" and a[0] == 1:
                        act.wait_ge(s["ti_init"], T + 1)
                    if kind == "pt" and a[0] >= 3:
                        full(act, "o", a[0] - 3)
                    src = b[:, 0:P] if kind == "pct" else b
                    if kind != "pct":
                        src = src.rearrange("p (h n) -> p h n", h=4)
                    release(A(dst, src, ACT.Copy), *job)
                elif kind == "ktok":
                    full(act, *job)
                    act.wait_ge(s["bg_ready"], 1)
                    for h in range(GH):
                        ins = A(KBG[:, T, h], b[:, h * P:(h + 1) * P], ACT.Copy, scale=bg[:, T, h:h + 1])
                    ins.then_inc(s["kbg_done"], 1)
                elif kind == "vtok":
                    full(act, *job)
                    act.wait_ge(s["sig_ready"], 1)
                    for h in range(GH):
                        ins = A(VB[:, T, h], b[:, h * P:(h + 1) * P], ACT.Copy, scale=SG[:, T, 24 + h:25 + h])
                    release(ins, *job)
                elif kind == "o1":
                    c = a[0]
                    r = slice(64 * (c % 2), 64 * (c % 2) + 64)
                    full(act, *job)
                    release(A(OG[r, c // 2], b[r, :].rearrange("p (h n) -> p h n", h=GH), ACT.Copy), *job)
                elif kind == "h1":
                    full(act, *job)
                    src = b[:, 0:64].rearrange("p (c n) -> p c n", c=2)
                    if a[0] == 0:
                        ins = A(HK, src, ACT.Gelu_apprx_tanh)
                    else:
                        for c in range(2):
                            ins = A(HV[:, c], src[:, c].rearrange("p (g n) -> p g n", g=2).unsqueeze(2)
                                    .to_broadcast([P, 2, 4, NC16]), ACT.Gelu_apprx_tanh)
                    release(ins, *job)
                elif kind == "s":
                    u = a[0]
                    t, br, h0, nh = UNITS[u]
                    nk = (t + 1) * P
                    act.wait_ge(s["sm_ready"], u + 1)
                    for i in range(nh):
                        v = SM[u % 3][:, i * nk:(i + 1) * nk]
                        last = A(v, v, ACT.Exp, bias=nm[u % 3][:, i:i + 1], scale=DH ** -0.5, accum_out=rs[:, u, i:i + 1])
                    last.then_inc(s["p_ready"], 1)
                elif kind == "sc":
                    act.wait_ge(s["scm_ready"], T + 1)
                    A(PC[T], PC[T], ACT.Exp, scale=DH ** -0.5).then_inc(s["pc_ready"], 1)
                elif kind == "ot":
                    full(act, *job)
                    t, hf = a
                    release(A(OT[:, 4 * hf:4 * hf + 4, t * P:(t + 1) * P], b.rearrange("p (c n) -> p c n", c=4), ACT.Copy),
                            *job)
                elif kind == "y":
                    t, hf = a
                    if t == 1:
                        split_query(hf)
                    evacuated(act, *job)
                    A(XNORM[:, t, hf * 512:(hf + 1) * 512], X[:, t, hf * 512:(hf + 1) * 512], ACT.Square,
                      accum_out=xss[:, t, hf:hf + 1]).then_inc(s["x1_sq"], 1)
                elif kind == "xt":
                    evacuated(act, *job)
                    A(tile4(H2H, *a), tile4(H2T, *a), ACT.Copy).then_inc(h2h_ready, 1)
                elif kind == "q":
                    full(act, *job)
                    if a[0] + 2 < 2 * PH:
                        split_query(a[0] + 2)
                    release(A(QRY[:, a[0]], b[:, 0:S], ACT.Copy), *job)

            for job in JOBS:
                run(job)

            def gelu(b, k):
                act.wait_ge(blocks_done, b + 1)
                A(view(GATED, b * S, (1, S)), PS[:, A_BANK + k % 2, 0:S], ACT.Gelu_apprx_tanh).then_inc(gelu_done, 1)

            def coef_round(ph, b, k):
                if k == 0:
                    act.wait_ge(gated, 2 * Q * (ph - 1))
                A(CFH[:, k % 2 * S:(k % 2 + 1) * S], view(GATED, (b - NBLK) * S, (1, S)), ACT.Copy).then_inc(coef_hi, 1)

            def step(ph, m):
                for k in range(RSLOTS):
                    b = 4 * m + 4 * Q * ph + k
                    act.wait_ge(table_in[k], 16 * (m + Q * ph + 1))
                    wait(act, blocks_done, b - 1)
                    turn = isinstance(b, int) and b == NBLK
                    if ph == 2 and not turn:
                        coef_round(ph, b, k)
                    for lo, hi in ((SPLIT[ph], D), (0, SPLIT[ph])):
                        A(TABH[:, k % 2 * D + lo:k % 2 * D + hi], RING[:, k * D + lo:k * D + hi], ACT.Copy)\
                            .then_inc(tab_hi, 1)
                    if turn:
                        gelu(b - 2, 0)
                    if ph == 3 or turn:
                        coef_round(ph, b, k)
                    if turn:
                        gelu(b - 1, 1)
                    if ph < 2 and not (isinstance(b, int) and b < 2):
                        gelu(b - 2, k)
                    if isinstance(b, int) and b == NBLK // 2:
                        act.wait_ge(route_exp_in, 1)
                        A(ROUTE[:, 2 * S:3 * S], GEXP, ACT.Exp).then_inc(route_exp, 1)
                    if isinstance(b, int) and b == NBLK // 2 + 1:
                        act.wait_ge(route_t_in, 2)
                        A(ROUTE_T[:, 0:2 * S], PS[:, G_BANK, :], ACT.Copy).then_inc(route_keys, 1)

            phases(act, step)

        @block.vector
        def _(dve):
            v = nc.vector
            count = [0]

            def link(ins):
                count[0] += 1
                ins.then_inc(dve_link, 1)
                dve.wait_ge(dve_link, count[0])

            def bc(a, axis, shape):
                return a.unsqueeze(axis).to_broadcast(shape)

            def heads(b, h):
                return b.rearrange("p (h n) -> p h n", h=h)

            def rotate(T):
                dve.wait_ge(s["xq_rstd"], T + 1)
                dve.wait_ge(s["xn_gain"], T + 1)
                link(v.tensor_tensor(XN[:, T], XN[:, T], bc(rs12[:, T], 2, [P, 12, DH]), ALU.mult))
                sq = TMP[:, 0:768].rearrange("p (h d) -> p h d", d=DH)
                cos = const("cos").rearrange("p (t d) -> p t d", t=NT)[:, T]
                sin = const("sin").rearrange("p (t d) -> p t d", t=NT)[:, T]
                hd = DH // 2
                v.tensor_tensor(XR[:, T], XN[:, T, 0:8], bc(cos, 1, [P, 8, DH]), ALU.mult)
                kr = TMP2[:, 0:4 * DH].rearrange("p (h d) -> p h d", d=DH)
                v.tensor_tensor(kr, XN[:, T, 8:12], bc(cos, 1, [P, 4, DH]), ALU.mult)
                v.tensor_tensor(sq[:, :, 0:hd], XN[:, T, :, hd:DH], bc(sin[:, 0:hd], 1, [P, 12, hd]), ALU.mult)
                link(v.tensor_tensor(sq[:, :, hd:DH], XN[:, T, :, 0:hd], bc(sin[:, hd:DH], 1, [P, 12, hd]), ALU.mult))
                v.tensor_tensor(XR[:, T], XR[:, T], sq[:, 0:8], ALU.add).then_inc(s["xr_ready"], 1)
                v.tensor_tensor(KR[:, T], bc(kr, 2, [P, 4, 2, DH]), bc(sq[:, 8:12], 2, [P, 4, 2, DH]), ALU.add)\
                    .then_inc(s["xr_ready"], 1)

            def run(job):
                kind, *a = job
                T = a[-1] if a else 0
                b = bank(*job)
                if kind == "ssq":
                    evacuated(dve, *job)
                    v.reciprocal(rcol, rcol).then_inc(s["rcol_ready"], 1)
                elif kind == "rrow":
                    full(dve, *job)
                    release(v.tensor_copy(RSTD, b[:, 0:S]), *job)
                    dve.wait_ge(s["rcol_ready"], 1)
                    for t in range(NT):
                        full(dve, "misc", t)
                        m = bank("misc", t)
                        v.tensor_scalar(VSW[:, t], m[:, 0:256].rearrange("p (h d) -> p h d", d=DH), rcol[:, t:t + 1], None,
                                        ALU.mult)
                        release(v.tensor_scalar(GAB[:, t], m[:, 256:288], rcol[:, t:t + 1], None, ALU.mult), "misc", t)
                        evacuated(dve, "misc", t)
                    evacuated(dve, *job)
                    dve.wait_ge(params_in, 16)
                    link(v.tensor_tensor(sp2, GAB[:, :, 28:32], bc(param("dtb"), 1, [P, NT, GH]), ALU.add))
                    link(v.tensor_scalar(sp1, sp2, -1.0, None, ALU.mult))
                    v.tensor_tensor(sp1, sp1, sp2, ALU.max).then_inc(s["softplus_in"], 1)
                    link(v.tensor_scalar(sp2, sp2, 0.0, None, ALU.max))
                elif kind == "qkv":
                    full(dve, *job)
                    dve.wait_ge(s["qp_zero"], 1)
                    qp = QP[:, 2 * a[0]:2 * a[0] + 2, CONV_K - 1:CONV_K - 1 + S]
                    release(v.tensor_tensor(qp, b.rearrange("p (b t) -> p b t", b=2), bc(RSTD, 1, [P, 2, S]), ALU.mult), *job)
                    evacuated(dve, *job)
                    w = param("conv").rearrange("p (b j) -> p b j", b=12)
                    for j in range(CONV_K):
                        for i in (2 * a[0], 2 * a[0] + 1):
                            src = QP[:, i, j:j + S]
                            if j == 0:
                                ins = v.tensor_scalar(CV[:, i], src, w[:, i, 0:1], None, ALU.mult)
                            else:
                                ins = v.scalar_tensor_tensor(CV[:, i], src, w[:, i, j:j + 1], CV[:, i], ALU.mult, ALU.add)
                        if j < CONV_K - 1:
                            link(ins)
                    ins.then_inc(s["conv_ready"], 1)
                    if a[0] == 0:
                        dve.wait_ge(s["softplus_ln"], 1)
                        dve.wait_ge(s["exp_misc_done"], 2)
                        link(v.tensor_tensor(sp2, sp2, sp1, ALU.add))
                        link(v.tensor_scalar(aexp, aexp, -1.0, None, ALU.mult))
                        v.tensor_tensor(gstep, sp2, bc(aexp, 1, [P, NT, GH]), ALU.mult).then_inc(s["g_ready"], 1)
                        link(v.tensor_scalar(SG, SG, 1.0, None, ALU.add))
                        v.reciprocal(SG, SG).then_inc(s["sig_ready"], 1)
                elif kind == "gcol":
                    full(dve, *job)
                    dve.wait_ge(consts_in, 16)
                    release(v.tensor_copy(gcs, b[:, 0:16].rearrange("p (t n) -> p t n", t=NT)), *job)
                    dve.wait_ge(s["gcs_exp"], 1)
                    dve.wait_ge(s["sig_ready"], 1)
                    v.tensor_tensor(bg, egs[:, :, 0:4], SG[:, :, 24:28], ALU.mult).then_inc(s["bg_ready"], 1)
                elif kind == "gb":
                    dve.wait_ge(s["eg_exp"], T + 1)
                    release(v.tensor_tensor(TMP2.rearrange("p (h n) -> p h n", h=GH), heads(b, GH),
                                            bc(gcs[:, T, 0:4], 2, [P, GH, P]), ALU.subtract), *job)
                    evacuated(dve, *job)
                    src = TMP2.rearrange("p (h n) -> p h n", h=GH)
                    v.tensor_tensor(DL[:, T], src, bc(const("nlower"), 1, [P, GH, P]), ALU.mult).then_inc(s["darg_ready"], 1)
                    v.tensor_tensor(DU[:, T], src, bc(const("upper"), 1, [P, GH, P]), ALU.mult).then_inc(s["darg_ready"], 1)
                    for f in range(2):
                        v.tensor_copy(gls[:, T, f], EG[:, T, :, 64 * f + 63]).then_inc(s["gls_ready"], 1)
                elif kind == "l2":
                    for i in range(4 if a[0] == 3 else 0):
                        evacuated(dve, "l2", i)
                        v.reciprocal(l2c[:, i], l2c[:, i]).then_inc(s["l2_ready"], 1)
                elif kind == "l2b":
                    i = a[0]
                    full(dve, *job)
                    dve.wait_ge(s["silu_done"], i + 1)
                    dve.wait_ge(s["sq_ready"], i + 1)
                    for k in range(2):
                        n = 2 * i + k
                        ins = v.scalar_tensor_tensor(CV[:, n], CV[:, n], GD ** -0.5 if n < 4 else 1.0,
                                                     b[:, k * S:(k + 1) * S], ALU.mult, ALU.mult)
                    release(ins, *job)
                elif kind == "kk":
                    full(dve, *job)
                    dve.wait_ge(s["dexp_done"], 2 * T + 2)
                    v.tensor_tensor(DU[:, T], DU[:, T], bc(const("upper"), 1, [P, GH, P]), ALU.mult)\
                        .then_inc(s["dmask_done"], 1)
                    link(v.tensor_tensor(DL[:, T], DL[:, T], bc(const("strict"), 1, [P, GH, P]), ALU.mult))
                    for h in range(GH):
                        ins = v.scalar_tensor_tensor(AM[:, T, h], b[:, h * P:(h + 1) * P], SG[:, T, 24 + h:25 + h],
                                                     DL[:, T, h], ALU.mult, ALU.mult)
                    release(ins, *job)
                    evacuated(dve, *job)
                    link(v.tensor_tensor(TI[:, T], AM[:, T], bc(const("nm0"), 1, [P, GH, P]), ALU.mult))
                    v.tensor_tensor(TI[:, T], TI[:, T], bc(IDENT, 1, [P, GH, P]), ALU.add).then_inc(s["ti_init"], 1)
                elif kind == "kq":
                    full(dve, *job)
                    dve.wait_ge(s["dmask_done"], T + 1)
                    release(v.tensor_tensor(DU[:, T], heads(b, GH), DU[:, T], ALU.mult), *job)
                elif kind == "at":
                    evacuated(dve, *job)
                    link(v.tensor_tensor(TT[:, T], AT_[:, T], bc(const("nm0t"), 1, [P, GH, P]), ALU.mult))
                    v.tensor_tensor(TT[:, T], TT[:, T], bc(IDENT, 1, [P, GH, P]), ALU.add).then_inc(s["tt_init"], 1)
                elif kind == "zp":
                    evacuated(dve, "kvp", T)
                    sq = TMP[:, 0:768].rearrange("p (h d) -> p h d", d=DH)
                    dve.wait_ge(s["xn_sq"], T + 1)
                    link(v.tensor_reduce(rs12[:, T], XSQ[:, T], AX.X, ALU.add))
                    v.tensor_scalar(rs12[:, T], rs12[:, T], 1.0 / DH, EPS, ALU.mult, ALU.add).then_inc(s["xq_mean"], 1)
                elif kind == "ktok":
                    full(dve, *job)
                    dve.wait_ge(s["kbg_done"], T + 1)
                    release(v.tensor_tensor(KD[:, T], heads(b, GH), bc(egs[:, T, 4:8], 2, [P, GH, P]), ALU.mult), *job)
                elif kind == "kt":
                    full(dve, *job)
                    dve.wait_ge(s["qd_ready"], NT)
                    pmv = const("pm")
                    for br in range(2):
                        o = KZ[:, br, :, :, T * P:(T + 1) * P]
                        i0 = bc(b[:, br * 256:br * 256 + 256].rearrange("p (g t) -> p g t", g=2), 2, [P, 2, 2, P])
                        ins = v.tensor_tensor(o, i0, pmv.unsqueeze(1).unsqueeze(3).to_broadcast([P, 2, 2, P]), ALU.mult)
                    release(ins, *job)
                    if T == 1:
                        for t in range(NT):
                            evacuated(dve, "kvct", t)
                        link(v.memset(YB[:, :, :, :, NCMP:NC16], 0.0))
                        pos = param("pos").rearrange("p (k m) -> p k m", k=2)
                        for kv in range(2):
                            for g in range(GROUPS):
                                for r in range(2):
                                    pr = slice(64 * r, 64 * r + 64)
                                    base = X2[pr, 2 * kv + g, r:r + 1]
                                    src = bass.AP(base.tensor, base.offset,
                                                  [list(base.ap[0]), [2, 16], [CMP_STRIDE, NCMP]])
                                    last = v.tensor_tensor(YB[pr, kv, :, g, 0:NCMP], src,
                                                           bc(pos[pr, kv], 2, [64, 16, NCMP]), ALU.add)
                            last.then_inc(s["y_ready"], 1)
                elif kind in ("pa", "pb"):
                    m = TI if kind == "pa" else TT
                    full(dve, *job)
                    release(v.tensor_tensor(m[:, T], m[:, T], heads(b, GH), ALU.subtract), *job)
                elif kind == "u":
                    if T == 0:
                        for t in range(NT):
                            evacuated(dve, "pb", LEVELS - 1, t)
                        v.memset(OG[0:64, 0], 0.0).then_inc(s["og_zero"], 1)
                elif kind == "kv":
                    c = a[0]
                    full(dve, *job)
                    for h in range(GH):
                        if c == 0:
                            ins = v.tensor_copy(STATE[:, h], b[:, h * P:(h + 1) * P])
                        else:
                            ins = v.scalar_tensor_tensor(STATE[:, h], STATE[:, h], gls[:, c // 2, c % 2, h:h + 1],
                                                         b[:, h * P:(h + 1) * P], ALU.mult, ALU.add)
                    release(ins, *job)
                elif kind == "vn":
                    c = a[0]
                    r = slice(64 * (c % 2), 64 * (c % 2) + 64)
                    full(dve, *job)
                    evacuated(dve, "u", c // 2)
                    release(v.tensor_tensor(U[r, c // 2], U[r, c // 2], heads(b[r, :], GH), ALU.subtract), *job)
                elif kind == "o2":
                    full(dve, *job)
                    evacuated(dve, "o1", 2 * T + 1)
                    dve.wait_ge(s["og_zero"], 1)
                    if T == 1:
                        evacuated(dve, "o1", 2)
                    release(v.tensor_tensor(OG[:, T], OG[:, T], heads(b, GH), ALU.add), *job)
                    evacuated(dve, *job)
                    sq = TMP[:, 512:1024].rearrange("p (h n) -> p h n", h=GH)
                    link(v.tensor_tensor(sq, OG[:, T], OG[:, T], ALU.mult))
                    link(v.tensor_reduce(gr[:, T], sq, AX.X, ALU.add))
                    v.tensor_scalar(gr[:, T], gr[:, T], 1.0 / GD, EPS, ALU.mult, ALU.add).then_inc(s["og_mean"], 1)
                    dve.wait_ge(s["og_rstd"], T + 1)
                    link(v.tensor_tensor(sq, OG[:, T], bc(gr[:, T], 2, [P, GH, GD]), ALU.mult))
                    link(v.tensor_tensor(sq, sq, bc(param("outg"), 1, [P, GH, GD]), ALU.mult))
                    v.tensor_tensor(OC[:, T, 512:1024].rearrange("p (h n) -> p h n", h=GH), sq, heads(Z[:, T], GH), ALU.mult)\
                        .then_inc(s["oc_gdn"], 1)
                elif kind == "c2k":
                    k = KC[0:32, :]
                    full(dve, *job)
                    release(v.tensor_copy(k, b[0:32, 0:DH]), *job)
                    evacuated(dve, *job)
                    k2 = KC3[0:32, :]
                    link(v.tensor_tensor(k2, k, k, ALU.mult))
                    link(v.tensor_reduce(kcs[0:32, :], k2, AX.X, ALU.add))
                    v.tensor_scalar(kcs[0:32, :], kcs[0:32, :], 1.0 / DH, EPS, ALU.mult, ALU.add).then_inc(s["kc_mean"], 1)
                    dve.wait_ge(s["kc_rstd"], 1)
                    link(v.scalar_tensor_tensor(k, k, kcs[0:32, :], param("kg0")[0:32, :], ALU.mult, ALU.mult))
                    hd = DH // 2
                    sin = const("sinc")[0:32, :]
                    q = TMP2[0:32, 0:DH]
                    v.tensor_tensor(k2, k, const("cosc")[0:32, :], ALU.mult)
                    v.tensor_tensor(q[:, 0:hd], k[:, hd:DH], sin[:, 0:hd], ALU.mult)
                    link(v.tensor_tensor(q[:, hd:DH], k[:, 0:hd], sin[:, hd:DH], ALU.mult))
                    v.tensor_tensor(KC2[0:32, :].rearrange("p (r d) -> p r d", r=2), bc(k2, 1, [32, 2, DH]),
                                    bc(q, 1, [32, 2, DH]), ALU.add).then_inc(s["kcr_ready"], 1)
                elif kind == "kct":
                    full(dve, *job)
                    i0 = bc(b[:, 0:32].rearrange("p (g n) -> p g n", g=2), 2, [P, 2, 2, NC16])
                    release(v.tensor_tensor(KCBD, i0, const("pm").unsqueeze(1).unsqueeze(3).to_broadcast([P, 2, 2, NC16]),
                                            ALU.mult), *job)
                    evacuated(dve, *job)
                elif kind == "c2v":
                    full(dve, *job)
                    release(v.tensor_tensor(VBD, bc(b[:, 0:DH], 1, [P, HEADS, DH]), bc(const("hm"), 2, [P, HEADS, DH]),
                                            ALU.mult), *job)
                    evacuated(dve, *job)
                elif kind == "sc":
                    pc = PC[T].rearrange("p (h n) -> p h n", h=HEADS)
                    cneg = const("cneg").rearrange("p (t n) -> p t n", t=NT)[:, T]
                    full(dve, *job)
                    release(v.tensor_tensor(pc, b[:, 0:P].rearrange("p (h n) -> p h n", h=HEADS),
                                            bc(cneg, 1, [P, HEADS, NC16]), ALU.add), *job)
                    evacuated(dve, *job)
                    link(v.tensor_reduce(mx, pc, AX.X, ALU.max))
                    v.tensor_tensor(pc, pc, bc(mx, 2, [P, HEADS, NC16]), ALU.subtract).then_inc(s["scm_ready"], 1)
                    dve.wait_ge(s["pc_ready"], T + 1)
                    link(v.tensor_reduce(cs[T], pc, AX.X, ALU.add))
                    link(v.reciprocal(cs[T], cs[T]))
                    gate = SG[:, T, 0:24].rearrange("p (h b) -> p h b", b=3)[:, :, 0]
                    link(v.scalar_tensor_tensor(rc[T], cs[T], const("any")[:, T:T + 1], gate, ALU.mult, ALU.mult))
                elif kind == "oc":
                    full(dve, *job)
                    dve.wait_ge(s["xr_ready"], 4)
                    for t in range(NT):
                        evacuated(dve, "qt", t)
                        full(dve, "kt", t)
                        full(dve, "kvct", t)
                    release(v.tensor_tensor(OC[:, T, 0:512].rearrange("p (h d) -> p h d", d=DH),
                                            b.rearrange("p (h d) -> p h d", d=DH), bc(rc[T], 2, [P, HEADS, DH]), ALU.mult),
                            *job)
                elif kind == "s":
                    u = a[0]
                    t, br, h0, nh = UNITS[u]
                    nk = (t + 1) * P
                    full(dve, *job)
                    if u >= 3:
                        full(dve, "pt", u - 3)
                    if u == 2:
                        full(dve, "h1", 1)
                    sm = SM[u % 3].rearrange("p (h k) -> p h k", h=nh)
                    neg = const("negc").rearrange("p (t k) -> p t k", t=NT)[:, t, 0:nk]
                    release(v.tensor_tensor(sm, b.rearrange("p (h k) -> p h k", h=nh), bc(neg, 1, [P, nh, nk]), ALU.add), *job)
                    evacuated(dve, *job)
                    link(v.tensor_reduce(mx[:, 0:nh], sm, AX.X, ALU.max))
                    v.tensor_scalar(nm[u % 3][:, 0:nh], mx[:, 0:nh], -DH ** -0.5, None, ALU.mult).then_inc(s["sm_ready"], 1)
                elif kind == "o":
                    u = a[0]
                    t, br, h0, nh = UNITS[u]
                    dve.wait_ge(s["p_ready"], u + 1)
                    link(v.reciprocal(rr[:, u, 0:nh], rs[:, u, 0:nh]))
                    gate = SG[:, t, 0:24].rearrange("p (h b) -> p h b", b=3)[:, h0:h0 + nh, 1 + br]
                    link(v.tensor_tensor(rr[:, u, 0:nh], rr[:, u, 0:nh], gate, ALU.mult))
                    full(dve, *job)
                    tmp = TMP[:, 0:nh * DH].rearrange("p (h d) -> p h d", d=DH)
                    release(v.tensor_tensor(tmp, b[:, 0:nh * DH].rearrange("p (h d) -> p h d", d=DH),
                                            bc(rr[:, u, 0:nh], 2, [P, nh, DH]), ALU.mult), *job)
                    evacuated(dve, *job)
                    o = OC[:, t, h0 * DH:(h0 + nh) * DH]
                    v.tensor_tensor(o, o, TMP[:, 0:nh * DH], ALU.add).then_inc(s["oc_nsa"], 1)
                elif kind == "y":
                    t, hf = a
                    full(dve, *job)
                    dve.wait_ge(x_in, 16)
                    xv = X[:, t, hf * 512:(hf + 1) * 512]
                    release(v.tensor_tensor(xv, xv, b, ALU.add), *job)
                    evacuated(dve, *job)
                    if t == 1 and hf == 0:
                        query_rest(v, dve, 0, 0, DC // 2).then_inc(query_lo_dve, 1)
                    if hf == 1:
                        dve.wait_ge(s["x1_sq"], 2 * t + 2)
                        link(v.tensor_tensor(xs[:, t:t + 1], xss[:, t, 0:1], xss[:, t, 1:2], ALU.add))
                        v.tensor_scalar(xs[:, t:t + 1], xs[:, t:t + 1], 1.0 / D, EPS, ALU.mult, ALU.add)\
                            .then_inc(s["x1_mean"], 1)
                        dve.wait_ge(s["x1_rstd"], t + 1)
                        v.tensor_scalar(XNORM[:, t], X[:, t], xs[:, t:t + 1], None, ALU.mult).then_inc(s["xn_ready"], 1)
                elif kind == "xt":
                    full(dve, *job)
                    dve.wait_ge(subk_in, 32)
                    gain = bc(FFNG[:, 4 * a[1]:4 * a[1] + 4], 2, [P, 4, P])
                    release(v.tensor_tensor(tile4(H2T, *a), b.rearrange("p (c n) -> p c n", c=4), gain, ALU.mult), *job)
                    if a[1] == 1:
                        for hf in range(2):
                            dve.wait_ge(h2h_ready, 2 * a[0] + hf + 1)
                            v.tensor_tensor(tile4(H2L, a[0], hf), tile4(H2T, a[0], hf), tile4(H2H, a[0], hf).bitcast(F32),
                                            ALU.subtract).then_inc(h2l_ready, 1)
                    if a == [1, 1]:
                        query_rest(v, dve, 1, 0, DC // 2).then_inc(query_lo_dve, 1)
                elif kind == "sk":
                    full(dve, *job)
                    t, k = a
                    o = t * 16 * NKEYS + k * 512
                    release(v.tensor_copy(SCORES[:, o:o + 512], b), *job)
                elif kind == "q" and a[0] >= 2:
                    query_rest(v, dve, a[0], 0, DC // 2).then_inc(query_lo_dve, 1)

            v.memset(ONES[:, :], 1.0).then_inc(s["ones_ready"], 1)
            v.memset(EPSC, EPS).then_inc(s["ones_ready"], 1)
            for c in range(DC):
                if c % 4 == 0:
                    dve.wait_ge(xt_in[0], 16)
                    if c:
                        dve.wait_ge(xt_in[1], 16)
                v.tensor_scalar(HT[:, c], XT[:, c], XG[:, c:c + 1], None, ALU.mult).then_inc(s["hT_ready"], 1)
            for i in range(2):
                dve.wait_ge(s["hth_ready"], i + 1)
                dve.wait_ge(s["xsq_ready"], i + 1)
                for c in range(4 * i, 4 * i + 4):
                    cols = slice(c * S, (c + 1) * S)
                    v.scalar_tensor_tensor(HTL[:, cols], XT[:, c], XG[:, c:c + 1], HTH[:, cols].bitcast(F32), ALU.mult,
                                           ALU.subtract).then_inc(s["htl_ready"], 1)
            for job in JOBS:
                run(job)
                for T in range(NT):
                    if job == ROTATE_AT[T]:
                        rotate(T)

            marked, carried = [0], [0]

            def topk(m, k):

                def mark(ins):
                    marked[0] += 1
                    ins.then_inc(topk_link, 1)

                def carry():
                    v.memset(CARRIER[:, carried[0] % 4:carried[0] % 4 + 1], 0.0)
                    carried[0] += 1

                def hold(by_carry=True):
                    dve.wait_ge(topk_link, TOPK_LINKS * m + marked[0])
                    if by_carry:
                        carry()

                first = isinstance(m, int) and m == 0
                if k == 0:
                    marked[0] = 0
                    mark(v.tensor_copy(KS, view(GATED, TOPT + 16 * S + m * 2 * NKEYS, (NKEYS, 2), (1, NKEYS))))
                    hold()
                    for f in range(2):
                        ins = v.max(KV_[:, f, 0:8], KS[:, f])
                    mark(ins)
                    hold()
                    for f in range(2):
                        v.max_index(KI[:, f, 0:8], KV_[:, f, 0:8], KS[:, f])
                    for f in range(2):
                        ins = v.match_replace(KS[:, f], KV_[:, f, 0:8], KS[:, f], LOWEST)
                    mark(ins)
                elif k == 1:
                    hold()
                    for f in range(2):
                        ins = v.max(KV_[:, f, 8:16], KS[:, f])
                    ins.then_inc(keys_ready, 1)
                    if not first:
                        compare()
                    dve.wait_ge(keys_ready, m + 1)
                    carry()
                    for f in range(2):
                        ins = v.max_index(KI[:, f, 8:16], KV_[:, f, 8:16], KS[:, f])
                    mark(ins)
                elif k == 2:
                    dve.wait_ge(cand_ready, m + 1)
                    carry()
                    mark(v.max(RES[:, 0:8], CAND))
                    hold()
                    v.max_index(POS[:, 0:8], RES[:, 0:8], CAND)
                    mark(v.match_replace(CAND, RES[:, 0:8], CAND, LOWEST))
                else:
                    hold()
                    mark(v.max(RES[:, 8:16], CAND))
                    if not first:
                        collect(m - 1)
                    hold()
                    mark(v.max_index(POS[:, 8:16], RES[:, 8:16], CAND))
                    v.tensor_copy(KIF, KI)
                    hold(by_carry=False)
                    v.tensor_scalar(POSU[:, 0], POS, 4, None, ALU.logical_shift_right)
                    mark(v.tensor_scalar(POSU[:, 1], POS, TOPK - 1, None, ALU.bitwise_and))
                    v.tensor_copy(view(ROUTE, 2 * S + m * TOPK, (1, TOPK)), RES)
                    hold(by_carry=False)
                    mark(v.tensor_copy(POSF, POSU))
                    assert marked[0] == TOPK_LINKS

            def compare():
                shape = [P, 2 * TOPK, TOPK]
                v.tensor_tensor(EQ.rearrange("p f k a -> p (f k) a"), bc(IOTA[:, 0:TOPK], 1, shape),
                                bc(POSF.rearrange("p f k -> p (f k)"), 2, shape), ALU.is_equal).then_inc(places_ready, 1)

            def collect(m):
                dve.wait_ge(placed, m + 1)
                return v.tensor_reduce(view(ROUTE, m * TOPK, (S, 2), (1, TOPK)), EQ, AX.X, ALU.add)

            def multiply(ph, m, bk):
                g = m + Q * (ph - 1)
                dve.wait_ge(gate_mm, 4 * g + 2 * bk + 2)
                o = view(GATED, (ph - 1) * 64 * S + m * 16 + 8 * bk, (S, 64), (1, 8))
                v.tensor_tensor(o, o, PS[:, G_BANK + bk, :].rearrange("p (t i) -> p i t", i=64), ALU.mult).then_inc(gated, 1)

            def onehots(ph, m, k):
                g = m + Q * (ph - 1)
                lo = (ph - 1) * 64
                wait(dve, onehot_ready, 4 * g + k)
                if k == 0:
                    v.tensor_copy(TOK, view(ROUTE_T, m * 16, (S, 2), (1, 16)))
                    v.tensor_copy(TOKG, view(GPART, m * 16, (S, PARTS), (1, 16))).then_inc(tok_ready, 1)
                    dve.wait_ge(tok_ready, g + 1)
                wait(dve, gate_mm, 4 * g + k - 1)
                q, t = 4 * k % OH_TOKENS, slice(4 * k, 4 * k + 4)
                shape = [P, 4, 64]
                v.tensor_tensor(EQ1, bc(IOTA[:, lo:lo + 64], 1, shape), bc(TOK[:, 0, t], 2, shape), ALU.is_equal)\
                    .then_inc(eq1_ready, 1)
                shape = [P, 4, P]
                v.tensor_tensor(ONEHOT2[:, q:q + 4], bc(IOTA, 1, shape), bc(TOK[:, 1, t], 2, shape), ALU.is_equal)
                dve.wait_ge(eq1_ready, 4 * g + k + 1)
                shape = [P, 4, PARTS, 64]
                last = v.tensor_tensor(ONEHOT1[:, q:q + 4], bc(EQ1, 2, shape),
                                       bc(TOKG[:, :, t].rearrange("p c q -> p q c"), 3, shape), ALU.mult)
                last.then_inc(onehot_ready, 1)

            def route_softmax():
                dve.wait_ge(topk_link, TOPK_LINKS * Q)
                compare()
                dve.wait_ge(places_ready, Q)
                link(v.tensor_tensor(EQ, EQ, bc(KIF, 2, [P, 2, TOPK, TOPK]), ALU.mult))
                v.tensor_reduce(view(ROUTE, (Q - 1) * TOPK, (S, 2), (1, TOPK)), EQ, AX.X, ALU.add)
                gv = ROUTE[:, 2 * S:3 * S].rearrange("p (u k) -> p u k", k=TOPK)
                shape = [P, 2 * PH, TOPK]
                v.tensor_tensor(GEXP.rearrange("p (u k) -> p u k", k=TOPK), gv, bc(gv[:, :, 0], 2, shape), ALU.subtract)\
                    .then_inc(route_exp_in, 1)
                dve.wait_ge(route_exp, 1)
                link(v.tensor_reduce(GSUM, gv, AX.X, ALU.add))
                link(v.reciprocal(GSUM, GSUM))
                v.tensor_tensor(gv, gv, bc(GSUM, 2, shape), ALU.mult).then_inc(route_ready, 1)

            def route_parts():
                dve.wait_ge(route_t_in, 1)
                rest = PS[:, G_BANK + 1, 0:S]
                for c in range(PARTS):
                    link(v.tensor_copy(GPART[:, c], rest))
                    if c < PARTS - 1:
                        link(v.tensor_tensor(GREST[:, c], rest, GPART[:, c], ALU.subtract))
                        rest = GREST[:, c]
                dve.wait_ge(route_keys, 1)

            def step(ph, m):
                for k in range(RSLOTS):
                    b = 4 * m + 4 * Q * ph + k
                    dve.wait_ge(tab_hi, 2 * b + 2)
                    table_rest(v, k, 0, SPLIT[ph]).then_inc(tab_lo_dve, 1)
                    if ph == 3:
                        dve.wait_ge(coef_hi, b - NBLK + 1)
                        coef_rest(v, b, k).then_inc(coef_lo_dve, 1)
                    turn = b - NBLK // 2 if isinstance(b, int) else None
                    if ph == 0:
                        topk(m, k)
                    elif turn == 0:
                        route_softmax()
                    elif turn == 1:
                        route_parts()
                        for n in range(3):
                            onehots(1, 0, n)
                    elif ph < 3:
                        if k == 0 and not (isinstance(m, int) and m == 0):
                            multiply(ph, m - 1, 1)
                        elif k == 2:
                            if isinstance(m, int) and m == 0:
                                dve.wait_ge(gelu_done, NBLK // 2 * ph)
                            multiply(ph, m, 0)
                        if k < 3:
                            onehots(ph, m, k + 1)
                        elif not (isinstance(m, int) and m == Q - 1):
                            onehots(ph, m + 1, 0)
                        elif ph == 1:
                            onehots(2, 0, 0)

            def finish(ph):
                if ph in (1, 2):
                    multiply(ph, Q - 1, 1)

            for t in range(NT):
                for k in range(4):
                    evacuated(dve, "sk", t, k)
            phases(dve, step, finish)
            dve.wait_ge(blocks_done, 2 * NBLK)
            for t in range(NT):
                for hf in range(2):
                    xv = X[:, t, hf * 512:(hf + 1) * 512]
                    v.tensor_tensor(xv, xv, PS[:, 2 * t + hf, :], ALU.add).then_inc(out_ready, 1)

    return


def prepare(inputs):
    i = {k: np.asarray(v) for k, v in inputs.items()}
    x = i["x"][0]
    w_in = i["w_in"][0]
    kv0 = HEADS * DH

    def kvcols(n):
        return w_in[:, kv0 + n * 128:kv0 + (n + 1) * 128]

    g0 = kv0 + 6 * 128
    qkv0 = g0 + 3 * HEADS
    z0 = qkv0 + 3 * GW
    a0 = z0 + GW

    def rows(a):
        return np.ascontiguousarray(a.reshape(-1, P, a.shape[1]).transpose(1, 0, 2).reshape(P, -1))

    misc = np.concatenate([kvcols(3), kvcols(5), w_in[:, g0:qkv0], w_in[:, a0 + GH:a0 + 2 * GH], w_in[:, a0:a0 + GH]], 1)
    slots = [w_in[:, qkv0 + j * 512:qkv0 + (j + 1) * 512] for j in range(3)]
    slots += [w_in[:, 0:512], np.concatenate([kvcols(2), kvcols(4), kvcols(0), kvcols(1)], 1), w_in[:, z0:z0 + 512]]
    slots = [rows(a) for a in slots]
    slots += [rows(i["cmp_w1"][0, j]) for j in range(2)]
    slots += [rows(i["w_out"][0][:, j * 512:(j + 1) * 512]) for j in range(2)]
    slots += [rows(i["peer_w_query"][0][:, j * 512:(j + 1) * 512]) for j in range(4)]
    par = np.zeros((P, NPARAM), np.float32)

    def put(name, a):
        lo, hi = PARAM[name]
        par[:, lo:hi] = a

    kg = i["nsa_k_gain"][0]
    put("gains", np.concatenate([np.tile(i["nsa_q_gain"][0], 8), np.tile(kg[1], 2), np.tile(kg[2], 2)])[None])
    put("kg0", kg[0][None])
    put("outg", i["gdn_out_gain"][0][None])
    put("alog", i["gdn_a_log"][0][None])
    put("dtb", i["gdn_dt_bias"][0][None])
    put("conv", i["gdn_conv"][0].reshape(CONV_K, 12, P).transpose(2, 1, 0).reshape(P, -1))
    put("pos", i["cmp_pos"][0].reshape(2, 16, 2, DH).transpose(2, 3, 0, 1).reshape(P, -1))
    put("w2", i["cmp_w2"][0].reshape(2, 2, P, DH).transpose(2, 0, 1, 3).reshape(P, -1))
    return {
        "consts": constants(), "keep": keep_constants(), "params": par,
        "ffng": np.ascontiguousarray(i["ffn_norm"][0].reshape(DC, P).T),
        "xt": np.concatenate([i["attn_norm"][0].reshape(DC, P).T, rows(np.ascontiguousarray(x.T))], 1),
        "x": rows(x), "wmisc": rows(misc), "wslots": np.stack(slots),
        "u": np.ascontiguousarray(i["peer_u"][0].reshape(NKEYS, NKEYS, DC, P).transpose(0, 3, 2, 1)).reshape(NKEYS, P, D),
        "v": i["peer_v"][0].reshape(NKEYS, NKEYS, D),
        "subk": np.ascontiguousarray(i["peer_subkeys"][0].transpose(2, 0, 1).reshape(P, -1)),
    }


def kernel(**inputs):
    import concourse.bacc as bacc
    from concourse.bass_utils import run_bass_kernel_spmd

    arrays = prepare(inputs)
    nc = bacc.Bacc("TRN2", target_bir_lowering=False, num_devices=1)
    d = {n: nc.dram_tensor("in_" + n, a.shape, F32, kind="ExternalInput").ap() for n, a in arrays.items()}
    out = nc.dram_tensor("out", (P, NT * D), F32, kind="ExternalOutput").ap()
    build(nc, d, out)
    r = run_bass_kernel_spmd(nc, [{"in_" + n: a for n, a in arrays.items()}], core_ids=[0])
    y = r.results[0]["out"]
    return y.reshape(P, NT, D).transpose(1, 0, 2).reshape(1, S, D)
```
